# Optimizing a Trainium2 kernel written in Bass

```python
import jax, jax.numpy as jnp
from jax import lax
import numpy as np
import math

D_MODEL = 2048
BATCH = 1
SEQ = 256
DEPTH = 2

CTX_LEN = 256
GRID_W = 64
EPS = 1e-6

POOL_WINDOWS = (2, 4, 8, 16)
POOL_W = D_MODEL // 2
POOL_GROUP = POOL_W // len(POOL_WINDOWS)
CONV_W = D_MODEL // 2
CONV_K = 3
EVEN_IN = 2 * POOL_W + 4 * CONV_W

HG_DK = 128
HG_HEADS = D_MODEL // HG_DK
HG_DV = D_MODEL // HG_HEADS
HG_K = HG_HEADS * HG_DK
HG_V = HG_HEADS * HG_DV
ODD_IN = 3 * HG_K + 2 * HG_V
CHUNK = 64

N_EVEN = (DEPTH + 1) // 2
N_ODD = DEPTH // 2


def rms_norm(x, g):
    xf = x.astype(jnp.float32)
    y = xf * lax.rsqrt(jnp.mean(xf * xf, axis=-1, keepdims=True) + EPS)
    return (y * g.astype(jnp.float32)).astype(x.dtype)

def box_mean(x, w, axis):
    n = x.shape[axis]
    cs = jnp.cumsum(x.astype(jnp.float32), axis=axis)
    pad = [(0, 0)] * x.ndim
    pad[axis] = (1, 0)
    cs = jnp.pad(cs, pad)
    t = jnp.arange(n)
    lo = jnp.maximum(t - w // 2, 0)
    hi = jnp.minimum(t + w // 2 - 1, n - 1)
    s = jnp.take(cs, hi + 1, axis=axis) - jnp.take(cs, lo, axis=axis)
    cnt = (hi - lo + 1).astype(jnp.float32).reshape((n,) + (1,) * (x.ndim - axis - 1))
    return (s / cnt).astype(x.dtype)

def multiscale_pool(v, pool_w, pool_scale, on_grid):
    b, n, _ = v.shape
    outs = []
    for gi, w in enumerate(POOL_WINDOWS):
        vg = v[..., gi * POOL_GROUP:(gi + 1) * POOL_GROUP]
        if on_grid:
            rows = n // GRID_W
            m = box_mean(box_mean(vg.reshape(b, rows, GRID_W, POOL_GROUP), w, 1), w, 2)
            m = m.reshape(b, n, POOL_GROUP)
        else:
            m = box_mean(vg, w, 1)
        outs.append(m - vg)
    pooled = jnp.stack(outs, axis=2)
    mixed = jnp.einsum('bngi,gio->bngo', pooled, pool_w).reshape(b, n, POOL_W)
    return mixed * pool_scale

def depthwise_conv3(u, w, bias):
    n = u.shape[1]
    up = jnp.pad(u, ((0, 0), (1, 1), (0, 0)))
    return up[:, :n] * w[0] + up[:, 1:n + 1] * w[1] + up[:, 2:] * w[2] + bias

def pool_conv_mixer(h, w_in, pool_w, pool_scale, conv_w, conv_b, w_out, on_grid):
    idx = [int(i) for i in np.cumsum([POOL_W, POOL_W, CONV_W, CONV_W, CONV_W])]
    a_v, a_g, b_x, b_b, b_c, b_g = jnp.split(h @ w_in, idx, axis=-1)
    a_out = multiscale_pool(a_v, pool_w, pool_scale, on_grid) * jax.nn.silu(a_g)
    b_out = b_b * depthwise_conv3(b_c * b_x, conv_w, conv_b) * jax.nn.silu(b_g)
    return jnp.concatenate([a_out, b_out], axis=-1) @ w_out

def _heads(t, d):
    return t.reshape(t.shape[0], t.shape[1], HG_HEADS, d)

def _chunks(t):
    b, n, hh, d = t.shape
    return t.reshape(b, n // CHUNK, CHUNK, hh, d)

def _rev(t, reverse):
    return jnp.flip(t, axis=1) if reverse else t

def hgrn2_gates(z, lb):
    zf = z.astype(jnp.float32)
    f = lb + (1.0 - lb) * jax.nn.sigmoid(zf)
    k = (1.0 - lb) * jax.nn.sigmoid(-zf)
    return _heads(k, HG_DK), _heads(jnp.log(f), HG_DK)

def chunk_state_scan(kc, vc, bc, s0, keep_starts):
    b_last = bc[:, :, -1]
    k_dec = kc * jnp.exp(b_last[:, :, None] - bc)
    ds = jnp.einsum('bnchk,bnchv->bnhkv', k_dec, vc)
    decay = jnp.exp(b_last)

    def step(s, inp):
        d, dsn = inp
        return d[..., None] * s + dsn, (s if keep_starts else None)

    s_fin, starts = lax.scan(step, s0, (jnp.moveaxis(decay, 1, 0), jnp.moveaxis(ds, 1, 0)))
    return s_fin, starts

def hgrn2_chunk_scan(q, k, v, logf, s0):
    qc, kc, vc = _chunks(q), _chunks(k), _chunks(v)
    bc = jnp.cumsum(_chunks(logf), axis=2)
    s_fin, starts = chunk_state_scan(kc, vc, bc, s0, True)
    starts = jnp.moveaxis(starts, 0, 1)
    q_dec = qc * jnp.exp(bc)
    k_inv = kc * jnp.exp(-bc)
    inter = jnp.einsum('bnchk,bnhkv->bnchv', q_dec, starts)
    scores = jnp.einsum('bnchk,bnshk->bnhcs', q_dec, k_inv)
    mask = jnp.tril(jnp.ones((CHUNK, CHUNK), dtype=bool))
    scores = jnp.where(mask, scores, 0.0)
    intra = jnp.einsum('bnhcs,bnshv->bnchv', scores, vc)
    o = (inter + intra).reshape(q.shape[0], q.shape[1], HG_HEADS, HG_DV)
    return o, s_fin

def hgrn2_final_state(k, v, logf, s0):
    bc = jnp.cumsum(_chunks(logf), axis=2)
    s_fin, _ = chunk_state_scan(_chunks(k), _chunks(v), bc, s0, False)
    return s_fin

def hgrn2_readout(o, g, onorm_g, w_out):
    b, n = o.shape[:2]
    o = o * lax.rsqrt(jnp.mean(o * o, axis=-1, keepdims=True) + EPS)
    o = o.reshape(b, n, HG_V) * onorm_g.astype(jnp.float32) * jax.nn.silu(g.astype(jnp.float32))
    return o.astype(g.dtype) @ w_out

def hgrn2_mixer(h_lat, h_ctx, w_in, onorm_g, w_out, lb_fwd, lb_bwd, ctx_out):
    idx = [int(i) for i in np.cumsum([HG_K, HG_K, HG_V, HG_K])]
    zf_l, zb_l, i_l, q_l, g_l = jnp.split(h_lat @ w_in, idx, axis=-1)
    if ctx_out:
        zf_c, zb_c, i_c, q_c, g_c = jnp.split(h_ctx @ w_in, idx, axis=-1)
        q_c = _heads(q_c.astype(jnp.float32), HG_DK)
    else:
        zf_c, zb_c, i_c = jnp.split(h_ctx @ w_in[:, :idx[2]], idx[:2], axis=-1)
    q_l = _heads(q_l.astype(jnp.float32), HG_DK)
    v_l = _heads(i_l.astype(jnp.float32), HG_DV)
    v_c = _heads(i_c.astype(jnp.float32), HG_DV)
    s0 = jnp.zeros((h_lat.shape[0], HG_HEADS, HG_DK, HG_DV), jnp.float32)
    outs_l, outs_c = [], []
    for lb, z_l, z_c, reverse in ((lb_fwd, zf_l, zf_c, False), (lb_bwd, zb_l, zb_c, True)):
        k_l, lf_l = hgrn2_gates(z_l, lb)
        k_c, lf_c = hgrn2_gates(z_c, lb)
        if ctx_out:
            o_c, s_ctx = hgrn2_chunk_scan(_rev(q_c, reverse), _rev(k_c, reverse),
                                          _rev(v_c, reverse), _rev(lf_c, reverse), s0)
            outs_c.append(_rev(o_c, reverse))
        else:
            s_ctx = hgrn2_final_state(_rev(k_c, reverse), _rev(v_c, reverse),
                                      _rev(lf_c, reverse), s0)
        o_l, _ = hgrn2_chunk_scan(_rev(q_l, reverse), _rev(k_l, reverse),
                                  _rev(v_l, reverse), _rev(lf_l, reverse), s_ctx)
        outs_l.append(_rev(o_l, reverse))
    y_l = hgrn2_readout(outs_l[0] + outs_l[1], g_l, onorm_g, w_out)
    y_c = hgrn2_readout(outs_c[0] + outs_c[1], g_c, onorm_g, w_out) if ctx_out else None
    return y_l, y_c

def first_inputs(seed: int = 0) -> dict:
    key = jax.random.key(seed)
    ks = jax.random.split(key, 18)
    D = D_MODEL

    def nrm(k, shape, s):
        return jax.random.normal(k, shape, jnp.float32) * s

    return {
        "x": nrm(ks[0], (BATCH, SEQ, D), 1.0),
        "c": nrm(ks[1], (BATCH, D), 1.0),
        "ctx": nrm(ks[2], (BATCH, CTX_LEN, D), 1.0),
        "c_ctx": nrm(ks[3], (D,), 1.0),
        "ada_w": nrm(ks[4], (DEPTH, D, 3 * D), 0.5 * D ** -0.5),
        "ada_b": nrm(ks[5], (DEPTH, 3 * D), 0.01),
        "pre_g": 1.0 + nrm(ks[6], (DEPTH, D), 0.05),
        "post_g": 1.0 + nrm(ks[7], (DEPTH, D), 0.05),
        "ev_w_in": nrm(ks[8], (N_EVEN, D, EVEN_IN), D ** -0.5),
        "ev_pool_w": nrm(ks[9], (N_EVEN, len(POOL_WINDOWS), POOL_GROUP, POOL_GROUP), POOL_GROUP ** -0.5),
        "ev_pool_scale": 1.0 + nrm(ks[10], (N_EVEN, POOL_W), 0.1),
        "ev_conv_w": nrm(ks[11], (N_EVEN, CONV_K, CONV_W), CONV_K ** -0.5),
        "ev_conv_b": nrm(ks[12], (N_EVEN, CONV_W), 0.01),
        "ev_w_out": nrm(ks[13], (N_EVEN, POOL_W + CONV_W, D), (POOL_W + CONV_W) ** -0.5),
        "od_w_in": nrm(ks[14], (N_ODD, D, ODD_IN), D ** -0.5),
        "od_onorm_g": 1.0 + nrm(ks[15], (N_ODD, HG_V), 0.05),
        "od_w_out": nrm(ks[16], (N_ODD, HG_V, D), HG_V ** -0.5),
        "lb_logits": nrm(ks[17], (2, DEPTH + 1, HG_K), 0.1),
    }

def first_block(x, c, ctx, c_ctx, ada_w, ada_b, pre_g, post_g, ev_w_in, ev_pool_w,
              ev_pool_scale, ev_conv_w, ev_conv_b, ev_w_out, od_w_in, od_onorm_g,
              od_w_out, lb_logits):
    lb_table = jnp.cumsum(jax.nn.softmax(lb_logits.astype(jnp.float32), axis=1), axis=1)
    s_lat = jax.nn.silu(c)
    s_ctx = jax.nn.silu(c_ctx)
    for layer in range(DEPTH):
        last = layer == DEPTH - 1
        shift, scale, gate = jnp.split((s_lat @ ada_w[layer] + ada_b[layer])[:, None, :], 3, axis=-1)
        h = rms_norm(x, pre_g[layer]) * (1.0 + scale) + shift
        need_ctx = (layer % 2 == 1) or not last
        if need_ctx:
            shift_c, scale_c, gate_c = jnp.split(s_ctx @ ada_w[layer] + ada_b[layer], 3)
            hc = rms_norm(ctx, pre_g[layer]) * (1.0 + scale_c) + shift_c
        if layer % 2 == 0:
            e = layer // 2
            y = pool_conv_mixer(h, ev_w_in[e], ev_pool_w[e], ev_pool_scale[e], ev_conv_w[e],
                                ev_conv_b[e], ev_w_out[e], True)
            if not last:
                yc = pool_conv_mixer(hc, ev_w_in[e], ev_pool_w[e], ev_pool_scale[e], ev_conv_w[e],
                                     ev_conv_b[e], ev_w_out[e], False)
        else:
            o = layer // 2
            y, yc = hgrn2_mixer(h, hc, od_w_in[o], od_onorm_g[o], od_w_out[o],
                                lb_table[0, layer], lb_table[1, layer], not last)
        x = x + gate * rms_norm(y, post_g[layer])
        if not last:
            ctx = ctx + gate_c * rms_norm(yc, post_g[layer])
    return x


ROPE_THETA = 10000.0
ROPE_DIM = 64
Q_BLOCK = 128
NORM_EPS = 1e-6
NEG_INF = -1e30

DA_HEADS = 4
DA_QK_DIM = 64
DA_V_DIM = 128
DA_WIDTH = DA_HEADS * DA_V_DIM
DA_SUBLN_EPS = 1e-5

SW_HEADS = 16
SW_KV_HEADS = 2
SW_HEAD_DIM = 64
SW_WINDOW = 128
SW_WIDTH = SW_HEADS * SW_HEAD_DIM
SW_KV_WIDTH = SW_KV_HEADS * SW_HEAD_DIM

MLA_HEADS = 4
MLA_NOPE_DIM = 128
MLA_ROPE_DIM = 64
MLA_V_DIM = 128
MLA_Q_RANK = 512
MLA_KV_RANK = 512
MLA_WIDTH = MLA_HEADS * MLA_V_DIM

D_MIX = DA_WIDTH + SW_WIDTH + MLA_WIDTH

IN_SPLITS = (
    2 * DA_HEADS * DA_QK_DIM, 2 * DA_HEADS * DA_QK_DIM, DA_WIDTH, DA_WIDTH,
    SW_WIDTH, SW_KV_WIDTH, SW_KV_WIDTH, SW_WIDTH,
    MLA_Q_RANK, MLA_KV_RANK, MLA_ROPE_DIM, MLA_WIDTH,
)
D_IN = 5952


def rms_norm_2(x, w, eps=NORM_EPS):
    xf = x.astype(jnp.float32)
    xf = xf * lax.rsqrt(jnp.mean(xf * xf, axis=-1, keepdims=True) + eps)
    return xf.astype(x.dtype) * w

def rope_tables(positions, dim):
    inv_freq = jnp.power(ROPE_THETA, -jnp.arange(0, dim, 2, dtype=jnp.float32) / dim)
    ang = positions.astype(jnp.float32)[..., None] * inv_freq
    return jnp.cos(ang), jnp.sin(ang)

def apply_rope(x, cos, sin):
    half = x.shape[-1] // 2
    x1, x2 = x[..., :half], x[..., half:]
    c, s = cos.astype(x.dtype), sin.astype(x.dtype)
    return jnp.concatenate([x1 * c - x2 * s, x2 * c + x1 * s], axis=-1)

def to_query_blocks(q):
    B, S = q.shape[:2]
    nb = S // Q_BLOCK
    qb = q.reshape((B, nb, Q_BLOCK) + q.shape[2:])
    return jnp.moveaxis(qb, 1, 0), nb

def from_query_blocks(o):
    o = jnp.moveaxis(o, 0, 1)
    return o.reshape((o.shape[0], o.shape[1] * o.shape[2]) + o.shape[3:])

def diff_attention(q, k, v, lam, subln_w, lam_init):
    S = q.shape[1]
    scale = q.shape[-1] ** -0.5
    qb, nb = to_query_blocks(q)
    k_pos = jnp.arange(S)

    def block(args):
        qblk, i = args
        s = jnp.einsum('bqhcd,bkhcd->bhcqk', qblk, k).astype(jnp.float32) * scale
        q_pos = i * Q_BLOCK + jnp.arange(Q_BLOCK)
        s = jnp.where(k_pos[None, :] <= q_pos[:, None], s, NEG_INF)
        p = jax.nn.softmax(s, axis=-1)
        a = (p[:, :, 0] - lam * p[:, :, 1]).astype(v.dtype)
        return jnp.einsum('bhqk,bkhd->bqhd', a, v)

    o = from_query_blocks(lax.map(block, (qb, jnp.arange(nb))))
    o = rms_norm_2(o, subln_w, DA_SUBLN_EPS) * (1.0 - lam_init)
    return o.reshape(o.shape[0], o.shape[1], -1)

def causal_attention(q, k, v, scale):
    S = q.shape[1]
    qb, nb = to_query_blocks(q)
    k_pos = jnp.arange(S)

    def block(args):
        qblk, i = args
        s = jnp.einsum('bqhd,bkhd->bhqk', qblk, k).astype(jnp.float32) * scale
        q_pos = i * Q_BLOCK + jnp.arange(Q_BLOCK)
        s = jnp.where(k_pos[None, :] <= q_pos[:, None], s, NEG_INF)
        p = jax.nn.softmax(s, axis=-1).astype(v.dtype)
        return jnp.einsum('bhqk,bkhd->bqhd', p, v)

    o = from_query_blocks(lax.map(block, (qb, jnp.arange(nb))))
    return o.reshape(o.shape[0], o.shape[1], -1)

def sliding_window_attention(q, k, v, sinks):
    B, S, Hq, d = q.shape
    Hkv = k.shape[2]
    rep = Hq // Hkv
    W = SW_WINDOW
    nb = S // W
    qb = q.reshape(B, nb, W, Hkv, rep, d)

    def band(t):
        tb = t.reshape(B, nb, W, Hkv, d)
        prev = jnp.concatenate([jnp.zeros_like(tb[:, :1]), tb[:, :-1]], axis=1)
        return jnp.concatenate([prev, tb], axis=2)

    kb, vb = band(k), band(v)
    s = jnp.einsum('bnqgrd,bnkgd->bngrqk', qb, kb).astype(jnp.float32) * (d ** -0.5)
    qi = jnp.arange(W)[:, None]
    kj = jnp.arange(2 * W)[None, :]
    rel = qi + W - kj
    in_band = (rel >= 0) & (rel < W)
    has_prev = (jnp.arange(nb) > 0)[:, None, None] | (kj >= W)[None]
    mask = in_band[None] & has_prev
    s = jnp.where(mask[None, :, None, None], s, NEG_INF)
    sink = jnp.broadcast_to(sinks.astype(jnp.float32).reshape(1, 1, Hkv, rep, 1, 1),
                            s.shape[:-1] + (1,))
    p = jax.nn.softmax(jnp.concatenate([s, sink], axis=-1), axis=-1)[..., :-1].astype(v.dtype)
    o = jnp.einsum('bngrqk,bnkgd->bnqgrd', p, vb)
    return o.reshape(B, S, Hq * d)

def hybrid_layer(x, cos, sin, layer, pre_w, post_w, w_in, lq1, lk1, lq2, lk2, subln_w,
                 sinks, q_norm_w, kv_norm_w, w_uq, w_ukv, w_out):
    B, S, _ = x.shape
    h = rms_norm_2(x, pre_w)
    proj = h @ w_in
    offsets = np.cumsum(IN_SPLITS)[:-1].tolist()
    a_q, a_k, a_v, a_g, b_q, b_k, b_v, b_g, c_q, c_kv, c_kr, c_g = jnp.split(proj, offsets, axis=-1)

    cos4, sin4 = cos[:, :, None, :], sin[:, :, None, :]
    cos5, sin5 = cos4[:, :, :, None], sin4[:, :, :, None]

    qa = apply_rope(a_q.reshape(B, S, DA_HEADS, 2, DA_QK_DIM), cos5, sin5)
    ka = apply_rope(a_k.reshape(B, S, DA_HEADS, 2, DA_QK_DIM), cos5, sin5)
    va = a_v.reshape(B, S, DA_HEADS, DA_V_DIM)
    lam_init = 0.8 - 0.6 * math.exp(-0.3 * layer)
    lam = (jnp.exp(jnp.sum(lq1.astype(jnp.float32) * lk1.astype(jnp.float32)))
           - jnp.exp(jnp.sum(lq2.astype(jnp.float32) * lk2.astype(jnp.float32))) + lam_init)
    y_a = diff_attention(qa, ka, va, lam, subln_w, lam_init)

    qb = apply_rope(b_q.reshape(B, S, SW_HEADS, SW_HEAD_DIM), cos4, sin4)
    kb = apply_rope(b_k.reshape(B, S, SW_KV_HEADS, SW_HEAD_DIM), cos4, sin4)
    vb = b_v.reshape(B, S, SW_KV_HEADS, SW_HEAD_DIM)
    y_b = sliding_window_attention(qb, kb, vb, sinks)

    qc = (rms_norm_2(c_q, q_norm_w) @ w_uq).reshape(B, S, MLA_HEADS, MLA_NOPE_DIM + MLA_ROPE_DIM)
    q_nope, q_rope = qc[..., :MLA_NOPE_DIM], apply_rope(qc[..., MLA_NOPE_DIM:], cos4, sin4)
    kvc = (rms_norm_2(c_kv, kv_norm_w) @ w_ukv).reshape(B, S, MLA_HEADS, MLA_NOPE_DIM + MLA_V_DIM)
    k_nope, vc = kvc[..., :MLA_NOPE_DIM], kvc[..., MLA_NOPE_DIM:]
    k_rope = apply_rope(c_kr[:, :, None, :], cos4, sin4)
    qc = jnp.concatenate([q_nope, q_rope], axis=-1)
    kc = jnp.concatenate([k_nope, jnp.broadcast_to(k_rope, (B, S, MLA_HEADS, MLA_ROPE_DIM))], axis=-1)
    y_c = causal_attention(qc, kc, vc, (MLA_NOPE_DIM + MLA_ROPE_DIM) ** -0.5)

    y = jnp.concatenate([y_a, y_b, y_c], axis=-1) * jax.nn.silu(jnp.concatenate([a_g, b_g, c_g], axis=-1))
    out = y @ w_out
    return x + rms_norm_2(out, post_w)

def second_inputs(seed: int = 0) -> dict:
    key = jax.random.key(seed)
    ks = jax.random.split(key, 16)
    f32 = jnp.float32
    L = DEPTH

    def nrm(k, shape, scale):
        return jax.random.normal(k, shape, f32) * scale

    return {
        "x": nrm(ks[0], (BATCH, SEQ, D_MODEL), 1.0),
        "positions": jnp.broadcast_to(jnp.arange(SEQ, dtype=jnp.int32), (BATCH, SEQ)),
        "pre_norm_w": 1.0 + nrm(ks[1], (L, D_MODEL), 0.02),
        "post_norm_w": 1.0 + nrm(ks[2], (L, D_MODEL), 0.02),
        "w_in": nrm(ks[3], (L, D_MODEL, D_IN), D_MODEL ** -0.5),
        "diff_lambda_q1": nrm(ks[4], (L, DA_QK_DIM), 0.1),
        "diff_lambda_k1": nrm(ks[5], (L, DA_QK_DIM), 0.1),
        "diff_lambda_q2": nrm(ks[6], (L, DA_QK_DIM), 0.1),
        "diff_lambda_k2": nrm(ks[7], (L, DA_QK_DIM), 0.1),
        "diff_subln_w": 1.0 + nrm(ks[8], (L, DA_V_DIM), 0.02),
        "sink_logits": nrm(ks[9], (L, SW_HEADS), 0.5),
        "mla_q_norm_w": 1.0 + nrm(ks[10], (L, MLA_Q_RANK), 0.02),
        "mla_kv_norm_w": 1.0 + nrm(ks[11], (L, MLA_KV_RANK), 0.02),
        "w_uq": nrm(ks[12], (L, MLA_Q_RANK, MLA_HEADS * (MLA_NOPE_DIM + MLA_ROPE_DIM)), MLA_Q_RANK ** -0.5),
        "w_ukv": nrm(ks[13], (L, MLA_KV_RANK, MLA_HEADS * (MLA_NOPE_DIM + MLA_V_DIM)), MLA_KV_RANK ** -0.5),
        "w_out": nrm(ks[14], (L, D_MIX, D_MODEL), D_MIX ** -0.5),
    }

def second_block(x, positions, pre_norm_w, post_norm_w, w_in, diff_lambda_q1, diff_lambda_k1,
              diff_lambda_q2, diff_lambda_k2, diff_subln_w, sink_logits, mla_q_norm_w,
              mla_kv_norm_w, w_uq, w_ukv, w_out):
    cos, sin = rope_tables(positions, ROPE_DIM)
    for layer in range(DEPTH):
        x = hybrid_layer(x, cos, sin, layer, pre_norm_w[layer], post_norm_w[layer], w_in[layer],
                         diff_lambda_q1[layer], diff_lambda_k1[layer], diff_lambda_q2[layer],
                         diff_lambda_k2[layer], diff_subln_w[layer], sink_logits[layer],
                         mla_q_norm_w[layer], mla_kv_norm_w[layer], w_uq[layer], w_ukv[layer],
                         w_out[layer])
    return x


def setup_inputs(seed=0):
    out = dict(first_inputs(seed))
    for name, value in second_inputs(seed + 1).items():
        if name != "x":
            out[name + "_2"] = value
    return out


def reference(
    x, c, ctx, c_ctx, ada_w, ada_b, pre_g, post_g, ev_w_in, ev_pool_w, ev_pool_scale, ev_conv_w,
    ev_conv_b, ev_w_out, od_w_in, od_onorm_g, od_w_out, lb_logits, positions_2, pre_norm_w_2,
    post_norm_w_2, w_in_2, diff_lambda_q1_2, diff_lambda_k1_2, diff_lambda_q2_2,
    diff_lambda_k2_2, diff_subln_w_2, sink_logits_2, mla_q_norm_w_2, mla_kv_norm_w_2, w_uq_2,
    w_ukv_2, w_out_2,
):
    x = first_block(
        x, c, ctx, c_ctx, ada_w, ada_b, pre_g, post_g, ev_w_in, ev_pool_w, ev_pool_scale,
        ev_conv_w, ev_conv_b, ev_w_out, od_w_in, od_onorm_g, od_w_out, lb_logits,
    )
    return second_block(
        x, positions_2, pre_norm_w_2, post_norm_w_2, w_in_2, diff_lambda_q1_2, diff_lambda_k1_2,
        diff_lambda_q2_2, diff_lambda_k2_2, diff_subln_w_2, sink_logits_2, mla_q_norm_w_2,
        mla_kv_norm_w_2, w_uq_2, w_ukv_2, w_out_2,
    )


_drawn_inputs = setup_inputs


def setup_inputs(seed=0):
    import zlib

    import numpy as np

    out = dict(_drawn_inputs(seed))
    spreads = {}
    factors = {'ev_conv_b': 8.0,
     'diff_subln_w_2': 10.553,
     'sink_logits_2': 27.149,
     'mla_q_norm_w_2': 8.0,
     'mla_kv_norm_w_2': 7.73}
    for name, (base, spread) in spreads.items():
        noise = np.random.default_rng([zlib.crc32(name.encode()), seed]).standard_normal(out[name].shape)
        drawn = base * np.exp(spread * noise) if base else spread * noise
        out[name] = __import__('jax').numpy.asarray(drawn.astype(out[name].dtype))
    for name, factor in factors.items():
        out[name] = (out[name] * factor).astype(out[name].dtype)
    return out
```

```python
import concourse.bass as bass
from concourse import mybir
from contextlib import ExitStack, contextmanager
import math

import numpy as np

F32 = mybir.dt.float32
F32R = mybir.dt.float32r
I32 = mybir.dt.int32
ACT = mybir.ActivationFunctionType
ALU = mybir.AluOpType
AX = mybir.AxisListType

P = 128
D = 2048
KT = D // P
SEQ = 256
TOK = 2 * SEQ
EPS = 1e-6
CHUNK = 64
NCH = TOK // CHUNK
POOL_WINDOWS = (2, 4, 8, 16)
POOL_W = D // 2
GRID_W = 64
PAD = max(POOL_WINDOWS) // 2
LATROW = GRID_W + 2 * PAD
CTXROW = SEQ + 2 * PAD
FLAT = (SEQ // GRID_W) * LATROW + CTXROW
HEADS = 16
BLK = 512
RAW = 4
SPL = 2

PARAM_ROWS = [
    [("c", 16), ("c_ctx", 16), ("ada_b", 96)],
    [("pre_g", 32), ("post_g", 32), ("ev_pool_scale", 8), ("ev_conv_w", 24), ("ev_conv_b", 8), ("od_onorm_g", 16)],
    [("lb_logits", 96), ("pre_norm_w_2", 32)],
    [("mla_q_norm_w_2", 8), ("mla_kv_norm_w_2", 8)],
]
PCOL = {}
for _t, _rows in enumerate(PARAM_ROWS):
    _at = 0
    for _name, _n in _rows:
        PCOL[_name] = _t * P + _at
        _at += _n

CONSTS = [("ident", P), ("ones", P), ("mask_f", P), ("mask_b", P), ("causal", 2 * P), ("band", 2 * P),
          ("reset", TOK), ("invf", 32), ("comb", 4), ("eps", 6)]
CCOL = {}
_at = 0
for _name, _n in CONSTS:
    CCOL[_name] = _at
    _at += _n
NCONST = _at


def shape_constants():
    c = np.zeros((P, NCONST), np.float32)

    def put(name, a):
        c[:, CCOL[name]:CCOL[name] + a.shape[1]] = a

    i = np.arange(P)
    put("ident", np.eye(P, dtype=np.float32))
    put("ones", np.ones((P, P), np.float32))
    same = (i[:, None] // CHUNK) == (i[None, :] // CHUNK)
    put("mask_f", (same & (i[:, None] <= i[None, :])).astype(np.float32))
    put("mask_b", (same & (i[:, None] >= i[None, :])).astype(np.float32))
    q, k = i[:, None] + P, np.arange(2 * P)[None, :]
    put("causal", np.where(k <= q, 0.0, -1e30).astype(np.float32))
    put("band", np.where((k <= q) & (q - k < 128), 0.0, -1e30).astype(np.float32))
    reset = np.ones((P, TOK), np.float32)
    reset[:, ::CHUNK] = 0.0
    put("reset", reset)
    put("invf", np.tile(np.power(np.float32(10000.0), -np.arange(0, 64, 2, dtype=np.float32) / np.float32(64)).astype(np.float32), (P, 1)))
    comb = np.zeros((P, 4), np.float32)
    comb[0, 0] = comb[2, 0] = comb[1, 1] = comb[3, 1] = 1.0
    put("comb", comb)
    lam = [0.8 - 0.6 * math.exp(-0.3 * l) for l in range(2)]
    put("eps", np.tile(np.array([EPS, 1e-5, *lam, *(1.0 - l for l in lam)], np.float32), (P, 1)))
    inv = np.zeros((4, TOK), np.float32)
    for g, w in enumerate(POOL_WINDOWS):
        def cnt(n):
            t = np.arange(n)
            return np.minimum(t + w // 2 - 1, n - 1) - np.maximum(t - w // 2, 0) + 1
        inv[g, :SEQ] = 1.0 / (cnt(SEQ // GRID_W)[:, None] * cnt(GRID_W)[None, :]).reshape(-1)
        inv[g, SEQ:] = 1.0 / cnt(SEQ)
    return c, inv


class Chain:

    def __init__(self, eng, sem):
        self.eng, self.sem, self.n, self.it, self.stride, self.base = eng, sem, 0, None, 0, 0

    def value(self):
        return self.n if self.it is None else self.it * self.stride + self.n

    def __call__(self, ins):
        self.n += 1
        ins.then_inc(self.sem, 1)
        return self

    def done(self):
        self.eng.wait_ge(self.sem, self.value())

    @contextmanager
    def loop(self, it, first, count, stride):
        start = self.n
        if isinstance(it, int):
            yield
            return
        self.it, self.stride = it, stride
        self.n = start - first * stride
        base = self.n
        yield
        assert self.n - base == stride, (self.sem, self.n - base)
        self.it = None
        self.n = start + count * stride


class Chunk:

    def __init__(self, number, raw, spl, arrived):
        self.number, self.raw, self.spl, self.arrived = number, raw, spl, arrived


class Stream:

    def __init__(self, phases):
        self.base, self.rawbase, self.loads = {}, {}, {}
        n, raw = RAW, [0] * RAW
        for name, times, loads in phases:
            assert len(loads) % RAW == 0
            self.base[name], self.rawbase[name], self.loads[name] = n, list(raw), loads
            n += times * len(loads)
            for c, l in enumerate(loads):
                raw[c % RAW] += 16 * l * times

    def chunk(self, name, it, c):
        loads = self.loads[name]
        slot = c % RAW
        per = 16 * sum(l for j, l in enumerate(loads) if j % RAW == slot)
        upto = 16 * sum(l for j, l in enumerate(loads[:c + 1]) if j % RAW == slot)
        return Chunk(it * len(loads) + (self.base[name] + c), slot, (self.base[name] + c) % SPL,
                     it * per + (self.rawbase[name][slot] + upto))

ARENA = 14848
MS = 66


def flat_rows(ap):
    names = "abcd"[:len(ap.shape)]
    flat = ap.rearrange(f"{' '.join(names)} -> ({' '.join(names)})") if len(names) > 1 else ap
    return flat.rearrange("(r p) -> r p", p=P)

A_Q, A_K, A_V, A_G, B_Q, B_K, B_G, C_Q, C_KV, C_KR, C_G = 0, 512, 1024, 1536, 2048, 3072, 3328, 4352, 4864, 5376, 5440
BLOCKS = [("cq", 4), ("ckv", 4), ("kvr", 4), ("bq0", 4), ("uq_nope", 1), ("uq_rope", 1), ("ukv_k", 1), ("ukv_v", 1),
          ("bq1", 4), ("bg0", 4), ("bg1", 4), ("aq", 4), ("ak", 4), ("av", 4), ("ag", 4), ("cg", 4)]
COLUMN = {"cq": C_Q, "ckv": C_KV, "bq0": B_Q, "bq1": B_Q + 512, "bg0": B_G, "bg1": B_G + 512, "aq": A_Q, "ak": A_K,
          "av": A_V, "ag": A_G, "cg": C_G}
BNUM = {name: i for i, (name, _) in enumerate(BLOCKS)}
BLOCK_OF = [i for i, (_, n) in enumerate(BLOCKS) for _ in range(n)]
NPROJ = len(BLOCK_OF)
HYB_LOADS = [{"kvr": 2, "uq_nope": 4, "uq_rope": 4, "ukv_k": 4, "ukv_v": 4}.get(BLOCKS[b][0], 1) for b in BLOCK_OF] + [1] * 16
PAIRS = [("m", 0), ("m", 1)] + [("b", i) for i in range(8)] + [("a", i) for i in range(4)]
NPAIR = len(PAIRS)
AFTER = {3: ["move cq"], 5: ["norm cq"], 7: ["move ckv"], 9: ["norm ckv"], 11: ["move kvr"], 12: ["turn kvr"],
         15: ["move bq0"], 16: ["turn bq0", "move uq_nope"], 17: ["move uq_rope"], 18: ["turn uq_rope", "move ukv_k"],
         19: ["move ukv_v"], 20: ["score 0"], 21: ["flip 0"], 22: ["weigh 0", "score 1"], 23: ["flip 1", "move bq1"],
         24: ["weigh 1", "turn bq1"], 25: ["score 2"], 26: ["flip 2"], 27: ["move bg0"], 28: ["weigh 2", "score 3"],
         29: ["flip 3"], 30: ["weigh 3", "score 4"], 31: ["flip 4", "move bg1"], 32: ["weigh 4", "score 5"], 33: ["flip 5"],
         34: ["weigh 5", "score 6"], 35: ["flip 6", "move aq"], 36: ["turn aq", "weigh 6", "score 7"], 37: ["flip 7"],
         38: ["weigh 7", "score 8"], 39: ["flip 8", "move ak"], 40: ["turn ak", "weigh 8", "score 9"], 41: ["flip 9"],
         42: ["weigh 9", "score 10"], 43: ["flip 10", "move av"], 44: ["weigh 10", "score 11"], 45: ["flip 11"],
         46: ["weigh 11", "score 12"], 47: ["flip 12", "move ag"], 48: ["weigh 12", "score 13"], 49: ["flip 13"],
         50: ["weigh 13"], 51: ["move cg"]}
USE45 = [x for i in sorted(AFTER) for x in AFTER[i] if x.split()[0] in ("norm", "score", "weigh")]
USE67 = [x for i in sorted(AFTER) for x in AFTER[i] if x.split()[0] in ("turn", "flip")]
TURNS = [x.split()[1] for i in sorted(AFTER) for x in AFTER[i] if x.startswith("turn")]
YT = KT // 2
TWO_PI = 6.283185307179586
PI_HI = 6.28125
PI_MID = float(np.float32(TWO_PI - PI_HI))
PI_LO = TWO_PI - PI_HI - PI_MID
ROUND = 12582912.0
ACT_STEPS = 24
DVE_STEPS = 135


def first_block_and_hybrid(nc, a):
    ctx = ExitStack()
    with ctx:
        def sb(name, shape, dt=F32):
            return ctx.enter_context(nc.sbuf_tensor(name, shape, dt))

        def sem(name):
            return ctx.enter_context(nc.semaphore(name))

        raw = sb("raw", [P, RAW, 4 * BLK])
        wh = sb("wh", [P, SPL, 4 * BLK], F32R)
        wl = sb("wl", [P, SPL, 4 * BLK], F32R)
        hTh = sb("hTh", [P, KT, TOK], F32R)
        hTl = sb("hTl", [P, KT, TOK], F32R)
        cst = sb("cst", [P, NCONST])
        prm = sb("prm", [P, 4 * P])
        adaT = sb("adaT", [P, 96, 2])
        s4 = sb("s4", [P, P], F32R)
        dg = sb("dg", [P, 4, P])
        small = sb("small", [P, 512])
        arena = sb("arena", [P, ARENA])

        ps = ctx.enter_context(nc.psum_tensor("ps", [P, 8, BLK], F32))
        x_save = nc.dram_tensor("x_save", (SEQ, D), F32, kind="Internal").ap()

        def C(name, n=None):
            w = dict(CONSTS)[name] if n is None else n
            return cst[:, CCOL[name]:CCOL[name] + w]

        ident, ones = C("ident"), C("ones")
        eps = C("eps")[:, 0:1]

        def area(at, *dims):
            n = int(np.prod(dims))
            v = arena[:, at:at + n]
            if len(dims) == 2:
                v = v.rearrange("p (a b) -> p a b", a=dims[0])
            if len(dims) == 3:
                v = v.rearrange("p (a b c) -> p a b c", a=dims[0], b=dims[1])
            return v

        X4 = area(0, 4, D)
        Y0 = area(0, KT, TOK)
        S0 = 4 * D
        HB = area(S0, 4, TOK)
        V = area(S0, 2, FLAT)
        SA = area(S0 + 2 * FLAT, 2, FLAT)
        SB_ = area(S0 + 4 * FLAT, 2, FLAT)
        G2 = area(S0 + 6 * FLAT, 2, TOK)
        PO = area(S0 + 6 * FLAT + 2 * TOK, 2, TOK)
        INV = area(S0 + 6 * FLAT + 4 * TOK, TOK)
        PW = area(S0 + 6 * FLAT + 5 * TOK, 2, 256)
        AROW = dg[:, :, :].rearrange("p a b -> p (a b)")
        GE = PO
        CX, CB, CC = area(S0, TOK), area(S0 + TOK, TOK), area(S0 + 2 * TOK, TOK)
        CT = area(S0 + 3 * TOK, 2, SEQ)
        CG, CE = area(S0 + 4 * TOK, TOK), INV
        U = area(S0 + 5 * TOK, 2, SEQ + 2)
        GB0 = area(S0, 2, D)
        XR0 = area(S0 + 2 * D, 2, D // 2)

        Y1 = area(0, KT, SEQ)
        W1 = 2 * D
        X1 = area(W1, 2, D)
        Z, R, B = (area(W1 + 2 * TOK * i, 2, TOK) for i in range(3))
        QD, KI = (area(W1 + 6 * TOK + TOK * i, 2, SEQ) for i in range(2))
        W1b = W1 + 8 * TOK
        Q, SG, GH = (area(W1b + SEQ * i, SEQ) for i in range(3))
        IT, V1, KD = area(W1b + 768, TOK), area(W1b + 1280, 4, P), area(W1b + 1792, 4, P)
        ST = area(W1b + 2304, 2, 4 * P)
        SX = area(W1b + 3328, 2, P)
        SC = area(W1b + 3584, 2, 2 * P)
        OS, RH = area(W1b + 4096, SEQ), area(W1b + 4352, SEQ)
        DEC = small[:, 360:376].rearrange("p (d n) -> p d n", d=2)
        GB1 = area(W1b + 4608, 1, D)
        XR1 = area(2 * W1, 2, D // 2)
        pT, pO = ps[:, 4, :], ps[:, 7, 0:SEQ]
        ORDER = [[4, 5, 6, 7, 0, 1, 2, 3], [7, 6, 5, 4, 3, 2, 1, 0]]
        Yt = area(0, 2, D)
        XN = X1
        M = 2 * D
        QN, QR, KN = area(M, 4, SEQ), area(M + 1024, 2, SEQ), area(M + 1536, 4, SEQ)
        KR, VC = area(M + 2560, SEQ), area(M + 2816, 2, BLK)
        AQ, AK, AV = area(M, 4, SEQ), area(M + 1024, 4, SEQ), area(M + 2048, 2, BLK)
        KS = area(M, 2, 3 * P)
        BK, BV = area(M + 3840, 2, SEQ), area(M + 4352, 2, P)
        BQ = area(M + 4608, 8, SEQ)
        SR, TM = area(M + 7680, 2, BLK), area(M + 8704, 2, SEQ)
        EX, PT = area(M + 9216, 2, 3 * P), area(M + 9984, 2, 3 * P)
        HQ = area(M + 9216, 4, SEQ)
        LQ = area(M + 9216, 4, 64)
        HBN = area(M + 4608, 4, SEQ)
        GBN = area(0, 1, D)
        XRN = area(D, 2, D // 2)
        DQ = area(M + 8704, 4, P)
        cosv = small[:, 8:72].rearrange("p (t d) -> p t d", t=2)
        sinv = small[:, 72:136].rearrange("p (t d) -> p t d", t=2)
        SUB = small[:, 136:264]
        SNK, NSK = small[:, 264:280], small[:, 316:332]
        NM, LS, ES, RL = (small[:, 280 + 4 * i:284 + 4 * i] for i in range(4))
        lamt, qss, qrs = small[:, 296:300], small[:, 304:308], small[:, 308:312]
        oss, ors, LN = small[:, 312:314], small[:, 314:316], small[:, 332:334]
        NL = small[:, 334:335]
        posf = small[:, 336:338]
        ang, turns_ = small[:, 376:440], small[:, 440:504]
        posi, posr = adaT.rearrange("p a b -> p (a b)")[0:2, 0:P].bitcast(I32), dg[0:2, 0, :]
        OJ = TM[:, :, 0:P]
        psA = ps[0:MS, 4, :]
        psT = ps[:, 5, 0:8].rearrange("p (a b) -> p a b", b=2)

        ssq = small[:, 0:4]
        rs = small[:, 4:8]
        silc = small[:, 8:40]
        sile = small[:, 40:72]
        lbt = small[:, 72:168].rearrange("p (d l k) -> p d l k", d=2, l=3)
        lbm = small[:, 168:200].rearrange("p (d k) -> p d k", d=2)
        lbs = small[:, 200:232].rearrange("p (d k) -> p d k", d=2)
        lb = small[:, 232:264]
        oml = small[:, 264:296]
        modA = small[:, 296:328].rearrange("p (k v) -> p k v", v=2)
        gp = small[:, 328:360].rearrange("p (k v) -> p k v", v=2)

        st = Stream([
            ("ada", 8, [1] * 4),
            ("pool", 4, [4] * 4 + [1] * 8),
            ("conv", 8, [4] * 4 + [1] * 4),
            ("out0", 2, [1] * 8),
            ("hg", 16, [2] * 8),
            ("out1", 2, [1] * 8),
            ("hyb", 2, HYB_LOADS),
        ])

        s_raw = [sem(f"raw_arrived{i}") for i in range(RAW)]
        s_load = sem("load_step")
        s_hi, s_lo, s_used = sem("high_ready"), sem("low_ready"), sem("chunk_used")
        s_dve, s_act = sem("dve_step"), sem("act_step")
        s_cst, s_prow, s_prT, s_prm = sem("const_arrived"), sem("param_rows"), sem("param_turned"), sem("param_ready")
        s_sil, s_s4h, s_s4 = sem("silu_ready"), sem("silu_high"), sem("silu_split")
        s_arow, s_adaP, s_adaT = sem("ada_row"), sem("ada_turned"), sem("ada_ready")
        s_mod = sem("mod_ready")
        s_xin = sem("x_arrived")
        s_rs, s_dg = sem("rstd_ready"), sem("diag_ready")
        s_pt, s_ph, s_phi, s_plo = sem("h_turned"), sem("h_ready"), sem("h_high"), sem("h_low")
        s_pz, s_pg = sem("pool_padding"), sem("pool_moved")
        s_inv, s_po, s_mix, s_py = sem("pool_consts"), sem("pooled"), sem("pool_mixed"), sem("pool_out")
        s_ce, s_cv = sem("conv_moved"), sem("conv_out")
        s_yh, s_yl = sem("y_high"), sem("y_low")
        s_gd, s_gb, s_gbe = sem("gate_diag"), sem("gate_spread"), sem("gate_moved")
        s_oe = sem("out_moved")
        s_xr, s_xa, s_save = [sem(f"residual_arrived{i}") for i in range(2)], sem("residual_added"), sem("x_saved")
        s_out = sem("result_stored")
        s_hev = sem("head_moved")
        s_f, s_ln, s_b, s_ex, s_kdr = sem("forget_ready"), sem("log_forget"), sem("decay_summed"), sem("decay_exp"), sem("keys_ready")
        s_vT, s_v, s_kT, s_kd = sem("v_turned"), sem("v_ready"), sem("k_turned"), sem("k_moved")
        s_ds, s_st, s_scp, s_sc = sem("state_steps"), sem("states_ready"), sem("scores"), sem("scores_masked")
        s_o, s_osq, s_sq, s_rso, s_y1 = sem("head_summed"), sem("head_squared"), sem("squares_summed"), sem("head_rstd"), sem("head_out")
        s_sgr = sem("head_gate")
        s_l1 = sem("layer1_region_free")
        s_pos, s_posf, s_posT, s_ang, s_sin = sem("positions"), sem("positions_float"), sem("positions_turned"), sem("angles"), sem("sines")
        s_lp, s_lam, s_lamx = sem("layer_params"), sem("lambda_parts"), sem("lambda_exp")
        s_bm = [sem(f"block_moved{i}") for i in range(2)]
        s_45, s_67 = sem("banks45_read"), sem("banks67_read")
        s_qs, s_qd, s_qn, s_qh, s_qhi, s_qlo = sem("rank_stats"), sem("rank_diag"), sem("rank_turned"), sem("rank_scaled"), sem("rank_high"), sem("rank_low")
        s_rr, s_tn = sem("roped"), sem("block_turned")
        s_S, s_nm, s_e, s_p = sem("scored"), sem("max_ready"), sem("exp_ready"), sem("probs_ready")
        s_fl, s_W, s_os = sem("probs_flipped"), sem("weighed"), sem("head_norm_ready")
        s_gx = sem("gate_exp")
        s_yt, s_yth, s_ytl = sem("y_turned"), sem("y_turned_high"), sem("y_turned_low")
        s_gl, s_ld = sem("post_norm_arrived"), sem("layer_done")

        block = ctx.enter_context(nc.Block())

        adaw = a["ada_w"].rearrange("l (c t p) n -> l c p t n", t=4, p=P)
        evw = a["ev_w_in"][0]
        w_out0 = a["ev_w_out"][0].rearrange("(c t p) n -> c p t n", t=4, p=P)

        @block.sync
        def _(sp):
            def load(ch, pieces):
                sp.wait_ge(s_lo, ch.number - (RAW - 1))
                sp.sem_inc(s_load, 1)
                for dst, src in pieces:
                    sp.dma_start(dst, src).then_inc(s_raw[ch.raw], 16)

            def slot4(ch):
                return raw[:, ch.raw, :].rearrange("p (t n) -> p t n", t=4)

            with sp.Fori(0, 8) as b:
                for c in range(4):
                    ch = st.chunk("ada", b, c)
                    load(ch, [(slot4(ch), adaw[0, c][:, :, bass.ds(b * BLK, BLK)])])
            for g in range(4):
                for c in range(4):
                    ch = st.chunk("pool", g, c)
                    load(ch, [(raw[:, ch.raw, t * BLK:(t + 1) * BLK].rearrange("p (a n) -> p a n", a=2),
                               evw[(4 * c + t) * P:(4 * c + t + 1) * P, 0:2 * POOL_W]
                               .rearrange("p (a n) -> p a n", a=2)[:, :, g * 256:(g + 1) * 256]) for t in range(4)])
                for c in range(8):
                    b = 8 + 2 * g + c // 4
                    ch = st.chunk("pool", g, 4 + c)
                    load(ch, [(slot4(ch), adaw[b // 12, c % 4][:, :, (b % 12) * BLK:(b % 12 + 1) * BLK])])
            with sp.Fori(0, 8) as j:
                for c in range(4):
                    ch = st.chunk("conv", j, c)
                    load(ch, [(raw[:, ch.raw, t * BLK:(t + 1) * BLK].rearrange("p (a n) -> p a n", a=4),
                               evw[(4 * c + t) * P:(4 * c + t + 1) * P, 2 * POOL_W:]
                               .rearrange("p (a n) -> p a n", a=4)[:, :, bass.ds(j * P, P)]) for t in range(4)])
                for c in range(4):
                    ch = st.chunk("conv", j, 4 + c)
                    load(ch, [(slot4(ch), adaw[1, c][:, :, bass.ds(j * BLK + 4 * BLK, BLK)])])
            with sp.Fori(0, 2) as i:
                for c in range(8):
                    ch = st.chunk("out0", i, c)
                    load(ch, [(slot4(ch), w_out0[c % 4][:, :, bass.ds(i * (2 * BLK) + (c // 4) * BLK, BLK)])])
            odw = a["od_w_in"][0]
            with sp.Fori(0, HEADS) as h:
                for c in range(8):
                    ch = st.chunk("hg", h, c)
                    load(ch, [(raw[:, ch.raw, t * 5 * P:(t + 1) * 5 * P].rearrange("p (a n) -> p a n", a=5),
                               odw[(2 * c + t) * P:(2 * c + t + 1) * P, :].rearrange("p (a n) -> p a n", a=5)[:, :, bass.ds(h * P, P)])
                              for t in range(2)])
            w_out1 = a["od_w_out"][0].rearrange("(c t p) n -> c p t n", t=4, p=P)
            with sp.Fori(0, 2) as i:
                for c in range(8):
                    ch = st.chunk("out1", i, c)
                    load(ch, [(slot4(ch), w_out1[c % 4][:, :, bass.ds(i * (2 * BLK) + (c // 4) * BLK, BLK)])])
            w_in2 = a["w_in_2"].rearrange("l (c t p) n -> l c p t n", t=4, p=P)
            w_out2 = a["w_out_2"].rearrange("l (c t p) n -> l c p t n", t=4, p=P)
            layer = lambda x, L: x[bass.ds(L, 1)]
            one = lambda x: x.rearrange("o p t n -> (o p) t n")
            with sp.Fori(0, 2) as L:
                for i in range(NPROJ):
                    name = BLOCKS[BLOCK_OF[i]][0]
                    c = i - BLOCK_OF.index(BLOCK_OF[i])
                    ch = st.chunk("hyb", L, i)
                    if name in COLUMN:
                        load(ch, [(slot4(ch), one(layer(w_in2[:, c], L)[:, :, :, COLUMN[name]:COLUMN[name] + BLK]))])
                    elif name == "kvr":
                        dst = raw[:, ch.raw, 0:4 * 320].rearrange("p (t n) -> p t n", t=4)
                        load(ch, [(dst[:, :, 0:256], one(layer(w_in2[:, c], L)[:, :, :, B_K:B_K + 256])),
                                  (dst[:, :, 256:320], one(layer(w_in2[:, c], L)[:, :, :, C_KR:C_KR + 64]))])
                    else:
                        w, per, first, n = {"uq_nope": ("w_uq_2", 192, 0, 128), "uq_rope": ("w_uq_2", 192, 128, 64),
                                            "ukv_k": ("w_ukv_2", 256, 0, 128), "ukv_v": ("w_ukv_2", 256, 128, 128)}[name]
                        load(ch, [(raw[:, ch.raw, t * 4 * n:(t + 1) * 4 * n].rearrange("p (a n) -> p a n", a=4),
                                   one(layer(a[w][:, t * P:(t + 1) * P, :].rearrange("l p (a n) -> l p a n", n=per), L)[:, :, :, first:first + n]))
                                  for t in range(4)])
                for i in range(16):
                    ch = st.chunk("hyb", L, NPROJ + i)
                    load(ch, [(slot4(ch), one(layer(w_out2[:, i % 4], L)[:, :, :, (i // 4) * BLK:(i // 4 + 1) * BLK]))])
            sp.wait_ge(s_xa, 20)
            for t in range(2):
                sp.dma_start(a["out"][0, t * P:(t + 1) * P, :], XN[:, t, :]).then_inc(s_out, 16)
            sp.wait_ge(s_out, 32)

        @block.scalar
        def _(act):
            step = Chain(act, s_act)

            def hi(ch, n=4 * BLK):
                act.wait_ge(s_raw[ch.raw], ch.arrived)
                act.wait_ge(s_used, ch.number - (SPL - 1))
                nc.scalar.activation(wh[:, ch.spl, 0:n], raw[:, ch.raw, 0:n], ACT.Copy).then_inc(s_hi, 1)

            act.sem_inc(s_hi, RAW)
            act.dma_start(cst[:, :], a["consts"]).then_inc(s_cst, 16)
            for t, rows in enumerate(PARAM_ROWS):
                at = 0
                for name, n in rows:
                    act.dma_start(dg[at:at + n, t, :], flat_rows(a[name])).then_inc(s_prow, 16)
                    at += n
            for t in range(4):
                src = a["x"][0] if t < 2 else a["ctx"][0]
                act.dma_start(X4[:, t, :], src[(t % 2) * P:(t % 2 + 1) * P, :]).then_inc(s_xin, 16)
            act.wait_ge(s_prm, 1)
            nc.scalar.activation(sile, prm[:, 0:32], ACT.Exp, scale=-1.0).then_inc(s_sil, 1)
            act.wait_ge(s_sil, 2)
            act.wait_ge(s_s4, 1)
            nc.scalar.activation(s4[:, 0:4 * KT].rearrange("p (k v) -> p k v", v=4)[:, :, 0:2], silc.rearrange("p (v k) -> p k v", v=2), ACT.Copy).then_inc(s_s4h, 1)
            act.wait_ge(s_sil, 3)
            nc.scalar.activation(lbt, lbt, ACT.Exp).then_inc(s_sil, 1)

            with act.Fori(0, 8) as b:
                for c in range(4):
                    hi(st.chunk("ada", b, c))

            def sums(X, T, ready):
                for t in range(T):
                    ready(t)
                    step(nc.scalar.activation(ps[:, 0:4, :], X[:, t, :].rearrange("p (a b) -> p a b", a=4), ACT.Square,
                                              accum_out=ssq[:, t:t + 1])).done()
                step(nc.scalar.activation(rs[:, 0:T], ssq[:, 0:T], ACT.Ln, scale=1.0 / D, bias=eps)).done()
                nc.scalar.activation(rs[:, 0:T], rs[:, 0:T], ACT.Exp, scale=-0.5).then_inc(s_rs, 1)

            def high_h(r, hb, n):
                for k in range(KT):
                    act.wait_ge(s_ph, r * KT + (k + 1))
                    nc.scalar.activation(hTh[:, k, 0:n], hb[:, k % 4, 0:n], ACT.Copy).then_inc(s_phi, 1)

            act.wait_ge(s_xin, 64)
            sums(X4, 4, lambda t: None)
            high_h(0, HB, TOK)

            for g in range(4):
                for c in range(4):
                    hi(st.chunk("pool", g, c))
                if g:
                    act.wait_ge(s_po, g)
                    act.wait_ge(s_py, g)
                else:
                    act.wait_ge(s_pz, 1)
                act.dma_start(INV, a["inv"][g]).then_inc(s_inv, 16)
                act.dma_start(PW, a["ev_pool_w"][0, g].rearrange("(a p) o -> p a o", p=P)).then_inc(s_inv, 16)
                act.wait_ge(s_used, st.chunk("pool", g, 3).number + 1)
                for t in range(2):
                    nc.scalar.activation(V[:, t, 0:4 * LATROW].rearrange("p (r c) -> p r c", r=4)[:, :, PAD:PAD + GRID_W],
                                         ps[:, t, 0:SEQ].rearrange("p (r c) -> p r c", r=4), ACT.Copy)
                    nc.scalar.activation(V[:, t, 4 * LATROW + PAD:4 * LATROW + PAD + SEQ], ps[:, t, SEQ:TOK], ACT.Copy)
                nc.scalar.activation(G2, ps[:, 2:4, :], ACT.Copy)
                nc.scalar.activation(GE, ps[:, 2:4, :], ACT.Exp, scale=-1.0).then_inc(s_pg, 1)
                for c in range(4, 12):
                    hi(st.chunk("pool", g, c))

            def conv_block(j):
                for c in range(4):
                    hi(st.chunk("conv", j, c))
                act.wait_ge(s_used, st.chunk("conv", j, 3).number + 1)
                act.wait_ge(s_cv, j + 1)
                nc.scalar.activation(CX, ps[:, 0, :], ACT.Copy)
                nc.scalar.activation(CB, ps[:, 1, :], ACT.Copy)
                nc.scalar.activation(CC, ps[:, 2, :], ACT.Copy)
                nc.scalar.activation(CG, ps[:, 3, :], ACT.Copy)
                nc.scalar.activation(CE, ps[:, 3, :], ACT.Exp, scale=-1.0).then_inc(s_ce, 1)
                for c in range(4, 8):
                    hi(st.chunk("conv", j, c))

            conv_block(0)
            with act.Fori(1, 8) as j:
                conv_block(j)
            act.wait_ge(s_cv, 9)
            for k in range(KT):
                nc.scalar.activation(hTh[:, k, :], Y0[:, k, :], ACT.Copy).then_inc(s_yh, 1)

            def spread(r, q, v, G):
                act.wait_ge(s_gb, r + 1)
                nc.scalar.activation(G[:, v, q * BLK:(q + 1) * BLK], ps[:, 6 + r % 2, :], ACT.Copy).then_inc(s_gbe, 1)

            for v in range(2):
                for q in range(4):
                    spread(4 * v + q, q, v, GB0)

            with act.Fori(0, 2) as i:
                for n in range(2):
                    for c in range(4):
                        hi(st.chunk("out0", i, 4 * n + c))
                    act.wait_ge(s_used, st.chunk("out0", i, 4 * n + 3).number + 1)
                    if n == 0:
                        act.wait_ge(s_yl, KT)
                    for t in range(4):
                        ins = nc.scalar.activation(X4[:, t, bass.ds(i * (2 * BLK) + n * BLK, BLK)], ps[:, 4 * n + t, :], ACT.Copy)
                    ins.then_inc(s_oe, 1)

            def residual(T, src, XR, base, x1, save):
                for u in range(2 * T):
                    if u >= 2:
                        act.wait_ge(s_xa, base + (u - 1))
                    act.dma_start(XR[:, u % 2, :], src(u // 2)[:, (u % 2) * (D // 2):(u % 2 + 1) * (D // 2)]).then_inc(s_xr[u % 2], 16)

            act.wait_ge(s_oe, 6)
            sums(X4, 4, lambda t: None)
            residual(4, lambda t: (a["x"][0] if t < 2 else a["ctx"][0])[(t % 2) * P:(t % 2 + 1) * P, :], XR0, 0, X4, None)
            def save(X, need, count):
                act.wait_ge(s_xa, need)
                for t in range(2):
                    act.dma_start(x_save[t * P:(t + 1) * P, :], X[:, t, :]).then_inc(s_save, 16)

            act.wait_ge(s_xa, 8)
            save(X4, 4, 0)
            for q in range(4):
                spread(8 + q, q, 0, GB1)
            sums(X4, 4, lambda t: None)
            high_h(1, HB, TOK)

            def head(h, proj, comp):
                def split(c):
                    if proj:
                        hi(st.chunk("hg", h, c), 10 * P)

                split(0)
                if comp:
                    act.wait_ge(s_used, st.chunk("hg", h, 0).number)
                    act.wait_ge(s_y1, h)
                    for d in range(2):
                        nc.scalar.activation(Z[:, d, :], ps[:, d, :], ACT.Exp, scale=-1.0).then_inc(s_hev, 1)
                    nc.scalar.activation(IT, ps[:, 2, :], ACT.Copy).then_inc(s_hev, 1)
                    nc.scalar.activation(Q, ps[:, 3, 0:SEQ], ACT.Copy)
                    nc.scalar.activation(SG, ps[:, 3, SEQ:TOK], ACT.Copy)
                    nc.scalar.activation(GH, ps[:, 3, SEQ:TOK], ACT.Exp, scale=-1.0).then_inc(s_hev, 1)
                split(1)

                def log_forget(d):
                    act.wait_ge(s_f, h * 2 - 1 + d)
                    nc.scalar.activation(R[:, d, :], R[:, d, :], ACT.Ln).then_inc(s_ln, 1)

                def decays(d):
                    act.wait_ge(s_b, h * 2 - 1 + d)
                    last = B[:, d, :].rearrange("p (n c) -> p n c", c=CHUNK)[:, :, CHUNK - 1] if d == 0 else \
                        B[:, d, :].rearrange("p (n c) -> p n c", c=CHUNK)[:, :, 0]
                    nc.scalar.activation(R[:, d, :], R[:, d, :], ACT.Exp)
                    nc.scalar.activation(QD[:, d, :], B[:, d, 0:SEQ], ACT.Exp)
                    nc.scalar.activation(KI[:, d, :], B[:, d, 0:SEQ], ACT.Exp, scale=-1.0)
                    nc.scalar.activation(DEC[:, d, :], last, ACT.Exp).then_inc(s_ex, 1)

                if comp:
                    log_forget(0)
                    act.wait_ge(s_vT, h)
                    nc.scalar.activation(V1, pT.rearrange("p (a b) -> p a b", a=4), ACT.Copy).then_inc(s_v, 1)
                split(2)
                if comp:
                    decays(0)
                    log_forget(1)
                split(3)
                if comp:
                    decays(1)
                for c in range(4, 8):
                    split(c)
                if comp:
                    act.wait_ge(s_o, h)
                    nc.scalar.activation(OS, pO, ACT.Square).then_inc(s_osq, 1)
                    act.wait_ge(s_sq, h)
                    step(nc.scalar.activation(RH, pT[:, 0:SEQ], ACT.Ln, scale=1.0 / P, bias=eps)).done()
                    nc.scalar.activation(RH, RH, ACT.Exp, scale=-0.5).then_inc(s_rso, 1)

            act.wait_ge(s_save, 32)
            act.wait_ge(s_plo, 2 * KT)
            act.wait_ge(s_l1, 1)
            act.sem_inc(s_rso, 1)
            head(0, True, False)
            with act.Fori(1, HEADS) as h, step.loop(h, 1, HEADS - 1, 1):
                head(h, True, True)
            head(HEADS, False, True)

            def high_y(Yk, n):
                for k in range(KT):
                    nc.scalar.activation(hTh[:, k, 0:n], Yk(k), ACT.Copy).then_inc(s_yh, 1)

            act.wait_ge(s_y1, HEADS + 1)
            high_y(lambda k: Y1[:, k, :], SEQ)
            with act.Fori(0, 2) as i:
                for n in range(2):
                    for c in range(4):
                        hi(st.chunk("out1", i, 4 * n + c))
                    act.wait_ge(s_used, st.chunk("out1", i, 4 * n + 3).number + 1)
                    for t in range(2):
                        ins = nc.scalar.activation(X1[:, t, bass.ds(i * (2 * BLK) + n * BLK, BLK)], ps[:, 2 * n + t, :], ACT.Copy)
                    ins.then_inc(s_oe, 1)
            act.wait_ge(s_oe, 10)
            sums(X1, 2, lambda t: None)
            residual(2, lambda t: x_save[t * P:(t + 1) * P, :], XR1, 8, X1, None)
            act.wait_ge(s_xa, 12)
            act.dma_start(posi, a["positions_2"][0].rearrange("(t p) -> t p", t=2)).then_inc(s_pos, 16)
            act.wait_ge(s_ang, 1)
            nc.scalar.activation(small[:, 8:136], small[:, 8:136], ACT.Sin).then_inc(s_sin, 1)

            def hyb_split(L, i):
                width = {"kvr": 4 * 320, "uq_rope": 4 * 256}.get(BLOCKS[BLOCK_OF[i]][0], 4 * BLK)
                hi(st.chunk("hyb", L, i), width)

            def hyb_layer(L):
                count = lambda total, n: L * total + n
                banks = lambda b: ps[:, 2 * (b % 2):2 * (b % 2) + 2, :]
                act.wait_ge(s_xa, L * 4 + 12)
                save(XN, L * 4 + 12, 0)
                for i, n in enumerate(("q1", "k1", "q2", "k2")):
                    act.dma_start(LQ[:, i, :], a[f"diff_lambda_{n}_2"][bass.ds(L, 1), :].rearrange("o n -> (o n)").partition_broadcast(P)).then_inc(s_lp, 16)
                act.dma_start(SUB, a["diff_subln_w_2"][bass.ds(L, 1), :].rearrange("o n -> (o n)").partition_broadcast(P)).then_inc(s_lp, 16)
                act.dma_start(SNK, a["sink_logits_2"][bass.ds(L, 1), :].rearrange("o n -> (o n)").partition_broadcast(P)).then_inc(s_lp, 16)
                act.wait_ge(s_lam, count(1, 1))
                nc.scalar.activation(lamt[:, 0:2], lamt[:, 0:2], ACT.Exp).then_inc(s_lamx, 1)
                sums(XN, 2, lambda t: None)
                high_h(L + 2, HBN, SEQ)
                act.wait_ge(s_save, L * 32 + 64)

                def read67(x):
                    return count(len(USE67), USE67.index(x) + 1)

                def done(i):
                    b = BLOCK_OF[i]
                    act.wait_ge(s_used, st.chunk("hyb", L, i).number + 1)
                    return b, BLOCKS[b][0]

                def move(name, i):
                    b, _ = done(i)
                    if name in ("cq", "ckv"):
                        v = ("cq", "ckv").index(name)
                        dst = (SR, VC)[v]
                        for t in range(2):
                            step(nc.scalar.activation(dst[:, t, :], banks(b)[:, t, :], ACT.Square, accum_out=qss[:, 2 * v + t:2 * v + t + 1])).done()
                        nc.scalar.activation(dst, banks(b), ACT.Copy).then_inc(s_bm[b % 2], 1)
                        step(nc.scalar.activation(qrs[:, 2 * v:2 * v + 2], qss[:, 2 * v:2 * v + 2], ACT.Ln, scale=1.0 / 512, bias=eps)).done()
                        nc.scalar.activation(qrs[:, 2 * v:2 * v + 2], qrs[:, 2 * v:2 * v + 2], ACT.Exp, scale=-0.5).then_inc(s_qs, 1)
                    elif name in ("uq_nope", "ukv_k"):
                        dst = QN if name == "uq_nope" else KN
                        nc.scalar.activation(dst.rearrange("p (a b) c -> p a b c", a=2), banks(b).rearrange("p a (b c) -> p a b c", b=2),
                                             ACT.Copy).then_inc(s_bm[b % 2], 1)
                    elif name in ("ukv_v", "av"):
                        nc.scalar.activation(VC if name == "ukv_v" else AV, banks(b), ACT.Copy).then_inc(s_bm[b % 2], 1)
                    elif name[1] == "g":
                        if name in ("bg0", "ag"):
                            act.wait_ge(s_tn, count(len(TURNS), TURNS.index("bq1" if name == "bg0" else "ak") + 1))
                        else:
                            before = BNUM["bg0" if name == "bg1" else "ag"]
                            act.wait_ge(s_bm[before % 2], count(len(BLOCKS) // 2, before // 2 + 1))
                        nc.scalar.activation(SR, banks(b), ACT.Exp, scale=-1.0).then_inc(s_gx, 1)

                def norm(name):
                    v = ("cq", "ckv").index(name)
                    for k in range(4):
                        act.wait_ge(s_qh, count(8, 4 * v + k + 1))
                        nc.scalar.activation(hTh[:, 4 * v + k, SEQ:TOK], HQ[:, k, :], ACT.Copy).then_inc(s_qhi, 1)

                def turn_move(name):
                    act.wait_ge(s_tn, count(len(TURNS), TURNS.index(name) + 1))
                    if name == "kvr":
                        nc.scalar.activation(KR, ps[:, 7, 0:SEQ], ACT.Copy)
                        src, dst = ps[:, 6, :].rearrange("p (a b) -> p a b", a=2), BK
                    elif name == "uq_rope":
                        src, dst = ps[:, 6, :].rearrange("p (a b) -> p a b", a=2), QR
                    else:
                        src = ps[:, 6:8, :].rearrange("p x (a b) -> p x a b", a=2)
                        dst = {"bq0": BQ[:, 0:4, :], "bq1": BQ[:, 4:8, :], "aq": AQ, "ak": AK}[name].rearrange("p (x a) b -> p x a b", x=2)
                    nc.scalar.activation(dst, src, ACT.Copy).then_inc(s_67, 1)

                def score(n):
                    act.wait_ge(s_nm, count(NPAIR, n + 1))
                    for q, seg in ((0, slice(0, 2 * P)), (1, slice(2 * P, 3 * P))):
                        for m in range(2):
                            at = 2 * q + m
                            ins = nc.scalar.activation(EX[:, m, seg], EX[:, m, seg], ACT.Exp, bias=NM[:, at:at + 1], accum_out=LS[:, at:at + 1])
                    if PAIRS[n][0] == "b":
                        ins = nc.scalar.activation(ES, ES, ACT.Exp)
                    ins.then_inc(s_e, 1)

                def flip(n):
                    act.wait_ge(s_fl, count(NPAIR, n + 1))
                    if n:
                        act.wait_ge(s_W, count(NPAIR, n))
                    k = 1 if PAIRS[n][0] == "a" else 2
                    nc.scalar.activation(PT[:, 0:k, :], ps[:, 6:6 + k, 0:3 * P], ACT.Copy).then_inc(s_67, 1)

                def weigh(n):
                    kind, h = PAIRS[n]
                    if kind == "a":
                        act.wait_ge(s_W, count(NPAIR, n + 1))
                        for q in range(2):
                            step(nc.scalar.activation(OJ[:, q, :], ps[:, 4, q * P:(q + 1) * P], ACT.Square, accum_out=oss[:, q:q + 1]))
                        step.done()
                        step(nc.scalar.activation(ors, oss, ACT.Ln, scale=1.0 / P, bias=C("eps")[:, 1:2])).done()
                        nc.scalar.activation(ors, ors, ACT.Exp, scale=-0.5).then_inc(s_os, 1)

                def after(i):
                    for what in AFTER.get(i, []):
                        verb, arg = what.split()
                        if verb == "move":
                            move(arg, i)
                        elif verb == "norm":
                            norm(arg)
                        elif verb == "turn":
                            turn_move(arg)
                        else:
                            {"score": score, "flip": flip, "weigh": weigh}[verb](int(arg))

                hyb_split(L, 0)
                for i in range(NPROJ):
                    if i + 1 < NPROJ:
                        hyb_split(L, i + 1)
                    after(i)
                for g in range(YT):
                    act.wait_ge(s_yt, count(YT, g + 1))
                    nc.scalar.activation(hTh[:, 2 * g:2 * g + 2, 0:SEQ], ps[:, 4 + g % 4, :].rearrange("p (a b) -> p a b", a=2),
                                         ACT.Copy).then_inc(s_yth, 1)
                act.wait_ge(s_yt, count(YT, YT))
                act.dma_start(GBN[:, 0, :], a["post_norm_w_2"][bass.ds(L, 1), :].rearrange("o n -> (o n)").partition_broadcast(P)).then_inc(s_gl, 16)
                for n in range(4):
                    for c in range(4):
                        hi(st.chunk("hyb", L, NPROJ + 4 * n + c))
                    act.wait_ge(s_used, st.chunk("hyb", L, NPROJ + 4 * n + 3).number + 1)
                    nc.scalar.activation(XN[:, :, n * BLK:(n + 1) * BLK], ps[:, 2 * (n % 2):2 * (n % 2) + 2, :], ACT.Copy).then_inc(s_oe, 1)
                act.wait_ge(s_oe, L * 4 + 14)
                sums(XN, 2, lambda t: None)
                residual(2, lambda t: x_save[t * P:(t + 1) * P, :], XRN, L * 4 + 12, XN, None)

            with act.Fori(0, 2) as L, step.loop(L, 0, 2, ACT_STEPS):
                hyb_layer(L)

        @block.tensor
        def _(pe):
            def three(out, w_h, w_l, x_h, x_l, first, last, weights_still=True):
                if weights_still:
                    nc.tensor.matmul(out, w_h, x_h, start=first, stop=False, skip_group_check=True)
                    nc.tensor.matmul(out, w_h, x_l, start=False, stop=False, skip_group_check=True)
                    return nc.tensor.matmul(out, w_l, x_h, start=False, stop=last, skip_group_check=True)
                nc.tensor.matmul(out, x_h, w_h, start=first, stop=False, skip_group_check=True)
                nc.tensor.matmul(out, x_h, w_l, start=False, stop=False, skip_group_check=True)
                return nc.tensor.matmul(out, x_l, w_h, start=False, stop=last, skip_group_check=True)

            pe.sem_inc(s_used, RAW)
            pe.wait_ge(s_cst, 16)
            pe.wait_ge(s_prow, 16 * sum(len(r) for r in PARAM_ROWS))
            for t, rows in enumerate(PARAM_ROWS):
                n = sum(x for _, x in rows)
                ins = nc.tensor.transpose(ps[:, 5, t * P:t * P + n], dg[0:n, t, :], ident[0:n, 0:n])
            ins.then_inc(s_prT, 1)

            def ada_block(chunks, b):
                for c, ch in enumerate(chunks):
                    pe.wait_ge(s_lo, ch.number + 1)
                    if c == 0:
                        pe.wait_ge(s_arow, b)
                    for t in range(4):
                        k = 4 * c + t
                        nc.tensor.matmul(psA, s4[:, 4 * k:4 * k + MS], wh[:, ch.spl, t * BLK:(t + 1) * BLK], start=(k == 0), stop=False)
                        ins = nc.tensor.matmul(psA, s4[:, 4 * k:4 * k + MS], wl[:, ch.spl, t * BLK:(t + 1) * BLK], start=False, stop=(k == KT - 1))
                    ins.then_inc(s_used, 1)
                pe.wait_ge(s_arow, b + 1)
                pe.wait_ge(s_adaT, b)
                for t in range(4):
                    ins = nc.tensor.matmul(psT[:, t, :], AROW[0:4, t * P:(t + 1) * P], C("comb")[0:4, 0:2],
                                           start=(t == 0), stop=(t == 3), skip_group_check=True)
                ins.then_inc(s_adaP, 1)

            pe.wait_ge(s_s4, 2)
            pe.wait_ge(s_prm, 1)
            with pe.Fori(0, 8) as b:
                ada_block([st.chunk("ada", b, c) for c in range(4)], b + 1)

            def turn(r, X, T):
                pe.wait_ge(s_dg, r + 1)
                for k in range(KT):
                    if k >= 4:
                        pe.wait_ge(s_ph, r * KT + (k - 3))
                    for t in range(T):
                        ins = nc.tensor.matmul(ps[:, k % 4, t * P:(t + 1) * P], X[:, t, k * P:(k + 1) * P], dg[:, t, :],
                                               start=(t == 0), stop=(t == T - 1), skip_group_check=True)
                    ins.then_inc(s_pt, 1)

            turn(0, X4, 4)

            def proj4(chunks, c0):
                for c, ch in enumerate(chunks):
                    pe.wait_ge(s_lo, ch.number + 1)
                    for t in range(4):
                        k = 4 * (c0 + c) + t
                        for f in range(4):
                            w = slice(t * BLK + f * P, t * BLK + (f + 1) * P)
                            ins = three(ps[:, f, :], wh[:, ch.spl, w], wl[:, ch.spl, w], hTh[:, k, :], hTl[:, k, :],
                                        k == 0, k == KT - 1)
                    ins.then_inc(s_used, 1)

            def mix(g):
                pe.wait_ge(s_po, g + 1)
                pe.wait_ge(s_inv, 32 * (g + 1))
                for o in range(2):
                    for i in range(2):
                        ins = nc.tensor.matmul(ps[:, 6 + o, :], PW[:, i, o * P:(o + 1) * P], PO[:, i, :],
                                               start=(i == 0), stop=(i == 1))
                ins.then_inc(s_mix, 1)

            pe.wait_ge(s_plo, KT)
            for g in range(4):
                if g:
                    pe.wait_ge(s_pg, g)
                proj4([st.chunk("pool", g, c) for c in range(2)], 0)
                if g:
                    if g > 1:
                        pe.wait_ge(s_py, g - 1)
                    mix(g - 1)
                proj4([st.chunk("pool", g, c) for c in range(2, 4)], 2)
                for h in range(2):
                    ada_block([st.chunk("pool", g, 4 + 4 * h + c) for c in range(4)], 9 + 2 * g + h)
            pe.wait_ge(s_pg, 4)
            proj4([st.chunk("conv", 0, c) for c in range(2)], 0)
            pe.wait_ge(s_py, 3)
            mix(3)
            proj4([st.chunk("conv", 0, c) for c in range(2, 4)], 2)
            ada_block([st.chunk("conv", 0, 4 + c) for c in range(4)], 17)
            with pe.Fori(1, 8) as j:
                pe.wait_ge(s_ce, j)
                proj4([st.chunk("conv", j, c) for c in range(4)], 0)
                ada_block([st.chunk("conv", j, 4 + c) for c in range(4)], j + 17)

            def gate_rows(r):
                pe.wait_ge(s_gd, r + 1)
                if r >= 2:
                    pe.wait_ge(s_gbe, r - 1)
                elif r == 0:
                    pe.wait_ge(s_py, 4)
                nc.tensor.matmul(ps[:, 6 + r % 2, :], ones, dg[:, :, :], start=True, stop=True).then_inc(s_gb, 1)

            for r in range(8):
                gate_rows(r)

            def out_block(chunks, T, bank):
                for c, ch in enumerate(chunks):
                    pe.wait_ge(s_lo, ch.number + 1)
                    for t in range(4):
                        k = 4 * c + t
                        for m in range(T):
                            ins = three(ps[:, bank + m, :], wh[:, ch.spl, t * BLK:(t + 1) * BLK],
                                        wl[:, ch.spl, t * BLK:(t + 1) * BLK],
                                        hTh[:, k, m * P:(m + 1) * P], hTl[:, k, m * P:(m + 1) * P],
                                        k == 0, k == KT - 1, False)
                    ins.then_inc(s_used, 1)

            pe.wait_ge(s_yl, KT)
            pe.wait_ge(s_gbe, 8)
            pe.wait_ge(s_adaT, 25)
            with pe.Fori(0, 2) as i:
                for n in range(2):
                    pe.wait_ge(s_oe, i * 2 + (n + 1))
                    out_block([st.chunk("out0", i, 4 * n + c) for c in range(4)], 4, 4 * n)
            for r in range(8, 12):
                gate_rows(r)
            turn(1, X4, 4)

            def head_proj(h, c, banks):
                ch = st.chunk("hg", h, c)
                pe.wait_ge(s_lo, ch.number + 1)
                order = [(t, f) for t in range(2) for f in range(5)] if c else [(t, f) for f in range(5) for t in range(2)]
                for t, f in order:
                    k = 2 * c + t
                    w = slice((5 * t + f) * P, (5 * t + f + 1) * P)
                    if k == 0 and banks and f < 4:
                        pe.wait_ge(s_hev, h * 4 - 3 + f)
                    n = TOK if f < 3 else SEQ
                    out = ps[:, f, :] if f < 3 else ps[:, 3, (f - 3) * SEQ:(f - 2) * SEQ]
                    ins = three(out, wh[:, ch.spl, w], wl[:, ch.spl, w], hTh[:, k, 0:n], hTl[:, k, 0:n], k == 0 and f != 4, k == KT - 1)
                ins.then_inc(s_used, 1)

            def v_turn(h):
                pe.wait_ge(s_hev, h * 4 - 1)
                pe.wait_ge(s_rso, h)
                for t in range(4):
                    ins = nc.tensor.transpose(pT[:, t * P:(t + 1) * P], IT[:, t * P:(t + 1) * P], ident)
                ins.then_inc(s_vT, 1)

            def k_turn(h, d):
                pe.wait_ge(s_kdr, h * 2 - 1 + d)
                if d == 0:
                    pe.wait_ge(s_v, h)
                else:
                    pe.wait_ge(s_sc, h * 2 - 1)
                for t in range(4):
                    ins = nc.tensor.transpose(pT[:, t * P:(t + 1) * P], R[:, d, t * P:(t + 1) * P], ident)
                ins.then_inc(s_kT, 1)

            def state_scores(h, d):
                pe.wait_ge(s_kd, h * 2 - 1 + d)
                pe.wait_ge(s_st, h * 2 - 1 + d)
                for j in range(7):
                    n = ORDER[d][j]
                    rows = slice(CHUNK * (n % 2), CHUNK * (n % 2 + 1))
                    ins = nc.tensor.matmul(ps[:, 5 + n % 2, (n // 2) * P:(n // 2 + 1) * P], KD[rows, n // 2, :], V1[rows, n // 2, :],
                                           start=True, stop=True, skip_group_check=True)
                ins.then_inc(s_ds, 1)
                for t in range(2):
                    tok = slice(t * P, (t + 1) * P)
                    ins = nc.tensor.matmul(pT[:, tok], KI[:, d, tok], QD[:, d, tok], start=True, stop=True, skip_group_check=True)
                ins.then_inc(s_scp, 1)

            def head_sum(h):
                pe.wait_ge(s_sc, h * 2)
                pe.wait_ge(s_st, h * 2 + 1)
                pe.wait_ge(s_y1, h)
                first = True
                for d in range(2):
                    for t in range(2):
                        tok = slice(t * P, (t + 1) * P)
                        nc.tensor.matmul(pO[:, tok], V1[:, t, :], SC[:, d, tok], start=first, stop=False, skip_group_check=True)
                        first = False
                for d in range(2):
                    for n in range(4):
                        tok = slice(n * CHUNK, (n + 1) * CHUNK)
                        ins = nc.tensor.matmul(pO[:, tok], ST[:, d, n * P:(n + 1) * P], QD[:, d, tok], start=False,
                                               stop=(d == 1 and n == 3), skip_group_check=True)
                ins.then_inc(s_o, 1)
                pe.wait_ge(s_osq, h)
                nc.tensor.matmul(pT[:, 0:SEQ], ones, OS, start=True, stop=True).then_inc(s_sq, 1)

            def head(h, proj, comp):
                for c in range(8):
                    if proj:
                        head_proj(h, c, comp)
                    if comp:
                        if c == 0:
                            v_turn(h)
                        if c == 2:
                            k_turn(h, 0)
                        if c == 3:
                            state_scores(h, 0)
                        if c == 4:
                            k_turn(h, 1)
                        if c == 6:
                            state_scores(h, 1)
                if comp:
                    head_sum(h)

            pe.wait_ge(s_plo, 2 * KT)
            head(0, True, False)
            with pe.Fori(1, HEADS) as h:
                head(h, True, True)
            head(HEADS, False, True)
            pe.wait_ge(s_yl, 2 * KT)
            with pe.Fori(0, 2) as i:
                for n in range(2):
                    pe.wait_ge(s_oe, i * 2 + (n + 5))
                    out_block([st.chunk("out1", i, 4 * n + c) for c in range(4)], 2, 2 * n)
            pe.wait_ge(s_posf, 1)
            nc.tensor.transpose(ps[:, 5, 0:2], posr, ident[0:2, 0:2]).then_inc(s_posT, 1)

            def hyb_layer(L):
                count = lambda total, n: L * total + n

                def free45(x):
                    n = USE45.index(x)
                    if n:
                        pe.wait_ge(s_45, count(len(USE45), n))

                def free67(x):
                    n = USE67.index(x)
                    if n:
                        pe.wait_ge(s_67, count(len(USE67), n))

                def project(i):
                    b = BLOCK_OF[i]
                    name = BLOCKS[b][0]
                    c = i - BLOCK_OF.index(b)
                    bank = 2 * (b % 2)
                    ch = st.chunk("hyb", L, i)
                    pe.wait_ge(s_lo, ch.number + 1)
                    if c == 0 and b >= 2:
                        pe.wait_ge(s_bm[b % 2], count(len(BLOCKS) // 2, b // 2))
                    if name == "uq_nope":
                        pe.wait_ge(s_qlo, count(8, 4))
                    if name == "ukv_k":
                        pe.wait_ge(s_qlo, count(8, 8))
                    if name in ("uq_nope", "ukv_k"):
                        r = 0 if name == "uq_nope" else 4
                        for k in range(4):
                            for f in range(4):
                                w = slice((4 * k + f) * P, (4 * k + f + 1) * P)
                                ins = three(ps[:, bank + f // 2, (f % 2) * SEQ:(f % 2 + 1) * SEQ], wh[:, ch.spl, w], wl[:, ch.spl, w],
                                            hTh[:, r + k, SEQ:TOK], hTl[:, r + k, SEQ:TOK], k == 0 and f % 2 == 0, k == 3)
                    elif name in ("uq_rope", "ukv_v"):
                        r, n = (0, 256) if name == "uq_rope" else (4, 512)
                        for k in range(4):
                            for m in range(2):
                                tok = slice(SEQ + m * P, SEQ + (m + 1) * P)
                                ins = three(ps[:, bank + m, 0:n], wh[:, ch.spl, k * n:(k + 1) * n], wl[:, ch.spl, k * n:(k + 1) * n],
                                            hTh[:, r + k, tok], hTl[:, r + k, tok], k == 0, k == 3, False)
                    else:
                        n = 320 if name == "kvr" else BLK
                        for t in range(4):
                            k = 4 * c + t
                            for m in range(2):
                                tok = slice(m * P, (m + 1) * P)
                                ins = three(ps[:, bank + m, 0:n], wh[:, ch.spl, t * n:(t + 1) * n], wl[:, ch.spl, t * n:(t + 1) * n],
                                            hTh[:, k, tok], hTl[:, k, tok], k == 0, k == KT - 1, False)
                    ins.then_inc(s_used, 1)

                def norm(name):
                    v = ("cq", "ckv").index(name)
                    free45("norm " + name)
                    pe.wait_ge(s_qd, count(2, v + 1))
                    src = (SR, VC)[v]
                    for k in range(4):
                        for t in range(2):
                            ins = nc.tensor.matmul(ps[:, 4 + k // 2, (k % 2) * SEQ + t * P:(k % 2) * SEQ + (t + 1) * P],
                                                   src[:, t, k * P:(k + 1) * P], DQ[:, 2 * v + t, :], start=(k % 2 == 0 and t == 0),
                                                   stop=True, skip_group_check=True)
                    ins.then_inc(s_qn, 1)

                def turn_block(name):
                    free67("turn " + name)
                    pe.wait_ge(s_rr, count(len(TURNS), TURNS.index(name) + 1))
                    src, n = (KS, 3) if name == "kvr" else (SR, 2 if name == "uq_rope" else 4)
                    for k in range(n):
                        for t in range(2):
                            ins = nc.tensor.transpose(ps[:, 6 + k // 2, (k % 2) * SEQ + t * P:(k % 2) * SEQ + (t + 1) * P],
                                                      src[:, t, k * P:(k + 1) * P], ident)
                    ins.then_inc(s_tn, 1)

                def turned(name):
                    pe.wait_ge(s_67, count(len(USE67), USE67.index("turn " + name) + 1))

                def moved(name):
                    b = BNUM[name]
                    pe.wait_ge(s_bm[b % 2], count(len(BLOCKS) // 2, b // 2 + 1))

                def score(n):
                    kind, h = PAIRS[n]
                    free45(f"score {n}")
                    if kind == "m":
                        turned("uq_rope")
                        moved("ukv_v")
                        moved("ukv_k")
                    elif kind == "b":
                        turned("bq0" if h < 4 else "bq1")
                    else:
                        turned("ak")
                    for m in range(2):
                        half = slice(64 * m, 64 * m + 64)
                        for o, q, k in ((slice(0, 2 * P), slice(P, 2 * P), slice(0, 2 * P)), (slice(2 * P, 3 * P), slice(0, P), slice(0, P))):
                            out = ps[:, 4 + m, o]
                            if kind == "m":
                                nc.tensor.matmul(out, QN[:, 2 * h + m, q], KN[:, 2 * h + m, k], start=True, stop=False, skip_group_check=True)
                                ins = nc.tensor.matmul(out, QR[half, h, q], KR[half, k], start=False, stop=True, skip_group_check=True)
                            elif kind == "b":
                                ins = nc.tensor.matmul(out, BQ[half, h, q], BK[half, h // 4, k], start=True, stop=True, skip_group_check=True)
                            else:
                                ins = nc.tensor.matmul(out, AQ[half, h, q], AK[half, h, k], start=True, stop=True, skip_group_check=True)
                    ins.then_inc(s_S, 1)

                def flip(n):
                    free67(f"flip {n}")
                    pe.wait_ge(s_p, count(NPAIR, n + 1))
                    for m in range(1 if PAIRS[n][0] == "a" else 2):
                        for k in range(3):
                            ins = nc.tensor.transpose(ps[:, 6 + m, k * P:(k + 1) * P], EX[:, m, k * P:(k + 1) * P], ident)
                    ins.then_inc(s_fl, 1)

                def weigh(n):
                    kind, h = PAIRS[n]
                    free45(f"weigh {n}")
                    pe.wait_ge(s_67, count(len(USE67), USE67.index(f"flip {n}") + 1))
                    if kind == "a":
                        moved("av")
                    for m in range(1 if kind == "a" else 2):
                        v, w = {"m": (VC, slice((2 * h + m) * P, (2 * h + m + 1) * P)), "b": (BV, slice((h // 4) * 64, (h // 4) * 64 + 64)),
                                "a": (AV, slice(h * P, (h + 1) * P))}[kind]
                        dv = w.stop - w.start
                        for k in range(2):
                            nc.tensor.matmul(ps[:, 4 + m, 0:dv], PT[:, m, k * P:(k + 1) * P], v[:, k, w], start=(k == 0), stop=(k == 1), skip_group_check=True)
                        ins = nc.tensor.matmul(ps[:, 4 + m, P:P + dv], PT[:, m, 2 * P:3 * P], v[:, 0, w], start=True, stop=True, skip_group_check=True)
                    ins.then_inc(s_W, 1)

                turn(L + 2, XN, 2)
                pe.wait_ge(s_plo, L * KT + 3 * KT)
                for i in range(NPROJ):
                    project(i)
                    for what in AFTER.get(i, []):
                        verb, arg = what.split()
                        if verb == "norm":
                            norm(arg)
                        elif verb == "turn":
                            turn_block(arg)
                        elif verb != "move":
                            {"score": score, "flip": flip, "weigh": weigh}[verb](int(arg))
                pe.wait_ge(s_45, count(len(USE45), len(USE45)))
                pe.wait_ge(s_67, count(len(USE67), len(USE67)))
                for g in range(YT):
                    if g == 6:
                        moved("cg")
                    if g >= 4:
                        pe.wait_ge(s_ytl, count(YT, g - 3))
                    for k in range(2):
                        for t in range(2):
                            ins = nc.tensor.transpose(ps[:, 4 + g % 4, k * SEQ + t * P:k * SEQ + (t + 1) * P],
                                                      Yt[:, t, (2 * g + k) * P:(2 * g + k + 1) * P], ident)
                    ins.then_inc(s_yt, 1)
                pe.wait_ge(s_ytl, count(YT, YT))
                for n in range(4):
                    if n == 0:
                        moved("ag")
                    if n >= 2:
                        pe.wait_ge(s_oe, L * 4 + (9 + n))
                    out_block([st.chunk("hyb", L, NPROJ + 4 * n + c) for c in range(4)], 2, 2 * (n % 2))

            with pe.Fori(0, 2) as L:
                hyb_layer(L)

        @block.vector
        def _(dve):
            step = Chain(dve, s_dve)

            def lo(ch, n=4 * BLK):
                dve.wait_ge(s_hi, ch.number + 1)
                nc.vector.tensor_tensor(wl[:, ch.spl, 0:n], raw[:, ch.raw, 0:n], wh[:, ch.spl, 0:n].bitcast(F32),
                                        ALU.subtract).then_inc(s_lo, 1)

            def pcol(name, i):
                return prm[:, PCOL[name] + i:PCOL[name] + i + 1]

            dve.sem_inc(s_lo, RAW)
            nc.vector.memset(s4[:, :].bitcast(F32), 0.0).then_inc(s_s4, 1)
            dve.sem_inc(s_arow, 1)
            dve.sem_inc(s_adaT, 1)
            dve.wait_ge(s_prT, 1)
            for t, rows in enumerate(PARAM_ROWS):
                n = sum(x for _, x in rows)
                ins = nc.vector.tensor_copy(prm[:, t * P:t * P + n], ps[:, 5, t * P:t * P + n])
            ins.then_inc(s_prm, 1)
            dve.wait_ge(s_prm, 1)
            dve.wait_ge(s_sil, 1)
            step(nc.vector.tensor_scalar(sile, sile, 1.0, None, ALU.add)).done()
            step(nc.vector.reciprocal(sile, sile)).done()
            nc.vector.tensor_tensor(silc, prm[:, 0:32], sile, ALU.mult).then_inc(s_sil, 1)
            dve.wait_ge(s_s4h, 1)
            sv = s4[:, 0:4 * KT].rearrange("p (k v) -> p k v", v=4)
            nc.vector.tensor_tensor(sv[:, :, 2:4], silc.rearrange("p (v k) -> p k v", v=2), sv[:, :, 0:2].bitcast(F32),
                                    ALU.subtract).then_inc(s_s4, 1)
            lg = prm[:, PCOL["lb_logits"]:PCOL["lb_logits"] + 96].rearrange("p (d l k) -> p d l k", d=2, l=3)
            step(nc.vector.tensor_tensor(lbm, lg[:, :, 0, :], lg[:, :, 1, :], ALU.max)).done()
            step(nc.vector.tensor_tensor(lbm, lbm, lg[:, :, 2, :], ALU.max)).done()
            for l in range(3):
                ins = nc.vector.tensor_tensor(lbt[:, :, l, :], lg[:, :, l, :], lbm, ALU.subtract)
            ins.then_inc(s_sil, 1)
            dve.wait_ge(s_sil, 4)
            step(nc.vector.tensor_tensor(lbm, lbt[:, :, 0, :], lbt[:, :, 1, :], ALU.add)).done()
            step(nc.vector.tensor_tensor(lbs, lbm, lbt[:, :, 2, :], ALU.add)).done()
            step(nc.vector.reciprocal(lbs, lbs)).done()
            lbv = lb.rearrange("p (d k) -> p d k", d=2)
            step(nc.vector.tensor_tensor(lbv, lbm, lbs, ALU.mult)).done()
            step(nc.vector.tensor_scalar(oml, lb, -1.0, 1.0, ALU.mult, ALU.add)).done()

            adab = prm[:, PCOL["ada_b"]:PCOL["ada_b"] + 96]

            def ada_move(b, last):
                dve.wait_ge(s_used, last.number + 1)
                nc.vector.tensor_copy(AROW[0:4, :], ps[0:4, 4, :]).then_inc(s_arow, 1)
                dve.wait_ge(s_adaP, b)
                at = bass.ds(b * 4 - 4, 4)
                nc.vector.tensor_tensor(adaT[:, at, :], psT, adab[:, at].unsqueeze(2).broadcast_to([P, 4, 2]),
                                        ALU.add).then_inc(s_adaT, 1)

            with dve.Fori(0, 8) as b:
                chs = [st.chunk("ada", b, c) for c in range(4)]
                for ch in chs:
                    lo(ch)
                ada_move(b + 1, chs[3])

            def modulation(l):
                step(nc.vector.tensor_scalar(modA, adaT[:, 48 * l + KT:48 * l + 2 * KT, :], 1.0, None, ALU.add)).done()
                g = prm[:, PCOL["pre_g"] + KT * l:PCOL["pre_g"] + KT * (l + 1)]
                step(nc.vector.tensor_tensor(modA, modA, g.unsqueeze(2).broadcast_to([P, KT, 2]), ALU.mult)).done()

            def diag(r, T):
                dve.wait_ge(s_rs, r)
                for t in range(T):
                    ins = nc.vector.tensor_scalar(dg[:, t, :], ident, rs[:, t:t + 1], None, ALU.mult)
                ins.then_inc(s_dg, 1)

            def low_h(r, hb, n, A, B):
                def low(k):
                    dve.wait_ge(s_phi, r * KT + (k + 1))
                    nc.vector.tensor_tensor(hTl[:, k, 0:n], hb[:, k % 4, 0:n], hTh[:, k, 0:n].bitcast(F32),
                                            ALU.subtract).then_inc(s_plo, 1)

                for k in range(KT):
                    dve.wait_ge(s_pt, r * KT + (k + 1))
                    if k >= 4:
                        dve.wait_ge(s_plo, r * KT + (k - 3))
                    for v in range(n // SEQ):
                        seg = slice(v * SEQ, (v + 1) * SEQ)
                        if B is None:
                            ins = nc.vector.tensor_scalar(hb[:, k % 4, seg], ps[:, k % 4, seg], A(k, v), None, ALU.mult)
                        else:
                            ins = nc.vector.tensor_scalar(hb[:, k % 4, seg], ps[:, k % 4, seg], A(k, v), B(k, v), ALU.mult, ALU.add)
                    ins.then_inc(s_ph, 1)
                    if k:
                        low(k - 1)
                low(KT - 1)

            dve.wait_ge(s_adaT, 9)
            modulation(0)
            diag(1, 4)
            low_h(0, HB, TOK, lambda k, v: modA[:, k, v:v + 1], lambda k, v: adaT[:, k, v:v + 1])
            dve.wait_ge(s_plo, KT)
            nc.vector.memset(area(S0, 2 * FLAT), 0.0).then_inc(s_pz, 1)

            def rows(buf, r, at=0):
                return buf[:, :, r * LATROW + PAD + at:r * LATROW + PAD + at + GRID_W]

            def pool_out(g):
                dve.wait_ge(s_mix, g + 1)
                for o in range(2):
                    ins = nc.vector.scalar_tensor_tensor(out=Y0[:, 2 * g + o, :], in0=ps[:, 6 + o, :],
                                                         scalar=pcol("ev_pool_scale", 2 * g + o), in1=G2[:, o, :],
                                                         op0=ALU.mult, op1=ALU.mult)
                ins.then_inc(s_py, 1)

            for g, w in enumerate(POOL_WINDOWS):
                for c in range(4):
                    lo(st.chunk("pool", g, c))
                    if g and c == 2:
                        pool_out(g - 1)
                rest = [st.chunk("pool", g, 4 + c) for c in range(8)]
                lo(rest[0])
                dve.wait_ge(s_pg, g + 1)
                step(nc.vector.tensor_scalar(GE, GE, 1.0, None, ALU.add)).done()
                step(nc.vector.reciprocal(GE, GE)).done()
                step(nc.vector.tensor_tensor(G2, G2, GE, ALU.mult)).done()
                lo(rest[1])
                step(nc.vector.memset(area(S0 + 2 * FLAT, 2 * FLAT), 0.0)).done()
                step(nc.vector.tensor_copy(SA[:, :, 4 * LATROW:FLAT], V[:, :, 4 * LATROW:FLAT]))
                if w == 2:
                    step(nc.vector.tensor_copy(rows(SA, 0), rows(V, 0)))
                    for r in range(1, 4):
                        step(nc.vector.tensor_tensor(rows(SA, r), rows(V, r), rows(V, r - 1), ALU.add))
                else:
                    step(nc.vector.tensor_tensor(rows(SA, 0), rows(V, 0), rows(V, 1), ALU.add))
                    step(nc.vector.tensor_tensor(rows(SB_, 0), rows(V, 2), rows(V, 3), ALU.add)).done()
                    if w == 4:
                        step(nc.vector.tensor_tensor(rows(SA, 1), rows(SA, 0), rows(V, 2), ALU.add))
                        step(nc.vector.tensor_tensor(rows(SA, 2), rows(SA, 0), rows(SB_, 0), ALU.add))
                        step(nc.vector.tensor_tensor(rows(SA, 3), rows(SB_, 0), rows(V, 1), ALU.add))
                    else:
                        for r in (1, 2, 3):
                            step(nc.vector.tensor_tensor(rows(SA, r), rows(SA, 0), rows(SB_, 0), ALU.add))
                        step(nc.vector.tensor_tensor(rows(SA, 0), rows(SA, 0), rows(SB_, 0), ALU.add))
                step.done()
                taken = 2
                lo(rest[2])
                src, dst, span, n = S0 + 2 * FLAT, S0 + 4 * FLAT, 1, 2 * FLAT
                while span < w:
                    n -= span
                    step(nc.vector.tensor_tensor(area(dst, n), area(src, n), area(src + span, n), ALU.add)).done()
                    src, dst, span = dst, src, 2 * span
                    if taken < 3:
                        taken = 3
                        lo(rest[3])
                        ada_move(9 + 2 * g, rest[3])
                W = area(src, 2, FLAT)
                dve.wait_ge(s_inv, 32 * (g + 1))
                PL = PO[:, :, 0:SEQ].rearrange("p a (r c) -> p a r c", r=4)
                lat = W[:, :, 0:4 * LATROW].rearrange("p a (r c) -> p a r c", r=4)[:, :, :, PAD - w // 2:PAD - w // 2 + GRID_W]
                latv = V[:, :, 0:4 * LATROW].rearrange("p a (r c) -> p a r c", r=4)[:, :, :, PAD:PAD + GRID_W]
                c0 = 4 * LATROW + PAD
                for t in range(2):
                    step(nc.vector.tensor_tensor(PL[:, t], lat[:, t], INV[:, 0:SEQ].rearrange("p (r c) -> p r c", r=4), ALU.mult))
                    step(nc.vector.tensor_tensor(PO[:, t, SEQ:TOK], W[:, t, c0 - w // 2:c0 - w // 2 + SEQ], INV[:, SEQ:TOK], ALU.mult))
                step.done()
                lo(rest[4])
                for t in range(2):
                    step(nc.vector.tensor_tensor(PL[:, t], PL[:, t], latv[:, t], ALU.subtract))
                    ins = nc.vector.tensor_tensor(PO[:, t, SEQ:TOK], PO[:, t, SEQ:TOK], V[:, t, c0:c0 + SEQ], ALU.subtract)
                ins.then_inc(s_po, 1)
                for c in range(5, 8):
                    lo(rest[c])
                ada_move(10 + 2 * g, rest[7])

            def conv_mix(j):
                dve.wait_ge(s_ce, j + 1)
                w0, w1, w2 = (prm[:, bass.ds(PCOL["ev_conv_w"] + 8 * i + j, 1)] for i in range(3))
                bias = prm[:, bass.ds(PCOL["ev_conv_b"] + j, 1)]
                v3 = lambda x: x.rearrange("p (a b) -> p a b", a=2)
                step(nc.vector.tensor_tensor(U[:, :, 1:SEQ + 1], v3(CC), v3(CX), ALU.mult))
                step(nc.vector.tensor_scalar(CE, CE, 1.0, None, ALU.add)).done()
                step(nc.vector.tensor_scalar(CT, U[:, :, 0:SEQ], w0, bias, ALU.mult, ALU.add))
                step(nc.vector.reciprocal(CE, CE)).done()
                step(nc.vector.scalar_tensor_tensor(out=CT, in0=U[:, :, 1:SEQ + 1], scalar=w1, in1=CT, op0=ALU.mult, op1=ALU.add))
                step(nc.vector.tensor_tensor(CG, CG, CE, ALU.mult)).done()
                step(nc.vector.scalar_tensor_tensor(out=CT, in0=U[:, :, 2:SEQ + 2], scalar=w2, in1=CT, op0=ALU.mult, op1=ALU.add)).done()
                step(nc.vector.tensor_tensor(CT, CT, v3(CB), ALU.mult)).done()
                nc.vector.tensor_tensor(Y0[:, bass.ds(8 + j, 1), :].rearrange("p a b -> p (a b)"), CT.rearrange("p a b -> p (a b)"), CG,
                                        ALU.mult).then_inc(s_cv, 1)

            def conv_ada(j):
                for c in range(4, 8):
                    lo(st.chunk("conv", j, c))
                ada_move(j + 17, st.chunk("conv", j, 7))

            dve.wait_ge(s_po, 4)
            nc.vector.memset(U, 0.0).then_inc(s_cv, 1)
            for c in range(3):
                lo(st.chunk("conv", 0, c))
            pool_out(3)
            lo(st.chunk("conv", 0, 3))
            conv_ada(0)
            with dve.Fori(1, 8) as j, step.loop(j, 1, 7, 8):
                lo(st.chunk("conv", j, 0))
                lo(st.chunk("conv", j, 1))
                conv_mix(j - 1)
                lo(st.chunk("conv", j, 2))
                lo(st.chunk("conv", j, 3))
                conv_ada(j)
            conv_mix(7)

            def split_y(Yk, n, base):
                for k in range(KT):
                    dve.wait_ge(s_yh, base + k + 1)
                    nc.vector.tensor_tensor(hTl[:, k, 0:n], Yk(k), hTh[:, k, 0:n].bitcast(F32), ALU.subtract).then_inc(s_yl, 1)

            split_y(lambda k: Y0[:, k, :], TOK, 0)

            def gate_diag(l, V_, first):
                g = prm[:, PCOL["post_g"] + KT * l:PCOL["post_g"] + KT * (l + 1)]
                step(nc.vector.tensor_tensor(gp, adaT[:, 48 * l + 2 * KT:48 * l + 3 * KT, :], g.unsqueeze(2).broadcast_to([P, KT, 2]),
                                             ALU.mult)).done()
                for v in range(V_):
                    for q in range(4):
                        r = first + 4 * v + q
                        if r:
                            dve.wait_ge(s_gb, r)
                        nc.vector.tensor_tensor(dg[:, :, :], ident.unsqueeze(1).broadcast_to([P, 4, P]),
                                                gp[:, 4 * q:4 * q + 4, v].unsqueeze(2).broadcast_to([P, 4, P]), ALU.mult).then_inc(s_gd, 1)

            dve.wait_ge(s_adaT, 25)
            gate_diag(0, 2, 0)

            dve.sem_inc(s_oe, 2)
            with dve.Fori(0, 2) as i:
                for c in range(8):
                    lo(st.chunk("out0", i, c))

            def residual_add(T, r, base, X, G, XR):
                dve.wait_ge(s_rs, r)
                for u in range(2 * T):
                    t, f = u // 2, slice((u % 2) * (D // 2), (u % 2 + 1) * (D // 2))
                    step(nc.vector.scalar_tensor_tensor(out=X[:, t, f], in0=X[:, t, f], scalar=rs[:, t:t + 1],
                                                        in1=G[:, t // 2, f], op0=ALU.mult, op1=ALU.mult)).done()
                    dve.wait_ge(s_xr[u % 2], base * 8 + 16 * (u // 2 + 1))
                    nc.vector.tensor_tensor(X[:, t, f], X[:, t, f], XR[:, u % 2, :], ALU.add).then_inc(s_xa, 1)

            dve.wait_ge(s_gbe, 8)
            residual_add(4, 2, 0, X4, GB0, XR0)
            gate_diag(1, 1, 8)
            modulation(1)
            dve.wait_ge(s_gb, 12)
            diag(3, 4)
            low_h(1, HB, TOK, lambda k, v: modA[:, k, v:v + 1], lambda k, v: adaT[:, 48 + k, v:v + 1])
            dve.wait_ge(s_save, 32)
            dve.wait_ge(s_plo, 2 * KT)
            dve.sem_inc(s_st, 1)
            dve.sem_inc(s_y1, 1)
            nc.vector.memset(SC, 0.0).then_inc(s_l1, 1)
            dve.wait_ge(s_l1, 1)
            chunked = lambda x: x.rearrange("p (n c) -> p n c", c=CHUNK)

            def head(h, proj, comp):
                def split(c):
                    if proj:
                        lo(st.chunk("hg", h, c), 10 * P)

                def bound(x, d):
                    return x[:, bass.ds(h + (d * KT - 1), 1)]

                def gates(d):
                    dve.wait_ge(s_hev, h * 4 - 3 + d)
                    step(nc.vector.tensor_scalar(R[:, d, :], Z[:, d, :], 1e30, 1.0, ALU.min, ALU.add)).done()
                    step(nc.vector.tensor_scalar(Z[:, d, :], Z[:, d, :], 1e30, bound(oml, d), ALU.min, ALU.mult))
                    step(nc.vector.reciprocal(R[:, d, :], R[:, d, :])).done()
                    step(nc.vector.tensor_tensor(Z[:, d, :], Z[:, d, :], R[:, d, :], ALU.mult)).done()
                    nc.vector.tensor_scalar(R[:, d, :], R[:, d, :], bound(oml, d), bound(lb, d), ALU.mult, ALU.add).then_inc(s_f, 1)

                def decay_sums(d):
                    dve.wait_ge(s_ln, h * 2 - 1 + d)
                    o, i = (B[:, 0, :], R[:, 0, :]) if d == 0 else (B[:, 1, ::-1], R[:, 1, ::-1])
                    step(nc.vector.tensor_tensor_scan(o, C("reset"), i, 0.0, ALU.mult, ALU.add)).done()
                    edge = CHUNK - 1 if d == 0 else 0
                    nc.vector.tensor_tensor(chunked(R[:, d, :]), chunked(B[:, d, :])[:, :, edge:edge + 1].broadcast_to([P, NCH, CHUNK]),
                                            chunked(B[:, d, :]), ALU.subtract).then_inc(s_b, 1)

                def keys(d):
                    dve.wait_ge(s_ex, h * 2 - 1 + d)
                    nc.vector.tensor_tensor(R[:, d, :], R[:, d, :], Z[:, d, :], ALU.mult)
                    nc.vector.tensor_tensor(QD[:, d, :], QD[:, d, :], Q, ALU.mult)
                    nc.vector.tensor_tensor(KI[:, d, :], KI[:, d, :], Z[:, d, 0:SEQ], ALU.mult).then_inc(s_kdr, 1)

                def k_move(d):
                    dve.wait_ge(s_kT, h * 2 - 1 + d)
                    nc.vector.tensor_copy(KD, pT.rearrange("p (a b) -> p a b", a=4)).then_inc(s_kd, 1)

                def states(d):
                    dve.wait_ge(s_ds, h * 2 - 1 + d)
                    at = lambda n: ps[:, 5 + n % 2, (n // 2) * P:(n // 2 + 1) * P]
                    step(nc.vector.tensor_copy(SX[:, 0, :], at(ORDER[d][0]))).done()
                    src = SX[:, 0, :]
                    for j in range(1, 7):
                        n = ORDER[d][j]
                        if j == 6:
                            dve.wait_ge(s_scp, h * 2 - 1 + d)
                        dst = SX[:, j % 2, :] if j < 3 else ST[:, d, ORDER[d][j + 1] * P:(ORDER[d][j + 1] + 1) * P]
                        ins = nc.vector.scalar_tensor_tensor(out=dst, in0=src, scalar=DEC[:, d, n:n + 1], in1=at(n),
                                                             op0=ALU.mult, op1=ALU.add)
                        if j < 6:
                            step(ins).done()
                        src = dst
                    ins.then_inc(s_st, 1)
                    nc.vector.copy_predicated(SC[:, d, :].rearrange("p (a b) -> p a b", a=2),
                                              C(("mask_f", "mask_b")[d]).bitcast(I32).unsqueeze(1).broadcast_to([P, 2, P]),
                                              pT[:, 0:SEQ].rearrange("p (a b) -> p a b", a=2)).then_inc(s_sc, 1)

                split(0)
                if comp:
                    gates(0)
                split(1)
                if comp:
                    decay_sums(0)
                    gates(1)
                split(2)
                if comp:
                    keys(0)
                    decay_sums(1)
                split(3)
                if comp:
                    k_move(0)
                    keys(1)
                split(4)
                if comp:
                    states(0)
                split(5)
                if comp:
                    k_move(1)
                    dve.wait_ge(s_hev, h * 4)
                    step(nc.vector.tensor_scalar(GH, GH, 1.0, None, ALU.add)).done()
                    step(nc.vector.reciprocal(GH, GH)).done()
                    nc.vector.scalar_tensor_tensor(out=SG, in0=SG, scalar=prm[:, bass.ds(h + (PCOL["od_onorm_g"] - 1), 1)], in1=GH,
                                                   op0=ALU.mult, op1=ALU.mult).then_inc(s_sgr, 1)
                split(6)
                split(7)
                if comp:
                    states(1)
                    dve.wait_ge(s_rso, h + 1)
                    step(nc.vector.tensor_tensor(OS, pO, RH, ALU.mult)).done()
                    nc.vector.tensor_tensor(Y1[:, bass.ds(h - 1, 1), :].rearrange("p a b -> p (a b)"), OS, SG, ALU.mult).then_inc(s_y1, 1)

            head(0, True, False)
            with dve.Fori(1, HEADS) as h, step.loop(h, 1, HEADS - 1, 25):
                head(h, True, True)
            head(HEADS, False, True)
            split_y(lambda k: Y1[:, k, :], SEQ, KT)
            with dve.Fori(0, 2) as i:
                for c in range(8):
                    lo(st.chunk("out1", i, c))
            residual_add(2, 4, 8, X1, GB1, XR1)
            dve.wait_ge(s_pos, 16)
            nc.vector.tensor_copy(posr, posi).then_inc(s_posf, 1)
            dve.wait_ge(s_posT, 1)
            step(nc.vector.tensor_copy(posf, ps[:, 5, 0:2])).done()
            for t in range(2):
                step(nc.vector.tensor_scalar(ang[:, 32 * t:32 * t + 32], C("invf"), posf[:, t:t + 1], None, ALU.mult))
            step.done()
            step(nc.vector.tensor_scalar(turns_, ang, 1.0 / TWO_PI, ROUND, ALU.mult, ALU.add)).done()
            step(nc.vector.tensor_scalar(turns_, turns_, -ROUND, None, ALU.add)).done()
            for part in (PI_HI, PI_MID, PI_LO):
                step(nc.vector.scalar_tensor_tensor(out=ang, in0=turns_, scalar=-part, in1=ang, op0=ALU.mult, op1=ALU.add)).done()
            step(nc.vector.tensor_scalar(ang, ang, 3.1415925, -3.1415925, ALU.min, ALU.max)).done()
            step(nc.vector.tensor_copy(small[:, 72:136], ang))
            step(nc.vector.scalar_tensor_tensor(out=turns_, in0=ang, scalar=-1.0, in1=ang, op0=ALU.mult, op1=ALU.max)).done()
            nc.vector.tensor_scalar(small[:, 8:72], turns_, -1.0, 1.5707963267948966, ALU.mult, ALU.add).then_inc(s_ang, 1)
            dve.wait_ge(s_sin, 1)

            def hyb_layer(L):
                count = lambda total, n: L * total + n
                banks = lambda b: ps[:, 2 * (b % 2):2 * (b % 2) + 2, :]

                dve.wait_ge(s_lp, L * 96 + 96)
                lq = LQ.rearrange("p (i j) d -> p i j d", j=2)
                step(nc.vector.tensor_tensor(lq[:, :, 0, :], lq[:, :, 0, :], lq[:, :, 1, :], ALU.mult)).done()
                nc.vector.tensor_reduce(lamt[:, 0:2], lq[:, :, 0, :], AX.X, ALU.add).then_inc(s_lam, 1)
                step(nc.vector.tensor_scalar(SUB, SUB, C("eps")[:, bass.ds(L + 4, 1)], None, ALU.mult))
                step(nc.vector.tensor_scalar(NSK, SNK, -1.0, None, ALU.mult))
                dve.wait_ge(s_lamx, count(1, 1))
                step(nc.vector.tensor_tensor(lamt[:, 2:3], lamt[:, 0:1], lamt[:, 1:2], ALU.subtract)).done()
                step(nc.vector.tensor_scalar(lamt[:, 3:4], lamt[:, 2:3], C("eps")[:, bass.ds(L + 2, 1)], None, ALU.add)).done()
                step(nc.vector.tensor_scalar(NL, lamt[:, 3:4], -1.0, None, ALU.mult)).done()

                diag(L * 2 + 5, 2)
                low_h(L + 2, HBN, SEQ, lambda k, v: prm[:, bass.ds(L * KT + (PCOL["pre_norm_w_2"] + k), 1)], None)
                dve.wait_ge(s_plo, L * KT + 3 * KT)

                def rope(src, dst, heads):
                    c, s = (x.unsqueeze(2).broadcast_to([P, 2, heads, 32]) for x in (cosv, sinv))
                    tm = TM[:, :, 0:32 * heads].rearrange("p t (h d) -> p t h d", d=32)
                    x1, x2, o1, o2 = src[:, :, :, 0:32], src[:, :, :, 32:64], dst[:, :, :, 0:32], dst[:, :, :, 32:64]
                    step(nc.vector.tensor_tensor(o1, x1, c, ALU.mult))
                    step(nc.vector.tensor_tensor(tm, x2, s, ALU.mult)).done()
                    step(nc.vector.tensor_tensor(o1, o1, tm, ALU.subtract)).done()
                    step(nc.vector.tensor_tensor(o2, x2, c, ALU.mult))
                    step(nc.vector.tensor_tensor(tm, x1, s, ALU.mult)).done()
                    return nc.vector.tensor_tensor(o2, o2, tm, ALU.add)

                def move(name, i):
                    b = BNUM[name]
                    dve.wait_ge(s_used, st.chunk("hyb", L, i).number + 1)
                    if name in ("cq", "ckv"):
                        v = ("cq", "ckv").index(name)
                        dve.wait_ge(s_qs, count(2, v + 1))
                        for t in range(2):
                            ins = nc.vector.tensor_scalar(DQ[:, 2 * v + t, :], ident, qrs[:, 2 * v + t:2 * v + t + 1], None, ALU.mult)
                        ins.then_inc(s_qd, 1)
                    elif name == "kvr":
                        dve.wait_ge(s_qn, count(2, 2))
                        kv = banks(b)[:, :, 0:320].rearrange("p t (h d) -> p t h d", d=64)
                        ks = KS.rearrange("p t (h r d) -> p t h r d", h=3, r=2)
                        step(rope(kv[:, :, 0:2], ks[:, :, 0:2, 0], 2)).done()
                        step(rope(kv[:, :, 4:5], ks[:, :, 2:3, 0], 1)).done()
                        nc.vector.tensor_copy(BV, banks(b)[:, :, P:2 * P]).then_inc(s_bm[b % 2], 1)
                        for t in range(2):
                            ins = nc.vector.tensor_copy(ks[:, t, :, 1], ks[:, t, :, 0])
                        ins.then_inc(s_rr, 1)
                    elif name in ("bq0", "bq1", "aq", "ak", "uq_rope"):
                        heads = 4 if name == "uq_rope" else 8
                        at = TURNS.index(name)
                        dve.wait_ge(s_tn, count(len(TURNS), at))
                        if name == "aq":
                            dve.wait_ge(s_bm[BNUM["bg1"] % 2], count(len(BLOCKS) // 2, BNUM["bg1"] // 2 + 1))
                        v = lambda x: x[:, :, 0:64 * heads].rearrange("p t (h d) -> p t h d", d=64)
                        ins = rope(v(banks(b)), v(SR), heads)
                        step(ins).done()
                        dve.sem_inc(s_bm[b % 2], 1)
                        dve.sem_inc(s_rr, 1)
                    elif name[1] == "g":
                        g = ("bg0", "bg1", "ag", "cg").index(name)
                        dve.wait_ge(s_gx, count(4, g + 1))
                        col = {"bg0": 512, "bg1": 1024, "ag": 0, "cg": 1536}[name]
                        y = Yt[:, :, col:col + BLK]
                        step(nc.vector.tensor_scalar(SR, SR, 1.0, None, ALU.add)).done()
                        step(nc.vector.reciprocal(SR, SR)).done()
                        if name[0] == "b":
                            nc.vector.tensor_tensor(y, banks(b), SR, ALU.mult).then_inc(s_bm[b % 2], 1)
                        else:
                            dve.wait_ge(s_45, count(len(USE45), USE45.index("weigh 11" if name == "ag" else "weigh 1") + 1))
                            n = 2 * P if name == "ag" else BLK
                            step(nc.vector.tensor_tensor(SR, banks(b), SR, ALU.mult)).done()
                            if n < BLK:
                                step(nc.vector.tensor_copy(y[:, :, n:], SR[:, :, n:]))
                            nc.vector.tensor_tensor(y[:, :, 0:n], y[:, :, 0:n], SR[:, :, 0:n], ALU.mult).then_inc(s_bm[b % 2], 1)

                def norm(name):
                    v = ("cq", "ckv").index(name)
                    w = PCOL["mla_q_norm_w_2"] if v == 0 else PCOL["mla_kv_norm_w_2"]
                    dve.wait_ge(s_qn, count(2, v + 1))
                    if v:
                        dve.wait_ge(s_qlo, count(8, 4))
                    for k in range(4):
                        ins = nc.vector.tensor_scalar(HQ[:, k, :], ps[:, 4 + k // 2, (k % 2) * SEQ:(k % 2 + 1) * SEQ],
                                                      prm[:, bass.ds(L * 4 + (w + k), 1)], None, ALU.mult)
                        ins.then_inc(s_qh, 1)
                    dve.wait_ge(s_qh, count(8, 4 * v + 4))
                    dve.sem_inc(s_45, 1)
                    for k in range(4):
                        dve.wait_ge(s_qhi, count(8, 4 * v + k + 1))
                        nc.vector.tensor_tensor(hTl[:, 4 * v + k, SEQ:TOK], HQ[:, k, :], hTh[:, 4 * v + k, SEQ:TOK].bitcast(F32),
                                                ALU.subtract).then_inc(s_qlo, 1)

                def score(n):
                    kind, h = PAIRS[n]
                    scale = 192 ** -0.5 if kind == "m" else 64 ** -0.5
                    dve.wait_ge(s_S, count(NPAIR, n + 1))
                    if n:
                        dve.wait_ge(s_fl, count(NPAIR, n))
                    mask = C("band") if kind == "b" else C("causal")
                    step(nc.vector.scalar_tensor_tensor(out=EX[:, :, 0:2 * P], in0=ps[:, 4:6, 0:2 * P], scalar=scale,
                                                        in1=mask.unsqueeze(1).broadcast_to([P, 2, 2 * P]), op0=ALU.mult, op1=ALU.add))
                    nc.vector.scalar_tensor_tensor(out=EX[:, :, 2 * P:3 * P], in0=ps[:, 4:6, 2 * P:3 * P], scalar=scale,
                                                   in1=C("causal")[:, P:2 * P].unsqueeze(1).broadcast_to([P, 2, P]),
                                                   op0=ALU.mult, op1=ALU.add).then_inc(s_45, 1)
                    dve.wait_ge(s_45, count(len(USE45), USE45.index(f"score {n}") + 1))
                    step(nc.vector.tensor_reduce(NM[:, 0:2], EX[:, :, 0:2 * P], AX.X, ALU.max, negate=True))
                    ins = nc.vector.tensor_reduce(NM[:, 2:4], EX[:, :, 2 * P:3 * P], AX.X, ALU.max, negate=True)
                    if kind == "b":
                        step(ins).done()
                        v = lambda x: x.rearrange("p (q m) -> p q m", q=2)
                        two = lambda x: x[:, 2 * h:2 * h + 2].unsqueeze(1).broadcast_to([P, 2, 2])
                        step(nc.vector.tensor_tensor(v(NM), v(NM), two(NSK), ALU.min)).done()
                        ins = nc.vector.tensor_tensor(v(ES), v(NM), two(SNK), ALU.add)
                    ins.then_inc(s_nm, 1)

                def flip(n):
                    kind, h = PAIRS[n]
                    dve.wait_ge(s_e, count(NPAIR, n + 1))
                    if kind == "b":
                        step(nc.vector.tensor_tensor(LS, LS, ES, ALU.add)).done()
                    ins = nc.vector.reciprocal(RL, LS)
                    if kind == "a":
                        step(ins).done()
                        step(nc.vector.tensor_scalar(LN, RL.rearrange("p (q m) -> p q m", q=2)[:, :, 1], NL, None, ALU.mult)).done()
                        for q, seg in ((0, slice(0, 2 * P)), (1, slice(2 * P, 3 * P))):
                            step(nc.vector.tensor_scalar(EX[:, 1, seg], EX[:, 1, seg], LN[:, q:q + 1], None, ALU.mult))
                        step.done()
                        for q, seg in ((0, slice(0, 2 * P)), (1, slice(2 * P, 3 * P))):
                            ins = nc.vector.scalar_tensor_tensor(out=EX[:, 0, seg], in0=EX[:, 0, seg], scalar=RL[:, 2 * q:2 * q + 1],
                                                                 in1=EX[:, 1, seg], op0=ALU.mult, op1=ALU.add)
                    ins.then_inc(s_p, 1)

                def moved(name):
                    b = BNUM[name]
                    dve.wait_ge(s_bm[b % 2], count(len(BLOCKS) // 2, b // 2 + 1))

                def weigh(n):
                    kind, h = PAIRS[n]
                    if kind == "b":
                        moved("bg0" if h < 4 else "bg1")
                    if kind == "a" and h >= 2:
                        moved("ag")
                    dve.wait_ge(s_W, count(NPAIR, n + 1))
                    if kind == "a":
                        dve.wait_ge(s_os, count(4, h + 1))
                        for q in range(2):
                            y = Yt[:, 1 - q, h * P:(h + 1) * P]
                            dst = y if h < 2 else OJ[:, q, :]
                            ins = nc.vector.scalar_tensor_tensor(out=dst, in0=ps[:, 4, q * P:(q + 1) * P], scalar=ors[:, q:q + 1], in1=SUB,
                                                                 op0=ALU.mult, op1=ALU.mult)
                            if h >= 2:
                                step(ins).done()
                                ins = nc.vector.tensor_tensor(y, OJ[:, q, :], y, ALU.mult)
                        ins.then_inc(s_45, 1)
                        return
                    for m in range(2):
                        for q in range(2):
                            r = RL[:, 2 * q + m:2 * q + m + 1]
                            if kind == "m":
                                y = Yt[:, 1 - q, 1536 + (2 * h + m) * P:1536 + (2 * h + m + 1) * P]
                                ins = nc.vector.tensor_scalar(y, ps[:, 4 + m, q * P:(q + 1) * P], r, None, ALU.mult)
                            else:
                                y = Yt[:, 1 - q, 512 + (2 * h + m) * 64:512 + (2 * h + m + 1) * 64]
                                ins = nc.vector.scalar_tensor_tensor(out=y, in0=ps[:, 4 + m, q * P:q * P + 64], scalar=r, in1=y,
                                                                     op0=ALU.mult, op1=ALU.mult)
                    ins.then_inc(s_45, 1)

                def after(i):
                    for what in AFTER.get(i, []):
                        verb, arg = what.split()
                        if verb == "move":
                            move(arg, i)
                        elif verb == "norm":
                            norm(arg)
                        elif verb != "turn":
                            {"score": score, "flip": flip, "weigh": weigh}[verb](int(arg))

                def split(i):
                    lo(st.chunk("hyb", L, i), {"kvr": 4 * 320, "uq_rope": 4 * 256}.get(BLOCKS[BLOCK_OF[i]][0], 4 * BLK))

                split(0)
                for i in range(NPROJ):
                    if i + 1 < NPROJ:
                        split(i + 1)
                    after(i)
                for g in range(YT):
                    dve.wait_ge(s_yth, count(YT, g + 1))
                    nc.vector.tensor_tensor(hTl[:, 2 * g:2 * g + 2, 0:SEQ], ps[:, 4 + g % 4, :].rearrange("p (a b) -> p a b", a=2),
                                            hTh[:, 2 * g:2 * g + 2, 0:SEQ].bitcast(F32), ALU.subtract).then_inc(s_ytl, 1)
                for i in range(16):
                    lo(st.chunk("hyb", L, NPROJ + i))
                dve.wait_ge(s_gl, L * 16 + 16)
                residual_add(2, L * 2 + 6, L * 4 + 12, XN, GBN, XRN)

            with dve.Fori(0, 2) as L, step.loop(L, 0, 2, DVE_STEPS):
                hyb_layer(L)


_SHAPES = ["consts", "inv"]
_INS = ["x", "c", "ctx", "c_ctx", "ada_w", "ada_b", "pre_g", "post_g", "ev_w_in", "ev_pool_w", "ev_pool_scale",
        "ev_conv_w", "ev_conv_b", "ev_w_out", "od_w_in", "od_onorm_g", "od_w_out", "lb_logits", "positions_2",
        "pre_norm_w_2", "post_norm_w_2", "w_in_2", "diff_lambda_q1_2", "diff_lambda_k1_2", "diff_lambda_q2_2",
        "diff_lambda_k2_2", "diff_subln_w_2", "sink_logits_2", "mla_q_norm_w_2", "mla_kv_norm_w_2", "w_uq_2",
        "w_ukv_2", "w_out_2"]


def kernel(**inputs):
    import numpy as _np
    import concourse.bacc as _bacc
    from concourse import mybir as _mybir
    from concourse.bass_utils import run_bass_kernel_spmd as _run

    nc = _bacc.Bacc("TRN2", target_bir_lowering=False, num_devices=1)
    arrays, a = {}, {}
    consts, inv = shape_constants()
    given = {name: _np.ascontiguousarray(inputs[name]) for name in _INS}
    given["consts"], given["inv"] = consts, _np.ascontiguousarray(_np.broadcast_to(inv[:, None, :], (4, P, TOK)))
    for name, v in given.items():
        arrays[f"in_{name}_dram"] = v
        a[name] = nc.dram_tensor(f"in_{name}_dram", v.shape, _mybir.dt.from_np(v.dtype), kind="ExternalInput").ap()
    a["out"] = nc.dram_tensor("out_0_dram", (1, SEQ, D), F32, kind="ExternalOutput").ap()
    first_block_and_hybrid(nc, a)
    r = _run(nc, [arrays], core_ids=[0])
    return r.results[0]["out_0_dram"]
```

```python
import concourse.bass as bass
from concourse import mybir
from contextlib import ExitStack, contextmanager
import math

import numpy as np

F32 = mybir.dt.float32
F32R = mybir.dt.float32r
I32 = mybir.dt.int32
ACT = mybir.ActivationFunctionType
ALU = mybir.AluOpType
AX = mybir.AxisListType

P = 128
D = 2048
KT = D // P
SEQ = 256
TOK = 2 * SEQ
EPS = 1e-6
CHUNK = 64
NCH = TOK // CHUNK
POOL_WINDOWS = (2, 4, 8, 16)
POOL_W = D // 2
GRID_W = 64
PAD = max(POOL_WINDOWS) // 2
LATROW = GRID_W + 2 * PAD
CTXROW = SEQ + 2 * PAD
FLAT = (SEQ // GRID_W) * LATROW + CTXROW
POOL_AT = (0, 3, 6, 10)
POOL_ADA = (1, 2, 4, 5, 7, 8, 9, 11)
HEADS = 16
OUT1 = [(0, 0), (0, 1), (0, 2), (1, 0), (1, 1), (1, 2), (0, 3), (1, 3)] + [(n, c) for n in (2, 3) for c in range(4)]
BLK = 512
RAW = 4
SPL = 2

PARAM_ROWS = [
    [("c", 16), ("c_ctx", 16), ("ada_b", 96)],
    [("pre_g", 32), ("post_g", 32), ("ev_pool_scale", 8), ("ev_conv_w", 24), ("ev_conv_b", 8), ("od_onorm_g", 16)],
    [("lb_logits", 96), ("pre_norm_w_2", 32)],
    [("mla_q_norm_w_2", 8), ("mla_kv_norm_w_2", 8)],
]
PCOL = {}
for _t, _rows in enumerate(PARAM_ROWS):
    _at = 0
    for _name, _n in _rows:
        PCOL[_name] = _t * P + _at
        _at += _n

CONSTS = [("ident", P), ("ones", P), ("mask_f", P), ("mask_b", P), ("causal", 2 * P), ("band", 2 * P),
          ("reset", TOK), ("invf", 32), ("comb", 4), ("eps", 6)]
CCOL = {}
_at = 0
for _name, _n in CONSTS:
    CCOL[_name] = _at
    _at += _n
NCONST = _at


def shape_constants():
    c = np.zeros((P, NCONST), np.float32)

    def put(name, a):
        c[:, CCOL[name]:CCOL[name] + a.shape[1]] = a

    i = np.arange(P)
    put("ident", np.eye(P, dtype=np.float32))
    put("ones", np.ones((P, P), np.float32))
    same = (i[:, None] // CHUNK) == (i[None, :] // CHUNK)
    put("mask_f", (same & (i[:, None] <= i[None, :])).astype(np.float32))
    put("mask_b", (same & (i[:, None] >= i[None, :])).astype(np.float32))
    q, k = i[:, None] + P, np.arange(2 * P)[None, :]
    put("causal", np.where(k <= q, 0.0, -1e30).astype(np.float32))
    put("band", np.where((k <= q) & (q - k < 128), 0.0, -1e30).astype(np.float32))
    reset = np.ones((P, TOK), np.float32)
    reset[:, ::CHUNK] = 0.0
    put("reset", reset)
    put("invf", np.tile(np.power(np.float32(10000.0), -np.arange(0, 64, 2, dtype=np.float32) / np.float32(64)).astype(np.float32), (P, 1)))
    comb = np.zeros((P, 4), np.float32)
    comb[0, 0] = comb[2, 0] = comb[1, 1] = comb[3, 1] = 1.0
    put("comb", comb)
    lam = [0.8 - 0.6 * math.exp(-0.3 * l) for l in range(2)]
    put("eps", np.tile(np.array([EPS, 1e-5, *lam, *(1.0 - l for l in lam)], np.float32), (P, 1)))
    inv = np.zeros((4, TOK), np.float32)
    for g, w in enumerate(POOL_WINDOWS):
        def cnt(n):
            t = np.arange(n)
            return np.minimum(t + w // 2 - 1, n - 1) - np.maximum(t - w // 2, 0) + 1
        inv[g, :SEQ] = 1.0 / (cnt(SEQ // GRID_W)[:, None] * cnt(GRID_W)[None, :]).reshape(-1)
        inv[g, SEQ:] = 1.0 / cnt(SEQ)
    return c, inv


class Chain:

    def __init__(self, eng, sem):
        self.eng, self.sem, self.n, self.it, self.stride, self.base = eng, sem, 0, None, 0, 0

    def value(self):
        return self.n if self.it is None else self.it * self.stride + self.n

    def __call__(self, ins):
        self.n += 1
        ins.then_inc(self.sem, 1)
        return self

    def done(self):
        self.eng.wait_ge(self.sem, self.value())

    @contextmanager
    def loop(self, it, first, count, stride):
        start = self.n
        if isinstance(it, int):
            yield
            return
        self.it, self.stride = it, stride
        self.n = start - first * stride
        base = self.n
        yield
        assert self.n - base == stride, (self.sem, self.n - base)
        self.it = None
        self.n = start + count * stride


class Chunk:

    def __init__(self, start, raw, spl, arrived):
        self.start, self.raw, self.spl, self.arrived = start, raw, spl, arrived

    def half(self, h):
        return self.start + (h + 1)


class Stream:

    def __init__(self, phases):
        self.base, self.rawbase, self.loads = {}, {}, {}
        n, raw = RAW, [0] * RAW
        for name, times, loads in phases:
            assert len(loads) % RAW == 0
            self.base[name], self.rawbase[name], self.loads[name] = n, list(raw), loads
            n += times * len(loads)
            for c, l in enumerate(loads):
                raw[c % RAW] += 16 * l * times

    def chunk(self, name, it, c):
        loads = self.loads[name]
        slot = c % RAW
        per = 16 * sum(l for j, l in enumerate(loads) if j % RAW == slot)
        upto = 16 * sum(l for j, l in enumerate(loads[:c + 1]) if j % RAW == slot)
        return Chunk(it * (2 * len(loads)) + 2 * (self.base[name] + c), slot, (self.base[name] + c) % SPL,
                     it * per + (self.rawbase[name][slot] + upto))

ARENA = 14848
MS = 66


def half_tile(t, n):
    at = (t // 2) * 2 * BLK + (t % 2) * n
    return slice(at, at + n)


def flat_rows(ap):
    names = "abcd"[:len(ap.shape)]
    flat = ap.rearrange(f"{' '.join(names)} -> ({' '.join(names)})") if len(names) > 1 else ap
    return flat.rearrange("(r p) -> r p", p=P)

A_Q, A_K, A_V, A_G, B_Q, B_K, B_G, C_Q, C_KV, C_KR, C_G = 0, 512, 1024, 1536, 2048, 3072, 3328, 4352, 4864, 5376, 5440
BLOCKS = [("cq", 4), ("ckv", 4), ("kvr", 4), ("bq0", 4), ("uq_nope", 1), ("uq_rope", 1), ("ukv_k", 1), ("ukv_v", 1),
          ("bg0", 4), ("bq1", 4), ("bg1", 4), ("aq", 4), ("ak", 4), ("av", 4), ("ag", 4), ("cg", 4)]
COLUMN = {"cq": C_Q, "ckv": C_KV, "bq0": B_Q, "bq1": B_Q + 512, "bg0": B_G, "bg1": B_G + 512, "aq": A_Q, "ak": A_K,
          "av": A_V, "ag": A_G, "cg": C_G}
BNUM = {name: i for i, (name, _) in enumerate(BLOCKS)}
BLOCK_OF = [i for i, (_, n) in enumerate(BLOCKS) for _ in range(n)]
NPROJ = len(BLOCK_OF)
HYB_LOADS = [{"kvr": 4, "uq_nope": 4, "uq_rope": 4, "ukv_k": 4, "ukv_v": 4}.get(BLOCKS[b][0], 1) for b in BLOCK_OF] + [1] * 16
PAIRS = [("m", 0), ("m", 1)] + [("b", i) for i in range(8)] + [("a", i) for i in range(4)]
NPAIR = len(PAIRS)
AFTER = {7: ["move cq"], 11: ["norm cq"], 15: ["move ckv"], 19: ["norm ckv"], 23: ["move kvr"], 25: ["turn kvr"],
         31: ["move bq0"], 33: ["turn bq0", "move uq_nope"], 35: ["move uq_rope"], 37: ["turn uq_rope", "move ukv_k"],
         39: ["move ukv_v"], 59: ["turn bq1"], 75: ["turn aq"], 83: ["turn ak"], 103: ["move cg"]}
for _n in range(NPAIR):
    _at = 41 + 4 * _n + (4 if PAIRS[_n][0] == "a" else 0)
    for _what, _h in (("score", _at), ("flip", _at + 3), ("weigh", _at + 5)):
        AFTER.setdefault(_h, []).append(f"{_what} {_n}")
for _h, _name in ((48, "bg0"), (56, "bq1"), (64, "bg1"), (72, "aq"), (80, "ak"), (88, "av"), (96, "ag")):
    AFTER.setdefault(_h, []).append(f"move {_name}")
USE45 = [x for i in sorted(AFTER) for x in AFTER[i] if x.split()[0] in ("norm", "score", "weigh")]
USE67 = [x for i in sorted(AFTER) for x in AFTER[i] if x.split()[0] in ("turn", "flip")]
TURNS = [x.split()[1] for i in sorted(AFTER) for x in AFTER[i] if x.startswith("turn")]
YT = KT // 2
TWO_PI = 6.283185307179586
PI_HI = 6.28125
PI_MID = float(np.float32(TWO_PI - PI_HI))
PI_LO = TWO_PI - PI_HI - PI_MID
ROUND = 12582912.0
ACT_STEPS = 32
DVE_STEPS = 131


def first_block_and_hybrid(nc, a):
    ctx = ExitStack()
    with ctx:
        def sb(name, shape, dt=F32):
            return ctx.enter_context(nc.sbuf_tensor(name, shape, dt))

        def sem(name):
            return ctx.enter_context(nc.semaphore(name))

        raw = sb("raw", [P, RAW, 4 * BLK])
        wh = sb("wh", [P, SPL, 4 * BLK], F32R)
        wl = sb("wl", [P, SPL, 4 * BLK], F32R)
        hTh = sb("hTh", [P, KT, TOK], F32R)
        hTl = sb("hTl", [P, KT, TOK], F32R)
        cst = sb("cst", [P, NCONST])
        prm = sb("prm", [P, 4 * P])
        adaT = sb("adaT", [P, 96, 2])
        s4 = sb("s4", [P, P], F32R)
        dg = sb("dg", [P, 4, P])
        small = sb("small", [P, 512])
        arena = sb("arena", [P, ARENA])

        ps = ctx.enter_context(nc.psum_tensor("ps", [P, 8, BLK], F32))
        x_save = nc.dram_tensor("x_save", (SEQ, D), F32, kind="Internal").ap()

        def C(name, n=None):
            w = dict(CONSTS)[name] if n is None else n
            return cst[:, CCOL[name]:CCOL[name] + w]

        ident, ones = C("ident"), C("ones")
        eps = C("eps")[:, 0:1]

        def area(at, *dims):
            n = int(np.prod(dims))
            v = arena[:, at:at + n]
            if len(dims) == 2:
                v = v.rearrange("p (a b) -> p a b", a=dims[0])
            if len(dims) == 3:
                v = v.rearrange("p (a b c) -> p a b c", a=dims[0], b=dims[1])
            return v

        X4 = area(0, 4, D)
        Y0 = area(0, KT, TOK)
        S0 = 4 * D
        HB = area(S0, 4, TOK)
        V = area(S0, 2, FLAT)
        SA = area(S0 + 2 * FLAT, 2, FLAT)
        SB_ = area(S0 + 4 * FLAT, 2, FLAT)
        G2 = area(S0 + 6 * FLAT, 2, TOK)
        PO = area(S0 + 6 * FLAT + 2 * TOK, 2, TOK)
        INV = area(S0 + 6 * FLAT + 4 * TOK, TOK)
        PW = area(S0 + 6 * FLAT + 5 * TOK, 2, 256)
        AROW = dg[:, :, :].rearrange("p a b -> p (a b)")
        GE = PO
        CX, CB, CC = area(S0, TOK), area(S0 + TOK, TOK), area(S0 + 2 * TOK, TOK)
        CT = area(S0 + 3 * TOK, 2, SEQ)
        CG, CE = area(S0 + 4 * TOK, TOK), INV
        U = area(S0 + 5 * TOK, 2, SEQ + 2)
        GB0 = area(S0, 2, D)
        XR0 = area(S0 + 2 * D, 2, D // 2)

        Y1 = area(0, KT, SEQ)
        W1 = 2 * D
        X1 = area(W1, 2, D)
        Z, R, B = (area(W1 + 2 * TOK * i, 2, TOK) for i in range(3))
        QD, KI = (area(W1 + 6 * TOK + TOK * i, 2, SEQ) for i in range(2))
        W1b = W1 + 8 * TOK
        Q, SG, GH = (area(W1b + SEQ * i, SEQ) for i in range(3))
        IT, V1, KD = area(W1b + 768, TOK), area(W1b + 1280, 4, P), area(W1b + 1792, 4, P)
        ST = area(W1b + 2304, 2, 4 * P)
        SX = area(W1b + 3328, 2, P)
        SC = area(W1b + 3584, 2, 2 * P)
        OS, RH = area(W1b + 4096, SEQ), area(W1b + 4352, SEQ)
        DEC = small[:, 360:376].rearrange("p (d n) -> p d n", d=2)
        GB1 = area(W1b + 4608, 1, D)
        XR1 = area(2 * W1, 2, D // 2)
        pT, pO, pQ = ps[:, 4, :], ps[:, 7, 0:SEQ], ps[:, 7, SEQ:TOK]
        ORDER = [[4, 5, 6, 7, 0, 1, 2, 3], [7, 6, 5, 4, 3, 2, 1, 0]]
        Yt = area(0, 2, D)
        XN = X1
        M = 2 * D
        QN, QR, KN = area(M, 4, SEQ), area(M + 1024, 2, SEQ), area(M + 1536, 4, SEQ)
        KR, VC = area(M + 2560, SEQ), area(M + 2816, 2, BLK)
        AQ, AK, AV = area(M, 4, SEQ), area(M + 1024, 4, SEQ), area(M + 2048, 2, BLK)
        KS = area(M, 2, 3 * P)
        BK, BV = area(M + 3840, 2, SEQ), area(M + 4352, 2, P)
        BQ = area(M + 4608, 8, SEQ)
        SR, TM = area(M + 7680, 2, BLK), area(M + 8704, 2, SEQ)
        EX, PT = area(M + 9216, 2, 3 * P), area(M + 9984, 2, 3 * P)
        HQ = area(M + 9216, 4, SEQ)
        LQ = area(M + 9216, 4, 64)
        HBN = area(M + 4608, 4, SEQ)
        GBN = area(0, 1, D)
        XRN = area(D, 2, D // 2)
        DQ = area(M + 8704, 4, P)
        csn = small[:, 376:504]
        cosv = small[:, 376:440].rearrange("p (t d) -> p t d", t=2)
        sinv = small[:, 440:504].rearrange("p (t d) -> p t d", t=2)
        SUB = small[:, 136:264]
        SNK, NSK = small[:, 264:280], small[:, 316:332]
        NM, LS, ES, RL = (small[:, 280 + 4 * i:284 + 4 * i] for i in range(4))
        lamt, qss, qrs = small[:, 296:300], small[:, 304:308], small[:, 308:312]
        oss, ors, LN = small[:, 312:314], small[:, 314:316], small[:, 332:334]
        NL = small[:, 334:335]
        posf = small[:, 504:506]
        ang, turns_ = small[:, 440:504], small[:, 8:72]
        posi, posr = ST[0:2, 0, 0:P].bitcast(I32), ST[0:2, 1, 0:P]
        OJ = TM[:, :, 0:P]
        psA = ps[0:MS, 4, :]
        psT = ps[:, 5, 0:8].rearrange("p (a b) -> p a b", b=2)

        ssq = small[:, 0:4]
        part = small[:, 360:376]
        AROW0 = area(S0 + 4 * TOK, TOK)
        SQ0, SQ1, SQN = area(S0 + 3 * D, BLK), area(2 * W1 + D, BLK), area(M + 8704, BLK)
        rs = small[:, 4:8]
        silc = small[:, 8:40]
        sile = small[:, 40:72]
        lbt = small[:, 72:168].rearrange("p (d l k) -> p d l k", d=2, l=3)
        lbm = small[:, 168:200].rearrange("p (d k) -> p d k", d=2)
        lbs = small[:, 200:232].rearrange("p (d k) -> p d k", d=2)
        lb = small[:, 232:264]
        oml = small[:, 264:296]
        modA = small[:, 296:328].rearrange("p (k v) -> p k v", v=2)
        gp = small[:, 328:360].rearrange("p (k v) -> p k v", v=2)

        st = Stream([
            ("ada", 8, [1] * 4),
            ("pool", 4, [4 if i in POOL_AT else 1 for i in range(12)]),
            ("conv", 8, [4, 1] * 4),
            ("out0", 2, [1] * 8),
            ("hg", 16, [2] * 8),
            ("out1", 2, [1] * 8),
            ("hyb", 2, HYB_LOADS),
        ])

        s_raw = [sem(f"raw_arrived{i}") for i in range(RAW)]
        s_load = sem("load_step")
        s_hi, s_lo, s_used = sem("high_ready"), sem("low_ready"), sem("chunk_used")
        s_dve, s_act = sem("dve_step"), sem("act_step")
        s_cst, s_prow, s_prT, s_prm = sem("const_arrived"), sem("param_rows"), sem("param_turned"), sem("param_ready")
        s_sil, s_s4h, s_s4 = sem("silu_ready"), sem("silu_high"), sem("silu_split")
        s_arow, s_adaP, s_adaT = sem("ada_row"), sem("ada_turned"), sem("ada_ready")
        s_mod = sem("mod_ready")
        s_xin = sem("x_arrived")
        s_rs, s_dg = sem("rstd_ready"), sem("diag_ready")
        s_sqp, s_ssq = sem("squares_taken"), sem("squares_added")
        s_pt, s_ph, s_phi, s_plo = sem("h_turned"), sem("h_ready"), sem("h_high"), sem("h_low")
        s_pg, s_pv = sem("pool_gate_moved"), sem("pool_moved")
        s_inv, s_po, s_mix, s_py = sem("pool_consts"), sem("pooled"), sem("pool_mixed"), sem("pool_out")
        s_ce, s_cx, s_cv = sem("conv_gate_moved"), sem("conv_moved"), sem("conv_out")
        s_yh, s_yl = sem("y_high"), sem("y_low")
        s_gd, s_gb, s_gbe = sem("gate_diag"), sem("gate_spread"), sem("gate_moved")
        s_oe = sem("out_moved")
        s_xr, s_xa, s_save = [sem(f"residual_arrived{i}") for i in range(2)], sem("residual_added"), sem("x_saved")
        s_out = sem("result_stored")
        s_hev = sem("head_moved")
        s_f, s_ln, s_b, s_ex, s_kdr = sem("forget_ready"), sem("log_forget"), sem("decay_summed"), sem("decay_exp"), sem("keys_ready")
        s_vT, s_v, s_kT, s_kd = sem("v_turned"), sem("v_ready"), sem("k_turned"), sem("k_moved")
        s_ds, s_st, s_scp, s_sc = sem("state_steps"), sem("states_ready"), sem("scores"), sem("scores_masked")
        s_o, s_osq, s_sq, s_rso, s_y1 = sem("head_summed"), sem("head_squared"), sem("squares_summed"), sem("head_rstd"), sem("head_out")
        s_sgr = sem("head_gate")
        s_l1 = sem("layer1_region_free")
        s_pos, s_posf, s_posT, s_ang, s_sin = sem("positions"), sem("positions_float"), sem("positions_turned"), sem("angles"), sem("sines")
        s_lp, s_lam, s_lamx = sem("layer_params"), sem("lambda_parts"), sem("lambda_exp")
        s_bm = [sem(f"block_moved{i}") for i in range(2)]
        s_45, s_67 = sem("banks45_read"), sem("banks67_read")
        s_qs, s_qd, s_qn, s_qh, s_qhi, s_qlo = sem("rank_stats"), sem("rank_diag"), sem("rank_turned"), sem("rank_scaled"), sem("rank_high"), sem("rank_low")
        s_rr, s_tn = sem("roped"), sem("block_turned")
        s_S, s_nm, s_e, s_p = sem("scored"), sem("max_ready"), sem("exp_ready"), sem("probs_ready")
        s_fl, s_W, s_os = sem("probs_flipped"), sem("weighed"), sem("head_norm_ready")
        s_gx = sem("gate_exp")
        s_yt, s_yth, s_ytl = sem("y_turned"), sem("y_turned_high"), sem("y_turned_low")
        s_gl, s_ld = sem("post_norm_arrived"), sem("layer_done")

        block = ctx.enter_context(nc.Block())

        adaw = a["ada_w"].rearrange("l (c t p) n -> l c p t n", t=4, p=P)
        evw = a["ev_w_in"][0]
        w_out0 = a["ev_w_out"][0].rearrange("(c t p) n -> c p t n", t=4, p=P)

        @block.sync
        def _(sp):
            def load(ch, pieces):
                sp.wait_ge(s_lo, ch.half(1) - 2 * RAW)
                sp.sem_inc(s_load, 1)
                for dst, src in pieces:
                    sp.dma_start(dst, src).then_inc(s_raw[ch.raw], 16)

            def slot4(ch):
                return raw[:, ch.raw, :].rearrange("p (t n) -> p t n", t=4)

            with sp.Fori(0, 8) as b:
                for c in range(4):
                    ch = st.chunk("ada", b, c)
                    load(ch, [(slot4(ch), adaw[0, c][:, :, bass.ds(b * BLK, BLK)])])
            for g in range(4):
                for i in range(12):
                    ch = st.chunk("pool", g, i)
                    if i in POOL_AT:
                        c = POOL_AT.index(i)
                        load(ch, [(raw[:, ch.raw, t * BLK:(t + 1) * BLK].rearrange("p (a n) -> p a n", a=2),
                                   evw[(4 * c + t) * P:(4 * c + t + 1) * P, 0:2 * POOL_W]
                                   .rearrange("p (a n) -> p a n", a=2)[:, :, g * 256:(g + 1) * 256]) for t in range(4)])
                    else:
                        c = POOL_ADA.index(i)
                        b = 8 + 2 * g + c // 4
                        load(ch, [(slot4(ch), adaw[b // 12, c % 4][:, :, (b % 12) * BLK:(b % 12 + 1) * BLK])])
            with sp.Fori(0, 8) as j:
                for c in range(4):
                    ch = st.chunk("conv", j, 2 * c)
                    load(ch, [(raw[:, ch.raw, t * BLK:(t + 1) * BLK].rearrange("p (a n) -> p a n", a=4),
                               evw[(4 * c + t) * P:(4 * c + t + 1) * P, 2 * POOL_W:]
                               .rearrange("p (a n) -> p a n", a=4)[:, :, bass.ds(j * P, P)]) for t in range(4)])
                    ch = st.chunk("conv", j, 2 * c + 1)
                    load(ch, [(slot4(ch), adaw[1, c][:, :, bass.ds(j * BLK + 4 * BLK, BLK)])])
            with sp.Fori(0, 2) as i:
                for c in range(8):
                    ch = st.chunk("out0", i, c)
                    load(ch, [(slot4(ch), w_out0[c % 4][:, :, bass.ds(i * (2 * BLK) + (c // 4) * BLK, BLK)])])
            odw = a["od_w_in"][0]
            with sp.Fori(0, HEADS) as h:
                for c in range(8):
                    ch = st.chunk("hg", h, c)
                    load(ch, [(raw[:, ch.raw, t * 2 * BLK:t * 2 * BLK + 5 * P].rearrange("p (a n) -> p a n", a=5),
                               odw[(2 * c + t) * P:(2 * c + t + 1) * P, :].rearrange("p (a n) -> p a n", a=5)[:, :, bass.ds(h * P, P)])
                              for t in range(2)])
            w_out1 = a["od_w_out"][0].rearrange("(c t p) n -> c p t n", t=4, p=P)
            for m, (n, c) in enumerate(OUT1):
                ch = st.chunk("out1", m // 8, m % 8)
                load(ch, [(slot4(ch), w_out1[c][:, :, n * BLK:(n + 1) * BLK])])
            w_in2 = a["w_in_2"].rearrange("l (c t p) n -> l c p t n", t=4, p=P)
            w_out2 = a["w_out_2"].rearrange("l (c t p) n -> l c p t n", t=4, p=P)
            layer = lambda x, L: x[bass.ds(L, 1)]
            one = lambda x: x.rearrange("o p t n -> (o p) t n")
            with sp.Fori(0, 2) as L:
                for i in range(NPROJ):
                    name = BLOCKS[BLOCK_OF[i]][0]
                    c = i - BLOCK_OF.index(BLOCK_OF[i])
                    ch = st.chunk("hyb", L, i)
                    if name in COLUMN:
                        load(ch, [(slot4(ch), one(layer(w_in2[:, c], L)[:, :, :, COLUMN[name]:COLUMN[name] + BLK]))])
                    elif name == "kvr":
                        dst = [raw[:, ch.raw, h * 2 * BLK:h * 2 * BLK + 2 * 320].rearrange("p (t n) -> p t n", t=2) for h in range(2)]
                        load(ch, [(dst[h][:, :, to], one(layer(w_in2[:, c], L)[:, :, 2 * h:2 * h + 2, at:at + n])) for h in range(2)
                                  for to, at, n in ((slice(0, 256), B_K, 256), (slice(256, 320), C_KR, 64))])
                    else:
                        w, per, first, n = {"uq_nope": ("w_uq_2", 192, 0, 128), "uq_rope": ("w_uq_2", 192, 128, 64),
                                            "ukv_k": ("w_ukv_2", 256, 0, 128), "ukv_v": ("w_ukv_2", 256, 128, 128)}[name]
                        load(ch, [(raw[:, ch.raw, half_tile(t, 4 * n)].rearrange("p (a n) -> p a n", a=4),
                                   one(layer(a[w][:, t * P:(t + 1) * P, :].rearrange("l p (a n) -> l p a n", n=per), L)[:, :, :, first:first + n]))
                                  for t in range(4)])
                for i in range(16):
                    ch = st.chunk("hyb", L, NPROJ + i)
                    load(ch, [(slot4(ch), one(layer(w_out2[:, i % 4], L)[:, :, :, (i // 4) * BLK:(i // 4 + 1) * BLK]))])
            for u in range(4):
                sp.wait_ge(s_xa, 17 + u)
                f = slice((u % 2) * (D // 2), (u % 2 + 1) * (D // 2))
                sp.dma_start(a["out"][0, (u // 2) * P:(u // 2 + 1) * P, f], XN[:, u // 2, f]).then_inc(s_out, 16)
            sp.wait_ge(s_out, 64)

        @block.scalar
        def _(act):
            step = Chain(act, s_act)

            def hi(ch, n=4 * BLK, halves=(0, 1)):
                for h in halves:
                    part = slice(h * 2 * BLK, h * 2 * BLK + n // 2)
                    if h == 0:
                        act.wait_ge(s_raw[ch.raw], ch.arrived)
                    act.wait_ge(s_used, ch.half(h) - 2 * SPL)
                    nc.scalar.activation(wh[:, ch.spl, part], raw[:, ch.raw, part], ACT.Copy).then_inc(s_hi, 1)

            act.sem_inc(s_hi, 2 * RAW)
            act.dma_start(cst[:, :], a["consts"]).then_inc(s_cst, 16)
            for t, rows in enumerate(PARAM_ROWS):
                at = 0
                for name, n in rows:
                    act.dma_start(dg[at:at + n, t, :], flat_rows(a[name])).then_inc(s_prow, 16)
                    at += n
            for t in range(4):
                src = a["x"][0] if t < 2 else a["ctx"][0]
                act.dma_start(X4[:, t, :], src[(t % 2) * P:(t % 2 + 1) * P, :]).then_inc(s_xin, 16)
            act.wait_ge(s_prm, 1)
            nc.scalar.activation(sile, prm[:, 0:32], ACT.Exp, scale=-1.0).then_inc(s_sil, 1)
            act.wait_ge(s_sil, 2)
            act.wait_ge(s_s4, 1)
            nc.scalar.activation(s4[:, 0:4 * KT].rearrange("p (k v) -> p k v", v=4)[:, :, 0:2], silc.rearrange("p (v k) -> p k v", v=2), ACT.Copy).then_inc(s_s4h, 1)
            act.wait_ge(s_sil, 3)
            nc.scalar.activation(lbt, lbt, ACT.Exp).then_inc(s_sil, 1)

            def inverse_rms(n, T):
                act.wait_ge(s_ssq, n)
                step(nc.scalar.activation(rs[:, 0:T], ssq[:, 0:T], ACT.Ln, scale=1.0 / D, bias=eps)).done()
                nc.scalar.activation(rs[:, 0:T], rs[:, 0:T], ACT.Exp, scale=-0.5).then_inc(s_rs, 1)

            def x_squares(X, T, base):
                for u in range(2 * T):
                    if u == 4:
                        step.done()
                    act.wait_ge(s_xa, base + (u + 1))
                    f = slice((u % 2) * (D // 2), (u % 2 + 1) * (D // 2))
                    step(nc.scalar.activation(ps[:, 2 * (u % 4):2 * (u % 4) + 2, :], X[:, u // 2, f].rearrange("p (a b) -> p a b", a=2),
                                              ACT.Square, accum_out=part[:, u:u + 1]))
                step.done()
                act.sem_inc(s_sqp, 1)

            def y_squares(T, bank, n, SQ):
                for t in range(T):
                    step(nc.scalar.activation(SQ, ps[:, bank + t, :], ACT.Square, accum_out=part[:, 4 * t + n:4 * t + n + 1])).done()
                    act.sem_inc(s_sqp, 1)

            for c in range(4):
                hi(st.chunk("ada", 0, c))
            act.wait_ge(s_xin, 64)
            for t in range(4):
                step(nc.scalar.activation(ps[:, 0:4, :], X4[:, t, :].rearrange("p (a b) -> p a b", a=4), ACT.Square,
                                          accum_out=ssq[:, t:t + 1])).done()
            act.sem_inc(s_ssq, 1)
            for c in range(4):
                hi(st.chunk("ada", 1, c))
            inverse_rms(1, 4)
            with act.Fori(2, 8) as b:
                for c in range(4):
                    hi(st.chunk("ada", b, c))

            def high_h(r, hb, n, split):
                for k in range(KT):
                    act.wait_ge(s_ph, r * KT + (k + 1))
                    nc.scalar.activation(hTh[:, k, 0:n], hb[:, k % 4, 0:n], ACT.Copy).then_inc(s_phi, 1)
                    split(k)

            hi(st.chunk("pool", 0, 0))
            hi(st.chunk("pool", 0, 1))
            high_h(0, HB, TOK, lambda k: None)

            def pool_move(g):
                if g:
                    act.wait_ge(s_po, g)
                    act.wait_ge(s_py, g)
                act.wait_ge(s_used, st.chunk("pool", g, POOL_AT[3]).half(1))
                nc.scalar.activation(G2, ps[:, 2:4, :], ACT.Copy)
                nc.scalar.activation(GE, ps[:, 2:4, :], ACT.Exp, scale=-1.0).then_inc(s_pg, 1)

            def pool_consts(g):
                act.dma_start(INV, a["inv"][g]).then_inc(s_inv, 16)
                act.dma_start(PW, a["ev_pool_w"][0, g].rearrange("(a p) o -> p a o", p=P)).then_inc(s_inv, 16)

            for g in range(4):
                for i in range(0 if g else 2, 12):
                    ch = st.chunk("pool", g, i)
                    if i == 0:
                        hi(ch, halves=(0,))
                        if g:
                            pool_move(g - 1)
                        hi(ch, halves=(1,))
                        if g:
                            pool_consts(g - 1)
                    else:
                        hi(ch)

            hi(st.chunk("conv", 0, 0), halves=(0,))
            pool_move(3)
            hi(st.chunk("conv", 0, 0), halves=(1,))
            pool_consts(3)
            for i in range(1, 8):
                hi(st.chunk("conv", 0, i))

            def conv_move(j):
                act.wait_ge(s_used, st.chunk("conv", j, 6).half(1))
                act.wait_ge(s_cv, j + 1)
                nc.scalar.activation(CC, ps[:, 2, :], ACT.Copy)
                nc.scalar.activation(CG, ps[:, 3, :], ACT.Copy)
                nc.scalar.activation(CE, ps[:, 3, :], ACT.Exp, scale=-1.0).then_inc(s_ce, 1)

            with act.Fori(1, 8) as j:
                hi(st.chunk("conv", j, 0), halves=(0,))
                conv_move(j - 1)
                hi(st.chunk("conv", j, 0), halves=(1,))
                for i in range(1, 8):
                    hi(st.chunk("conv", j, i))
            def high_y(k, Yk, n):
                nc.scalar.activation(hTh[:, k, 0:n], Yk, ACT.Copy).then_inc(s_yh, 1)

            hi(st.chunk("out0", 0, 0))
            conv_move(7)
            for k in range(8):
                high_y(k, Y0[:, k, :], TOK)
            hi(st.chunk("out0", 0, 1))
            act.wait_ge(s_cv, 9)
            for k in range(8, KT):
                high_y(k, Y0[:, k, :], TOK)

            def spread(r, q, v, G):
                act.wait_ge(s_gb, r + 1)
                nc.scalar.activation(G[:, v, q * BLK:(q + 1) * BLK], ps[:, 6 + r % 2, :], ACT.Copy).then_inc(s_gbe, 1)

            def load_x(u, src, XR):
                act.dma_start(XR[:, u % 2, :], src(u // 2)[:, (u % 2) * (D // 2):(u % 2 + 1) * (D // 2)]).then_inc(s_xr[u % 2], 16)

            def residual(T, src, XR, base):
                for u in range(2, 2 * T):
                    act.wait_ge(s_xa, base + (u - 1))
                    load_x(u, src, XR)

            def out_split(name, i, before):
                for m in range(before, 16):
                    hi(st.chunk(name, i, m))

            x_of = lambda t: (a["x"][0] if t < 2 else a["ctx"][0])[(t % 2) * P:(t % 2 + 1) * P, :]
            for u in range(2):
                load_x(u, x_of, XR0)
            spreads = {2: (0, 1, 2), 3: (3, 4, 5, 6), 4: (7,)}
            for m in range(2, 16):
                hi(st.chunk("out0", m // 8, m % 8))
                for r in spreads.get(m, ()):
                    spread(r, r % 4, r // 4, GB0)
                if m % 4 == 1 and m > 4:
                    act.wait_ge(s_used, st.chunk("out0", (m - 2) // 8, (m - 2) % 8).half(1))
                    y_squares(4, 4 * ((m // 4 - 1) % 2), m // 4 - 1, SQ0)
            act.wait_ge(s_used, st.chunk("out0", 1, 7).half(1))
            y_squares(4, 4, 3, SQ0)
            inverse_rms(2, 4)
            residual(4, x_of, XR0, 0)
            x_squares(X4, 4, 0)

            def save(X, base):
                act.wait_ge(s_xa, base + 4)
                for t in range(2):
                    act.dma_start(x_save[t * P:(t + 1) * P, :], X[:, t, :]).then_inc(s_save, 16)

            save(X4, 0)
            inverse_rms(3, 4)
            for c in range(2):
                hi(st.chunk("hg", 0, c), 10 * P)
            high_h(1, HB, TOK, lambda k: hi(st.chunk("hg", 0, (k - 1) // 2), 10 * P) if k >= 5 and k % 2 else None)

            def head(h, split, comp=True, fin=True):
                split(0)
                if comp:
                    act.wait_ge(s_used, st.chunk("hg", h, 0).half(1) - 2)
                    act.wait_ge(s_kdr, h * 2)
                    for d in range(2):
                        nc.scalar.activation(Z[:, d, :], ps[:, d, :], ACT.Exp, scale=-1.0).then_inc(s_hev, 1)
                    nc.scalar.activation(IT, ps[:, 2, :], ACT.Copy).then_inc(s_hev, 1)
                    nc.scalar.activation(Q, ps[:, 3, 0:SEQ], ACT.Copy)
                    act.wait_ge(s_sgr, h)
                    nc.scalar.activation(SG, ps[:, 3, SEQ:TOK], ACT.Copy)
                    nc.scalar.activation(GH, ps[:, 3, SEQ:TOK], ACT.Exp, scale=-1.0).then_inc(s_hev, 1)
                split(1)

                def log_forget(d):
                    act.wait_ge(s_f, h * 2 - 1 + d)
                    nc.scalar.activation(R[:, d, :], R[:, d, :], ACT.Ln).then_inc(s_ln, 1)

                def decays(d):
                    act.wait_ge(s_b, h * 2 - 1 + d)
                    last = B[:, d, :].rearrange("p (n c) -> p n c", c=CHUNK)[:, :, CHUNK - 1] if d == 0 else \
                        B[:, d, :].rearrange("p (n c) -> p n c", c=CHUNK)[:, :, 0]
                    nc.scalar.activation(R[:, d, :], R[:, d, :], ACT.Exp)
                    nc.scalar.activation(QD[:, d, :], B[:, d, 0:SEQ], ACT.Exp)
                    nc.scalar.activation(KI[:, d, :], B[:, d, 0:SEQ], ACT.Exp, scale=-1.0)
                    nc.scalar.activation(DEC[:, d, :], last, ACT.Exp).then_inc(s_ex, 1)

                if fin:
                    square_head(h - 1)
                if comp:
                    act.wait_ge(s_vT, h)
                    nc.scalar.activation(V1, pT.rearrange("p (a b) -> p a b", a=4), ACT.Copy).then_inc(s_v, 1)
                    log_forget(0)
                split(2)
                if fin:
                    head_rms(h - 1)
                if comp:
                    decays(0)
                split(3)
                if comp:
                    log_forget(1)
                split(4)
                if comp:
                    decays(1)
                for c in range(5, 8):
                    split(c)

            def square_head(h):
                act.wait_ge(s_o, h)
                nc.scalar.activation(OS, pO, ACT.Square).then_inc(s_osq, 1)

            def head_rms(h):
                act.wait_ge(s_sq, h)
                step(nc.scalar.activation(RH, pQ, ACT.Ln, scale=1.0 / P, bias=eps)).done()
                nc.scalar.activation(RH, RH, ACT.Exp, scale=-0.5).then_inc(s_rso, 1)

            def head_chunks(h):
                return lambda c: hi(st.chunk("hg", h, c), 10 * P)

            act.wait_ge(s_l1, 1)
            act.dma_start(posi, a["positions_2"][0].rearrange("(t p) -> t p", t=2)).then_inc(s_pos, 16)
            for q in range(4):
                spread(8 + q, q, 0, GB1)
            act.wait_ge(s_ang, 1)
            nc.scalar.activation(csn, csn, ACT.Sin).then_inc(s_sin, 1)
            act.wait_ge(s_save, 32)
            act.wait_ge(s_plo, 2 * KT)
            head(1, head_chunks(1), fin=False)
            with act.Fori(2, HEADS) as h, step.loop(h, 2, HEADS - 2, 1):
                head(h, head_chunks(h))

            def out_chunks(c):
                if c < 7:
                    hi(st.chunk("out1", 0, c))
                for k in {0: range(4), 1: range(4, 8), 2: range(8, 12), 4: range(12, 15)}.get(c, ()):
                    act.wait_ge(s_y1, k + 2)
                    high_y(k, Y1[:, k, :], SEQ)

            head(HEADS, out_chunks)
            square_head(HEADS)
            head_rms(HEADS)
            x_rows = lambda t: x_save[t * P:(t + 1) * P, :]
            act.wait_ge(s_y1, HEADS + 1)
            high_y(KT - 1, Y1[:, KT - 1, :], SEQ)
            for u in range(2):
                load_x(u, x_rows, XR1)
            for m in range(7, 16):
                hi(st.chunk("out1", m // 8, m % 8))
                if m in (8, 9):
                    act.wait_ge(s_used, st.chunk("out1", 0, m - 2).half(1))
                    y_squares(2, 2 * (m - 8), m - 8, SQ1)
                if m == 13:
                    act.wait_ge(s_used, st.chunk("out1", 1, 3).half(1))
                    y_squares(2, 0, 2, SQ1)
            act.wait_ge(s_used, st.chunk("out1", 1, 7).half(1))
            y_squares(2, 2, 3, SQ1)
            inverse_rms(4, 2)
            residual(2, x_rows, XR1, 8)

            def hyb_split(L, i, halves=(0, 1)):
                width = {"kvr": 4 * 320, "uq_rope": 4 * 256}.get(BLOCKS[BLOCK_OF[i]][0], 4 * BLK) if i < NPROJ else 4 * BLK
                hi(st.chunk("hyb", L, i), width, halves)

            def hyb_layer(L):
                count = lambda total, n: L * total + n
                banks = lambda b: ps[:, 2 * (b % 2):2 * (b % 2) + 2, :]
                x_squares(XN, 2, L * 4 + 8)
                save(XN, L * 4 + 8)
                inverse_rms(L * 2 + 5, 2)
                hyb_split(L, 0)
                hyb_split(L, 1)
                high_h(L + 2, HBN, SEQ, lambda k: hyb_split(L, {8: 2, 13: 3}[k]) if k in (8, 13) else None)
                for i, n in enumerate(("q1", "k1", "q2", "k2")):
                    act.dma_start(LQ[:, i, :], a[f"diff_lambda_{n}_2"][bass.ds(L, 1), :].rearrange("o n -> (o n)").partition_broadcast(P)).then_inc(s_lp, 16)
                act.dma_start(SUB, a["diff_subln_w_2"][bass.ds(L, 1), :].rearrange("o n -> (o n)").partition_broadcast(P)).then_inc(s_lp, 16)
                act.dma_start(SNK, a["sink_logits_2"][bass.ds(L, 1), :].rearrange("o n -> (o n)").partition_broadcast(P)).then_inc(s_lp, 16)
                act.wait_ge(s_save, L * 32 + 64)

                def read67(x):
                    return count(len(USE67), USE67.index(x) + 1)

                def done(i):
                    b = BLOCK_OF[i]
                    act.wait_ge(s_used, st.chunk("hyb", L, i).half(1))
                    return b, BLOCKS[b][0]

                def move(name, i):
                    b, _ = done(i)
                    if name in ("cq", "ckv"):
                        v = ("cq", "ckv").index(name)
                        dst = (SR, VC)[v]
                        for t in range(2):
                            step(nc.scalar.activation(dst[:, t, :], banks(b)[:, t, :], ACT.Square, accum_out=qss[:, 2 * v + t:2 * v + t + 1])).done()
                        nc.scalar.activation(dst, banks(b), ACT.Copy).then_inc(s_bm[b % 2], 1)
                        step(nc.scalar.activation(qrs[:, 2 * v:2 * v + 2], qss[:, 2 * v:2 * v + 2], ACT.Ln, scale=1.0 / 512, bias=eps)).done()
                        nc.scalar.activation(qrs[:, 2 * v:2 * v + 2], qrs[:, 2 * v:2 * v + 2], ACT.Exp, scale=-0.5).then_inc(s_qs, 1)
                    elif name in ("uq_nope", "ukv_k"):
                        dst = QN if name == "uq_nope" else KN
                        nc.scalar.activation(dst.rearrange("p (a b) c -> p a b c", a=2), banks(b).rearrange("p a (b c) -> p a b c", b=2),
                                             ACT.Copy).then_inc(s_bm[b % 2], 1)
                    elif name in ("ukv_v", "av"):
                        nc.scalar.activation(VC if name == "ukv_v" else AV, banks(b), ACT.Copy).then_inc(s_bm[b % 2], 1)
                    elif name[1] == "g":
                        if name != "cg":
                            act.wait_ge(s_tn, count(len(TURNS), TURNS.index({"bg0": "uq_rope", "bg1": "bq1", "ag": "ak"}[name]) + 1))
                        else:
                            before = BNUM["ag"]
                            act.wait_ge(s_bm[before % 2], count(len(BLOCKS) // 2, before // 2 + 1))
                        nc.scalar.activation(SR, banks(b), ACT.Exp, scale=-1.0).then_inc(s_gx, 1)

                def norm(name):
                    v = ("cq", "ckv").index(name)
                    for k in range(4):
                        act.wait_ge(s_qh, count(8, 4 * v + k + 1))
                        nc.scalar.activation(hTh[:, 4 * v + k, SEQ:TOK], HQ[:, k, :], ACT.Copy).then_inc(s_qhi, 1)

                def turn_move(name):
                    act.wait_ge(s_tn, count(len(TURNS), TURNS.index(name) + 1))
                    if name == "kvr":
                        nc.scalar.activation(KR, ps[:, 7, 0:SEQ], ACT.Copy)
                        src, dst = ps[:, 6, :].rearrange("p (a b) -> p a b", a=2), BK
                    elif name == "uq_rope":
                        src, dst = ps[:, 6, :].rearrange("p (a b) -> p a b", a=2), QR
                    else:
                        src = ps[:, 6:8, :].rearrange("p x (a b) -> p x a b", a=2)
                        dst = {"bq0": BQ[:, 0:4, :], "bq1": BQ[:, 4:8, :], "aq": AQ, "ak": AK}[name].rearrange("p (x a) b -> p x a b", x=2)
                    nc.scalar.activation(dst, src, ACT.Copy).then_inc(s_67, 1)

                def score(n):
                    act.wait_ge(s_nm, count(NPAIR, n + 1))
                    for q, seg in ((0, slice(0, 2 * P)), (1, slice(2 * P, 3 * P))):
                        for m in range(2):
                            at = 2 * q + m
                            ins = nc.scalar.activation(EX[:, m, seg], EX[:, m, seg], ACT.Exp, bias=NM[:, at:at + 1], accum_out=LS[:, at:at + 1])
                    if PAIRS[n][0] == "b":
                        ins = nc.scalar.activation(ES, ES, ACT.Exp)
                    ins.then_inc(s_e, 1)

                def flip(n):
                    act.wait_ge(s_fl, count(NPAIR, n + 1))
                    if n:
                        act.wait_ge(s_W, count(NPAIR, n))
                    k = 1 if PAIRS[n][0] == "a" else 2
                    nc.scalar.activation(PT[:, 0:k, :], ps[:, 6:6 + k, 0:3 * P], ACT.Copy).then_inc(s_67, 1)

                def weigh(n):
                    kind, h = PAIRS[n]
                    if kind == "a":
                        act.wait_ge(s_W, count(NPAIR, n + 1))
                        for q in range(2):
                            step(nc.scalar.activation(OJ[:, q, :], ps[:, 4, q * P:(q + 1) * P], ACT.Square, accum_out=oss[:, q:q + 1]))
                        step.done()
                        step(nc.scalar.activation(ors, oss, ACT.Ln, scale=1.0 / P, bias=C("eps")[:, 1:2])).done()
                        nc.scalar.activation(ors, ors, ACT.Exp, scale=-0.5).then_inc(s_os, 1)

                def after(i):
                    for what in AFTER.get(i, []):
                        verb, arg = what.split()
                        if verb == "move":
                            move(arg, (i - 1) // 2)
                        elif verb == "norm":
                            norm(arg)
                        elif verb == "turn":
                            turn_move(arg)
                        else:
                            {"score": score, "flip": flip, "weigh": weigh}[verb](int(arg))

                hyb_split(L, 4, (0,))
                for i in range(6, 2 * NPROJ):
                    if i + 3 < 2 * NPROJ:
                        hyb_split(L, (i + 3) // 2, ((i + 3) % 2,))
                    if i == 8:
                        act.wait_ge(s_lam, count(1, 1))
                        nc.scalar.activation(lamt[:, 0:2], lamt[:, 0:2], ACT.Exp).then_inc(s_lamx, 1)
                    after(i)
                hi(st.chunk("hyb", L, NPROJ))
                for g in range(YT):
                    act.wait_ge(s_yt, count(YT, g + 1))
                    nc.scalar.activation(hTh[:, 2 * g:2 * g + 2, 0:SEQ], ps[:, 4 + g % 4, :].rearrange("p (a b) -> p a b", a=2),
                                         ACT.Copy).then_inc(s_yth, 1)
                    if g == 3:
                        hi(st.chunk("hyb", L, NPROJ + 1))
                act.wait_ge(s_yt, count(YT, YT))
                act.dma_start(GBN[:, 0, :], a["post_norm_w_2"][bass.ds(L, 1), :].rearrange("o n -> (o n)").partition_broadcast(P)).then_inc(s_gl, 16)
                for u in range(2):
                    load_x(u, x_rows, XRN)
                for m in range(2, 16):
                    hi(st.chunk("hyb", L, NPROJ + m))
                    if m % 4 == 1 and m > 4:
                        act.wait_ge(s_used, st.chunk("hyb", L, NPROJ + m - 2).half(1))
                        y_squares(2, 2 * ((m // 4 - 1) % 2), m // 4 - 1, SQN)
                act.wait_ge(s_used, st.chunk("hyb", L, NPROJ + 15).half(1))
                y_squares(2, 2, 3, SQN)
                inverse_rms(L * 2 + 6, 2)
                residual(2, x_rows, XRN, L * 4 + 12)

            with act.Fori(0, 2) as L, step.loop(L, 0, 2, ACT_STEPS):
                hyb_layer(L)

        @block.tensor
        def _(pe):
            def three(out, w_h, w_l, x_h, x_l, first, last, weights_still=True):
                if weights_still:
                    nc.tensor.matmul(out, w_h, x_h, start=first, stop=False, skip_group_check=True)
                    nc.tensor.matmul(out, w_h, x_l, start=False, stop=False, skip_group_check=True)
                    return nc.tensor.matmul(out, w_l, x_h, start=False, stop=last, skip_group_check=True)
                nc.tensor.matmul(out, x_h, w_h, start=first, stop=False, skip_group_check=True)
                nc.tensor.matmul(out, x_h, w_l, start=False, stop=False, skip_group_check=True)
                return nc.tensor.matmul(out, x_l, w_h, start=False, stop=last, skip_group_check=True)

            pe.sem_inc(s_used, 2 * RAW)
            pe.wait_ge(s_cst, 16)
            pe.wait_ge(s_prow, 16 * sum(len(r) for r in PARAM_ROWS))
            for t, rows in enumerate(PARAM_ROWS):
                n = sum(x for _, x in rows)
                ins = nc.tensor.transpose(ps[:, 5, t * P:t * P + n], dg[0:n, t, :], ident[0:n, 0:n])
            ins.then_inc(s_prT, 1)

            def ada_sums(ch, c, b):
                if c == 0:
                    pe.wait_ge(s_arow, b)
                for t in range(4):
                    if t % 2 == 0:
                        pe.wait_ge(s_lo, ch.half(t // 2))
                    k = 4 * c + t
                    nc.tensor.matmul(psA, s4[:, 4 * k:4 * k + MS], wh[:, ch.spl, t * BLK:(t + 1) * BLK], start=(k == 0), stop=False,
                                     skip_group_check=True)
                    ins = nc.tensor.matmul(psA, s4[:, 4 * k:4 * k + MS], wl[:, ch.spl, t * BLK:(t + 1) * BLK], start=False,
                                           stop=(k == KT - 1), skip_group_check=True)
                    if t % 2:
                        ins.then_inc(s_used, 1)

            def ada_turn(b, row=AROW):
                pe.wait_ge(s_arow, b + 1)
                pe.wait_ge(s_adaT, b)
                for t in range(4):
                    ins = nc.tensor.matmul(psT[:, t, :], row[0:4, t * P:(t + 1) * P], C("comb")[0:4, 0:2],
                                           start=(t == 0), stop=(t == 3), skip_group_check=True)
                ins.then_inc(s_adaP, 1)

            def first_ada(b, before):
                for c in range(4):
                    ada_sums(st.chunk("ada", b, c), c, b + 1)
                    if c == 0 and before:
                        ada_turn(b, AROW0)

            pe.wait_ge(s_s4, 2)
            pe.wait_ge(s_prm, 1)
            first_ada(0, False)
            with pe.Fori(1, 8) as b:
                first_ada(b, True)
            ada_turn(8, AROW0)

            def turn(r, X, T, k):
                if k == 0:
                    pe.wait_ge(s_dg, r + 1)
                if k >= 4:
                    pe.wait_ge(s_ph, r * KT + (k - 3))
                for t in range(T):
                    ins = nc.tensor.matmul(ps[:, 4 + k % 4, t * P:(t + 1) * P], X[:, t, k * P:(k + 1) * P], dg[:, t, :],
                                           start=(t == 0), stop=(t == T - 1), skip_group_check=True)
                ins.then_inc(s_pt, 1)

            def ahead(r, X, T, k, n=1):
                for j in range(4 + n * k, min(4 + n * (k + 1), KT)):
                    turn(r, X, T, j)
                pe.wait_ge(s_plo, r * KT + (k + 1))

            pe.wait_ge(s_arow, 9)
            pe.wait_ge(s_adaT, 9)
            for k in range(4):
                turn(0, X4, 4, k)

            def proj4(ch, c, first=False):
                for t in range(4):
                    if t % 2 == 0:
                        pe.wait_ge(s_lo, ch.half(t // 2))
                    k = 4 * c + t
                    if first:
                        ahead(0, X4, 4, k, 3)
                    for f in range(4):
                        w = slice(t * BLK + f * P, t * BLK + (f + 1) * P)
                        ins = three(ps[:, f, :], wh[:, ch.spl, w], wl[:, ch.spl, w], hTh[:, k, :], hTl[:, k, :],
                                    k == 0, k == KT - 1)
                    if t % 2:
                        ins.then_inc(s_used, 1)

            def mix(g):
                pe.wait_ge(s_po, g + 1)
                pe.wait_ge(s_inv, 32 * (g + 1))
                for o in range(2):
                    for i in range(2):
                        ins = nc.tensor.matmul(ps[:, 6 + o, :], PW[:, i, o * P:(o + 1) * P], PO[:, i, :],
                                               start=(i == 0), stop=(i == 1))
                ins.then_inc(s_mix, 1)

            for g in range(4):
                if g:
                    pe.wait_ge(s_pg, g)
                    pe.wait_ge(s_pv, g)
                for i in range(12):
                    ch = st.chunk("pool", g, i)
                    if i in POOL_AT:
                        proj4(ch, POOL_AT.index(i), g == 0 and i == 0)
                        if g == 0 and i == 0:
                            pe.wait_ge(s_ph, KT)
                            pe.wait_ge(s_plo, KT)
                    else:
                        n = POOL_ADA.index(i)
                        ada_sums(ch, n % 4, 9 + 2 * g + n // 4)
                    if i == 0 and g:
                        ada_turn(8 + 2 * g)
                    if i == 5 and g:
                        if g > 1:
                            pe.wait_ge(s_py, g - 1)
                        mix(g - 1)
                    if i == 6:
                        ada_turn(9 + 2 * g)

            def conv_chunk(j, i):
                ch = st.chunk("conv", j, i)
                if i % 2 == 0:
                    proj4(ch, i // 2)
                else:
                    ada_sums(ch, i // 2, j + 17)

            pe.wait_ge(s_pg, 4)
            pe.wait_ge(s_pv, 4)
            conv_chunk(0, 0)
            ada_turn(16)
            for i in range(1, 8):
                if i == 5:
                    pe.wait_ge(s_py, 3)
                    mix(3)
                conv_chunk(0, i)
            with pe.Fori(1, 8) as j:
                pe.wait_ge(s_ce, j)
                pe.wait_ge(s_cx, j)
                conv_chunk(j, 0)
                ada_turn(j + 16)
                for i in range(1, 8):
                    conv_chunk(j, i)

            def gate_rows(r):
                pe.wait_ge(s_gd, r + 1)
                if r >= 2:
                    pe.wait_ge(s_gbe, r - 1)
                elif r == 0:
                    pe.wait_ge(s_py, 4)
                nc.tensor.matmul(ps[:, 6 + r % 2, :], ones, dg[:, :, :], start=True, stop=True).then_inc(s_gb, 1)

            def out_block(chunks, T, bank, before=None, after=None):
                for c, ch in enumerate(chunks):
                    for t in range(4):
                        if t % 2 == 0:
                            pe.wait_ge(s_lo, ch.half(t // 2))
                        k = 4 * c + t
                        if before:
                            before(k)
                        for m in range(T):
                            ins = three(ps[:, bank + m, :], wh[:, ch.spl, t * BLK:(t + 1) * BLK],
                                        wl[:, ch.spl, t * BLK:(t + 1) * BLK],
                                        hTh[:, k, m * P:(m + 1) * P], hTl[:, k, m * P:(m + 1) * P],
                                        k == 0, k == KT - 1, False)
                        if t % 2:
                            ins.then_inc(s_used, 1)
                        if after:
                            after(k)

            def spread_gates(k):
                if k == 3:
                    ada_turn(24)
                if 4 <= k < 12:
                    gate_rows(k - 4)

            def free_banks(moved, n):
                pe.wait_ge(s_oe, moved + (n - 1))

            for n in range(4):
                if n == 1:
                    pe.wait_ge(s_gbe, 8)
                    pe.wait_ge(s_adaT, 25)
                if n >= 2:
                    free_banks(0, n)
                out_block([st.chunk("out0", n // 2, 4 * (n % 2) + c) for c in range(4)], 4, 4 * (n % 2),
                          (lambda k: pe.wait_ge(s_yl, k + 1)) if n == 0 else None, spread_gates if n == 0 else None)
            for k in range(4):
                turn(1, X4, 4, k)

            def head_proj(h, c, banks):
                ch = st.chunk("hg", h, c)
                order = [(t, f) for t in range(2) for f in range(5)] if c or not banks else [(t, f) for f in range(5) for t in range(2)]
                for t, f in order:
                    if f == 0:
                        pe.wait_ge(s_lo, ch.half(t))
                    k = 2 * c + t
                    if f == 0 and not banks:
                        ahead(1, X4, 4, k)
                    w = slice(t * 2 * BLK + f * P, t * 2 * BLK + (f + 1) * P)
                    if k == 0 and banks and f < 4:
                        pe.wait_ge(s_hev, h * 4 - 3 + f)
                    n = TOK if f < 3 else SEQ
                    out = ps[:, f, :] if f < 3 else ps[:, 3, (f - 3) * SEQ:(f - 2) * SEQ]
                    ins = three(out, wh[:, ch.spl, w], wl[:, ch.spl, w], hTh[:, k, 0:n], hTl[:, k, 0:n], k == 0 and f != 4, k == KT - 1)
                    if f == 4:
                        ins.then_inc(s_used, 1)

            def v_turn(h):
                pe.wait_ge(s_hev, h * 4 - 1)
                pe.wait_ge(s_sc, h * 2)
                for t in range(4):
                    ins = nc.tensor.transpose(pT[:, t * P:(t + 1) * P], IT[:, t * P:(t + 1) * P], ident)
                ins.then_inc(s_vT, 1)

            def k_turn(h, d):
                pe.wait_ge(s_kdr, h * 2 + 1 + d)
                if d == 0:
                    pe.wait_ge(s_v, h)
                else:
                    pe.wait_ge(s_sc, h * 2 + 1)
                for t in range(4):
                    ins = nc.tensor.transpose(pT[:, t * P:(t + 1) * P], R[:, d, t * P:(t + 1) * P], ident)
                ins.then_inc(s_kT, 1)

            def state_scores(h, d):
                pe.wait_ge(s_kd, h * 2 - 1 + d)
                pe.wait_ge(s_st, h * 2 - 1 + d)
                for j in range(7):
                    n = ORDER[d][j]
                    rows = slice(CHUNK * (n % 2), CHUNK * (n % 2 + 1))
                    ins = nc.tensor.matmul(ps[:, 5 + n % 2, (n // 2) * P:(n // 2 + 1) * P], KD[rows, n // 2, :], V1[rows, n // 2, :],
                                           start=True, stop=True, skip_group_check=True)
                ins.then_inc(s_ds, 1)
                for t in range(2):
                    tok = slice(t * P, (t + 1) * P)
                    ins = nc.tensor.matmul(pT[:, tok], KI[:, d, tok], QD[:, d, tok], start=True, stop=True, skip_group_check=True)
                ins.then_inc(s_scp, 1)

            def head_sum(h):
                pe.wait_ge(s_sc, h * 2 + 2)
                pe.wait_ge(s_st, h * 2 + 1)
                pe.wait_ge(s_y1, h)
                first = True
                for d in range(2):
                    for t in range(2):
                        tok = slice(t * P, (t + 1) * P)
                        nc.tensor.matmul(pO[:, tok], V1[:, t, :], SC[:, d, tok], start=first, stop=False, skip_group_check=True)
                        first = False
                for d in range(2):
                    for n in range(4):
                        tok = slice(n * CHUNK, (n + 1) * CHUNK)
                        ins = nc.tensor.matmul(pO[:, tok], ST[:, d, n * P:(n + 1) * P], QD[:, d, tok], start=False,
                                               stop=(d == 1 and n == 3), skip_group_check=True)
                ins.then_inc(s_o, 1)

            def head_squares(h):
                pe.wait_ge(s_osq, h)
                nc.tensor.matmul(pQ, ones, OS, start=True, stop=True).then_inc(s_sq, 1)

            def head(h, chunk, comp=True, fin=True):
                for c in range(8):
                    chunk(c)
                    if fin and c == 0:
                        head_sum(h - 1)
                    if comp and c == 0:
                        v_turn(h)
                    if fin and c == 1:
                        head_squares(h - 1)
                    if comp and c == 3:
                        k_turn(h, 0)
                    if comp and c == 4:
                        state_scores(h, 0)
                    if comp and c == 5:
                        k_turn(h, 1)
                    if comp and c == 7:
                        state_scores(h, 1)

            head(0, lambda c: head_proj(0, c, False), False, False)
            pe.wait_ge(s_ph, 2 * KT)
            for r in range(8, 12):
                gate_rows(r)
            pe.wait_ge(s_posf, 1)
            nc.tensor.transpose(ps[:, 5, 0:2], posr, ident[0:2, 0:2]).then_inc(s_posT, 1)
            pe.wait_ge(s_gbe, 12)
            pe.wait_ge(s_ang, 1)
            head(1, lambda c: head_proj(1, c, True), fin=False)
            with pe.Fori(2, HEADS) as h:
                head(h, lambda c: head_proj(h, c, True))

            def out1_chunk(m, halves=(0, 1)):
                n, c = OUT1[m]
                ch = st.chunk("out1", m // 8, m % 8)
                for t in (t for h in halves for t in (2 * h, 2 * h + 1)):
                    k = 4 * c + t
                    if t % 2 == 0:
                        pe.wait_ge(s_lo, ch.half(t // 2))
                    pe.wait_ge(s_yl, KT + (k + 1))
                    for m_ in range(2):
                        ins = three(ps[:, 2 * (n % 2) + m_, :], wh[:, ch.spl, t * BLK:(t + 1) * BLK],
                                    wl[:, ch.spl, t * BLK:(t + 1) * BLK],
                                    hTh[:, k, m_ * P:(m_ + 1) * P], hTl[:, k, m_ * P:(m_ + 1) * P], k == 0, k == KT - 1, False)
                    if t % 2:
                        ins.then_inc(s_used, 1)

            def out_before(c):
                if c < 6:
                    if c in (0, 3):
                        pe.wait_ge(s_hev, HEADS * 4 - (2 if c == 0 else 0))
                    out1_chunk(c)
                if c == 7:
                    out1_chunk(6, (0,))

            head(HEADS, out_before)
            head_sum(HEADS)
            head_squares(HEADS)
            out1_chunk(6, (1,))
            out1_chunk(7)
            for m in range(8, 16):
                if m % 4 == 0:
                    free_banks(4, OUT1[m][0])
                out1_chunk(m)

            def hyb_layer(L):
                count = lambda total, n: L * total + n

                def free45(x):
                    n = USE45.index(x)
                    if n:
                        pe.wait_ge(s_45, count(len(USE45), n))

                def free67(x):
                    n = USE67.index(x)
                    if n:
                        pe.wait_ge(s_67, count(len(USE67), n))

                def project(i, half):
                    b = BLOCK_OF[i]
                    name = BLOCKS[b][0]
                    c = i - BLOCK_OF.index(b)
                    bank = 2 * (b % 2)
                    ch = st.chunk("hyb", L, i)
                    if c == 0 and b >= 2 and half == 0:
                        pe.wait_ge(s_bm[b % 2], count(len(BLOCKS) // 2, b // 2))
                    if name == "uq_nope":
                        pe.wait_ge(s_qlo, count(8, 4))
                    if name == "ukv_k":
                        pe.wait_ge(s_qlo, count(8, 8))
                    if name in ("uq_nope", "ukv_k"):
                        r = 0 if name == "uq_nope" else 4
                        for k in (2 * half, 2 * half + 1):
                            if k % 2 == 0:
                                pe.wait_ge(s_lo, ch.half(half))
                            for f in range(4):
                                w = slice((4 * k + f) * P, (4 * k + f + 1) * P)
                                ins = three(ps[:, bank + f // 2, (f % 2) * SEQ:(f % 2 + 1) * SEQ], wh[:, ch.spl, w], wl[:, ch.spl, w],
                                            hTh[:, r + k, SEQ:TOK], hTl[:, r + k, SEQ:TOK], k == 0 and f % 2 == 0, k == 3)
                            if k % 2:
                                ins.then_inc(s_used, 1)
                    elif name in ("uq_rope", "ukv_v"):
                        r, n = (0, 256) if name == "uq_rope" else (4, 512)
                        for k in (2 * half, 2 * half + 1):
                            if k % 2 == 0:
                                pe.wait_ge(s_lo, ch.half(half))
                            for m in range(2):
                                tok = slice(SEQ + m * P, SEQ + (m + 1) * P)
                                ins = three(ps[:, bank + m, 0:n], wh[:, ch.spl, half_tile(k, n)], wl[:, ch.spl, half_tile(k, n)],
                                            hTh[:, r + k, tok], hTl[:, r + k, tok], k == 0, k == 3, False)
                            if k % 2:
                                ins.then_inc(s_used, 1)
                    else:
                        n = 320 if name == "kvr" else BLK
                        for t in (2 * half, 2 * half + 1):
                            k = 4 * c + t
                            if t % 2 == 0:
                                pe.wait_ge(s_lo, ch.half(half))
                            if b == 0:
                                ahead(L + 2, XN, 2, k)
                            for m in range(2):
                                tok = slice(m * P, (m + 1) * P)
                                ins = three(ps[:, bank + m, 0:n], wh[:, ch.spl, half_tile(t, n)], wl[:, ch.spl, half_tile(t, n)],
                                            hTh[:, k, tok], hTl[:, k, tok], k == 0, k == KT - 1, False)
                            if t % 2:
                                ins.then_inc(s_used, 1)

                def norm(name):
                    v = ("cq", "ckv").index(name)
                    free45("norm " + name)
                    pe.wait_ge(s_qd, count(2, v + 1))
                    src = (SR, VC)[v]
                    for k in range(4):
                        for t in range(2):
                            ins = nc.tensor.matmul(ps[:, 4 + k // 2, (k % 2) * SEQ + t * P:(k % 2) * SEQ + (t + 1) * P],
                                                   src[:, t, k * P:(k + 1) * P], DQ[:, 2 * v + t, :], start=(k % 2 == 0 and t == 0),
                                                   stop=True, skip_group_check=True)
                    ins.then_inc(s_qn, 1)

                def turn_block(name):
                    free67("turn " + name)
                    pe.wait_ge(s_rr, count(len(TURNS), TURNS.index(name) + 1))
                    src, n = (KS, 3) if name == "kvr" else (SR, 2 if name == "uq_rope" else 4)
                    for k in range(n):
                        for t in range(2):
                            ins = nc.tensor.transpose(ps[:, 6 + k // 2, (k % 2) * SEQ + t * P:(k % 2) * SEQ + (t + 1) * P],
                                                      src[:, t, k * P:(k + 1) * P], ident)
                    ins.then_inc(s_tn, 1)

                def turned(name):
                    pe.wait_ge(s_67, count(len(USE67), USE67.index("turn " + name) + 1))

                def moved(name):
                    b = BNUM[name]
                    pe.wait_ge(s_bm[b % 2], count(len(BLOCKS) // 2, b // 2 + 1))

                def score(n):
                    kind, h = PAIRS[n]
                    free45(f"score {n}")
                    if kind == "m":
                        turned("uq_rope")
                        moved("ukv_v")
                        moved("ukv_k")
                    elif kind == "b":
                        turned("bq0" if h < 4 else "bq1")
                    else:
                        turned("ak")
                    for m in range(2):
                        half = slice(64 * m, 64 * m + 64)
                        for o, q, k in ((slice(0, 2 * P), slice(P, 2 * P), slice(0, 2 * P)), (slice(2 * P, 3 * P), slice(0, P), slice(0, P))):
                            out = ps[:, 4 + m, o]
                            if kind == "m":
                                nc.tensor.matmul(out, QN[:, 2 * h + m, q], KN[:, 2 * h + m, k], start=True, stop=False, skip_group_check=True)
                                ins = nc.tensor.matmul(out, QR[half, h, q], KR[half, k], start=False, stop=True, skip_group_check=True)
                            elif kind == "b":
                                ins = nc.tensor.matmul(out, BQ[half, h, q], BK[half, h // 4, k], start=True, stop=True, skip_group_check=True)
                            else:
                                ins = nc.tensor.matmul(out, AQ[half, h, q], AK[half, h, k], start=True, stop=True, skip_group_check=True)
                    ins.then_inc(s_S, 1)

                def flip(n):
                    free67(f"flip {n}")
                    pe.wait_ge(s_p, count(NPAIR, n + 1))
                    for m in range(1 if PAIRS[n][0] == "a" else 2):
                        for k in range(3):
                            ins = nc.tensor.transpose(ps[:, 6 + m, k * P:(k + 1) * P], EX[:, m, k * P:(k + 1) * P], ident)
                    ins.then_inc(s_fl, 1)

                def weigh(n):
                    kind, h = PAIRS[n]
                    free45(f"weigh {n}")
                    pe.wait_ge(s_67, count(len(USE67), USE67.index(f"flip {n}") + 1))
                    if kind == "a":
                        moved("av")
                    for m in range(1 if kind == "a" else 2):
                        v, w = {"m": (VC, slice((2 * h + m) * P, (2 * h + m + 1) * P)), "b": (BV, slice((h // 4) * 64, (h // 4) * 64 + 64)),
                                "a": (AV, slice(h * P, (h + 1) * P))}[kind]
                        dv = w.stop - w.start
                        for k in range(2):
                            nc.tensor.matmul(ps[:, 4 + m, 0:dv], PT[:, m, k * P:(k + 1) * P], v[:, k, w], start=(k == 0), stop=(k == 1), skip_group_check=True)
                        ins = nc.tensor.matmul(ps[:, 4 + m, P:P + dv], PT[:, m, 2 * P:3 * P], v[:, 0, w], start=True, stop=True, skip_group_check=True)
                    ins.then_inc(s_W, 1)

                for k in range(4):
                    turn(L + 2, XN, 2, k)
                for i in range(2 * NPROJ):
                    project(i // 2, i % 2)
                    for what in AFTER.get(i, []):
                        verb, arg = what.split()
                        if verb == "norm":
                            norm(arg)
                        elif verb == "turn":
                            turn_block(arg)
                        elif verb != "move":
                            {"score": score, "flip": flip, "weigh": weigh}[verb](int(arg))
                def turn_y(g):
                    if g == 6:
                        moved("cg")
                    if g >= 4:
                        pe.wait_ge(s_ytl, count(YT, g - 3))
                    for k in range(2):
                        for t in range(2):
                            ins = nc.tensor.transpose(ps[:, 4 + g % 4, k * SEQ + t * P:k * SEQ + (t + 1) * P],
                                                      Yt[:, t, (2 * g + k) * P:(2 * g + k + 1) * P], ident)
                    ins.then_inc(s_yt, 1)

                def y_ahead(k):
                    if k % 2 == 0:
                        if k < 8:
                            turn_y(4 + k // 2)
                        pe.wait_ge(s_ytl, count(YT, k // 2 + 1))

                pe.wait_ge(s_45, count(len(USE45), len(USE45)))
                pe.wait_ge(s_67, count(len(USE67), len(USE67)))
                moved("ag")
                for g in range(4):
                    turn_y(g)
                for n in range(4):
                    if n == 1:
                        moved("cg")
                    if n >= 2:
                        free_banks(L * 4 + 8, n)
                    out_block([st.chunk("hyb", L, NPROJ + 4 * n + c) for c in range(4)], 2, 2 * (n % 2), y_ahead if n == 0 else None)

            with pe.Fori(0, 2) as L:
                hyb_layer(L)

        @block.vector
        def _(dve):
            step = Chain(dve, s_dve)

            def lo(ch, n=4 * BLK, halves=(0, 1)):
                for h in halves:
                    part = slice(h * 2 * BLK, h * 2 * BLK + n // 2)
                    dve.wait_ge(s_hi, ch.half(h))
                    nc.vector.tensor_tensor(wl[:, ch.spl, part], raw[:, ch.raw, part], wh[:, ch.spl, part].bitcast(F32),
                                            ALU.subtract).then_inc(s_lo, 1)

            def pcol(name, i):
                return prm[:, PCOL[name] + i:PCOL[name] + i + 1]

            dve.sem_inc(s_lo, 2 * RAW)
            nc.vector.memset(s4[:, :].bitcast(F32), 0.0).then_inc(s_s4, 1)
            dve.sem_inc(s_arow, 1)
            dve.sem_inc(s_adaT, 1)
            dve.wait_ge(s_prT, 1)
            for t, rows in enumerate(PARAM_ROWS):
                n = sum(x for _, x in rows)
                ins = nc.vector.tensor_copy(prm[:, t * P:t * P + n], ps[:, 5, t * P:t * P + n])
            ins.then_inc(s_prm, 1)
            dve.wait_ge(s_prm, 1)
            dve.wait_ge(s_sil, 1)
            step(nc.vector.tensor_scalar(sile, sile, 1.0, None, ALU.add)).done()
            step(nc.vector.reciprocal(sile, sile)).done()
            nc.vector.tensor_tensor(silc, prm[:, 0:32], sile, ALU.mult).then_inc(s_sil, 1)
            dve.wait_ge(s_s4h, 1)
            sv = s4[:, 0:4 * KT].rearrange("p (k v) -> p k v", v=4)
            nc.vector.tensor_tensor(sv[:, :, 2:4], silc.rearrange("p (v k) -> p k v", v=2), sv[:, :, 0:2].bitcast(F32),
                                    ALU.subtract).then_inc(s_s4, 1)
            lg = prm[:, PCOL["lb_logits"]:PCOL["lb_logits"] + 96].rearrange("p (d l k) -> p d l k", d=2, l=3)
            step(nc.vector.tensor_tensor(lbm, lg[:, :, 0, :], lg[:, :, 1, :], ALU.max)).done()
            step(nc.vector.tensor_tensor(lbm, lbm, lg[:, :, 2, :], ALU.max)).done()
            for l in range(3):
                ins = nc.vector.tensor_tensor(lbt[:, :, l, :], lg[:, :, l, :], lbm, ALU.subtract)
            ins.then_inc(s_sil, 1)
            dve.wait_ge(s_sil, 4)
            step(nc.vector.tensor_tensor(lbm, lbt[:, :, 0, :], lbt[:, :, 1, :], ALU.add)).done()
            step(nc.vector.tensor_tensor(lbs, lbm, lbt[:, :, 2, :], ALU.add)).done()
            step(nc.vector.reciprocal(lbs, lbs)).done()
            lbv = lb.rearrange("p (d k) -> p d k", d=2)
            step(nc.vector.tensor_tensor(lbv, lbm, lbs, ALU.mult)).done()
            step(nc.vector.tensor_scalar(oml, lb, -1.0, 1.0, ALU.mult, ALU.add)).done()

            adab = prm[:, PCOL["ada_b"]:PCOL["ada_b"] + 96]

            def ada_row(b, last, row=AROW):
                dve.wait_ge(s_used, last.half(1))
                nc.vector.tensor_copy(row[0:4, :], ps[0:4, 4, :]).then_inc(s_arow, 1)

            def ada_columns(b):
                dve.wait_ge(s_adaP, b)
                at = bass.ds(b * 4 - 4, 4)
                nc.vector.tensor_tensor(adaT[:, at, :], psT, adab[:, at].unsqueeze(2).broadcast_to([P, 4, 2]),
                                        ALU.add).then_inc(s_adaT, 1)

            for c in range(4):
                lo(st.chunk("ada", 0, c))
            with dve.Fori(1, 8) as b:
                lo(st.chunk("ada", b, 0))
                ada_row(b, st.chunk("ada", b - 1, 3), AROW0)
                lo(st.chunk("ada", b, 1))
                lo(st.chunk("ada", b, 2))
                ada_columns(b)
                lo(st.chunk("ada", b, 3))
            ada_row(8, st.chunk("ada", 7, 3), AROW0)

            def modulation(l):
                step(nc.vector.tensor_scalar(modA, adaT[:, 48 * l + KT:48 * l + 2 * KT, :], 1.0, None, ALU.add)).done()
                g = prm[:, PCOL["pre_g"] + KT * l:PCOL["pre_g"] + KT * (l + 1)]
                step(nc.vector.tensor_tensor(modA, modA, g.unsqueeze(2).broadcast_to([P, KT, 2]), ALU.mult)).done()

            def diag(r, T):
                dve.wait_ge(s_rs, r)
                for t in range(T):
                    ins = nc.vector.tensor_scalar(dg[:, t, :], ident, rs[:, t:t + 1], None, ALU.mult)
                ins.then_inc(s_dg, 1)

            def low_h(r, hb, n, A, B, split):
                def low(k):
                    dve.wait_ge(s_phi, r * KT + (k + 1))
                    nc.vector.tensor_tensor(hTl[:, k, 0:n], hb[:, k % 4, 0:n], hTh[:, k, 0:n].bitcast(F32),
                                            ALU.subtract).then_inc(s_plo, 1)

                for k in range(KT):
                    dve.wait_ge(s_pt, r * KT + (k + 1))
                    if k >= 4:
                        dve.wait_ge(s_plo, r * KT + (k - 3))
                    for v in range(n // SEQ):
                        seg = slice(v * SEQ, (v + 1) * SEQ)
                        if B is None:
                            ins = nc.vector.tensor_scalar(hb[:, k % 4, seg], ps[:, 4 + k % 4, seg], A(k, v), None, ALU.mult)
                        else:
                            ins = nc.vector.tensor_scalar(hb[:, k % 4, seg], ps[:, 4 + k % 4, seg], A(k, v), B(k, v), ALU.mult, ALU.add)
                    ins.then_inc(s_ph, 1)
                    if k:
                        low(k - 1)
                    split(k)
                low(KT - 1)

            diag(1, 4)
            ada_columns(8)
            dve.wait_ge(s_adaT, 9)
            modulation(0)
            lo(st.chunk("pool", 0, 0))
            lo(st.chunk("pool", 0, 1))
            low_h(0, HB, TOK, lambda k, v: modA[:, k, v:v + 1], lambda k, v: adaT[:, k, v:v + 1], lambda k: None)
            dve.wait_ge(s_plo, KT)
            step(nc.vector.memset(area(S0, 2 * FLAT), 0.0)).done()

            def rows(buf, r, at=0):
                return buf[:, :, r * LATROW + PAD + at:r * LATROW + PAD + at + GRID_W]

            def pool_out(g):
                dve.wait_ge(s_mix, g + 1)
                for o in range(2):
                    ins = nc.vector.scalar_tensor_tensor(out=Y0[:, 2 * g + o, :], in0=ps[:, 6 + o, :],
                                                         scalar=pcol("ev_pool_scale", 2 * g + o), in1=G2[:, o, :],
                                                         op0=ALU.mult, op1=ALU.mult)
                ins.then_inc(s_py, 1)

            def pool_v(g):
                dve.wait_ge(s_used, st.chunk("pool", g, POOL_AT[3]).half(1))
                if g:
                    dve.wait_ge(s_po, g)
                for t in range(2):
                    nc.vector.tensor_copy(V[:, t, 0:4 * LATROW].rearrange("p (r c) -> p r c", r=4)[:, :, PAD:PAD + GRID_W],
                                          ps[:, t, 0:SEQ].rearrange("p (r c) -> p r c", r=4))
                    ins = nc.vector.tensor_copy(V[:, t, 4 * LATROW + PAD:4 * LATROW + PAD + SEQ], ps[:, t, SEQ:TOK])
                ins.then_inc(s_pv, 1)

            def pool_gate(g):
                dve.wait_ge(s_pg, g + 1)
                step(nc.vector.tensor_scalar(GE, GE, 1.0, None, ALU.add)).done()
                step(nc.vector.reciprocal(GE, GE)).done()
                step(nc.vector.tensor_tensor(G2, G2, GE, ALU.mult)).done()

            def pool_rows(g, w):
                dve.wait_ge(s_pv, g + 1)
                step(nc.vector.memset(area(S0 + 2 * FLAT, 2 * FLAT), 0.0)).done()
                step(nc.vector.tensor_copy(SA[:, :, 4 * LATROW:FLAT], V[:, :, 4 * LATROW:FLAT]))
                if w == 2:
                    step(nc.vector.tensor_copy(rows(SA, 0), rows(V, 0)))
                    for r in range(1, 4):
                        step(nc.vector.tensor_tensor(rows(SA, r), rows(V, r), rows(V, r - 1), ALU.add))
                else:
                    step(nc.vector.tensor_tensor(rows(SA, 0), rows(V, 0), rows(V, 1), ALU.add))
                    step(nc.vector.tensor_tensor(rows(SB_, 0), rows(V, 2), rows(V, 3), ALU.add)).done()
                    if w == 4:
                        step(nc.vector.tensor_tensor(rows(SA, 1), rows(SA, 0), rows(V, 2), ALU.add))
                        step(nc.vector.tensor_tensor(rows(SA, 2), rows(SA, 0), rows(SB_, 0), ALU.add))
                        step(nc.vector.tensor_tensor(rows(SA, 3), rows(SB_, 0), rows(V, 1), ALU.add))
                    else:
                        for r in (1, 2, 3):
                            step(nc.vector.tensor_tensor(rows(SA, r), rows(SA, 0), rows(SB_, 0), ALU.add))
                        step(nc.vector.tensor_tensor(rows(SA, 0), rows(SA, 0), rows(SB_, 0), ALU.add))
                step.done()

            def pool_means(g, w):
                src, dst, span, n = S0 + 2 * FLAT, S0 + 4 * FLAT, 1, 2 * FLAT
                while span < w:
                    n -= span
                    step(nc.vector.tensor_tensor(area(dst, n), area(src, n), area(src + span, n), ALU.add)).done()
                    src, dst, span = dst, src, 2 * span
                W = area(src, 2, FLAT)
                dve.wait_ge(s_inv, 32 * (g + 1))
                PL = PO[:, :, 0:SEQ].rearrange("p a (r c) -> p a r c", r=4)
                lat = W[:, :, 0:4 * LATROW].rearrange("p a (r c) -> p a r c", r=4)[:, :, :, PAD - w // 2:PAD - w // 2 + GRID_W]
                latv = V[:, :, 0:4 * LATROW].rearrange("p a (r c) -> p a r c", r=4)[:, :, :, PAD:PAD + GRID_W]
                c0 = 4 * LATROW + PAD
                for t in range(2):
                    step(nc.vector.tensor_tensor(PL[:, t], lat[:, t], INV[:, 0:SEQ].rearrange("p (r c) -> p r c", r=4), ALU.mult))
                    step(nc.vector.tensor_tensor(PO[:, t, SEQ:TOK], W[:, t, c0 - w // 2:c0 - w // 2 + SEQ], INV[:, SEQ:TOK], ALU.mult))
                step.done()
                for t in range(2):
                    step(nc.vector.tensor_tensor(PL[:, t], PL[:, t], latv[:, t], ALU.subtract))
                    ins = nc.vector.tensor_tensor(PO[:, t, SEQ:TOK], PO[:, t, SEQ:TOK], V[:, t, c0:c0 + SEQ], ALU.subtract)
                ins.then_inc(s_po, 1)

            for g in range(4):
                for i in range(0 if g else 2, 12):
                    if i == 0 and g:
                        pool_v(g - 1)
                    lo(st.chunk("pool", g, i))
                    if i == 1 and g:
                        ada_row(8 + 2 * g, st.chunk("pool", g - 1, 11))
                        pool_gate(g - 1)
                        pool_rows(g - 1, POOL_WINDOWS[g - 1])
                    if i == 4 and g:
                        ada_columns(8 + 2 * g)
                        pool_means(g - 1, POOL_WINDOWS[g - 1])
                    if i == 6:
                        ada_row(9 + 2 * g, st.chunk("pool", g, 5))
                    if i == 9:
                        ada_columns(9 + 2 * g)
                    if i == 10 and g:
                        pool_out(g - 1)

            def conv_mix(j):
                dve.wait_ge(s_ce, j + 1)
                dve.wait_ge(s_cx, j + 1)
                w0, w1, w2 = (prm[:, bass.ds(PCOL["ev_conv_w"] + 8 * i + j, 1)] for i in range(3))
                bias = prm[:, bass.ds(PCOL["ev_conv_b"] + j, 1)]
                v3 = lambda x: x.rearrange("p (a b) -> p a b", a=2)
                step(nc.vector.tensor_tensor(U[:, :, 1:SEQ + 1], v3(CC), v3(CX), ALU.mult))
                step(nc.vector.tensor_scalar(CE, CE, 1.0, None, ALU.add)).done()
                step(nc.vector.tensor_scalar(CT, U[:, :, 0:SEQ], w0, bias, ALU.mult, ALU.add))
                step(nc.vector.reciprocal(CE, CE)).done()
                step(nc.vector.scalar_tensor_tensor(out=CT, in0=U[:, :, 1:SEQ + 1], scalar=w1, in1=CT, op0=ALU.mult, op1=ALU.add))
                step(nc.vector.tensor_tensor(CG, CG, CE, ALU.mult)).done()
                step(nc.vector.scalar_tensor_tensor(out=CT, in0=U[:, :, 2:SEQ + 2], scalar=w2, in1=CT, op0=ALU.mult, op1=ALU.add)).done()
                step(nc.vector.tensor_tensor(CT, CT, v3(CB), ALU.mult)).done()
                nc.vector.tensor_tensor(Y0[:, bass.ds(8 + j, 1), :].rearrange("p a b -> p (a b)"), CT.rearrange("p a b -> p (a b)"), CG,
                                        ALU.mult).then_inc(s_cv, 1)

            def conv_x(j):
                dve.wait_ge(s_used, st.chunk("conv", j, 6).half(1))
                dve.wait_ge(s_cv, j + 1)
                nc.vector.tensor_copy(CX, ps[:, 0, :])
                nc.vector.tensor_copy(CB, ps[:, 1, :]).then_inc(s_cx, 1)

            pool_v(3)
            for i in range(8):
                lo(st.chunk("conv", 0, i))
                if i == 1:
                    ada_row(16, st.chunk("pool", 3, 11))
                    pool_gate(3)
                    pool_rows(3, POOL_WINDOWS[3])
                if i == 3:
                    ada_columns(16)
                    pool_means(3, POOL_WINDOWS[3])
                if i == 6:
                    pool_out(3)
            dve.wait_ge(s_po, 4)
            dve.wait_ge(s_py, 4)
            nc.vector.memset(U, 0.0).then_inc(s_cv, 1)
            with dve.Fori(1, 8) as j, step.loop(j, 1, 7, 8):
                conv_x(j - 1)
                lo(st.chunk("conv", j, 0))
                lo(st.chunk("conv", j, 1))
                ada_row(j + 16, st.chunk("conv", j - 1, 7))
                conv_mix(j - 1)
                lo(st.chunk("conv", j, 2))
                lo(st.chunk("conv", j, 3))
                ada_columns(j + 16)
                for i in range(4, 8):
                    lo(st.chunk("conv", j, i))
            def low_y(k, Yk, n, base):
                dve.wait_ge(s_yh, base + k + 1)
                nc.vector.tensor_tensor(hTl[:, k, 0:n], Yk, hTh[:, k, 0:n].bitcast(F32), ALU.subtract).then_inc(s_yl, 1)

            def gate_scale(l):
                g = prm[:, PCOL["post_g"] + KT * l:PCOL["post_g"] + KT * (l + 1)]
                step(nc.vector.tensor_tensor(gp, adaT[:, 48 * l + 2 * KT:48 * l + 3 * KT, :], g.unsqueeze(2).broadcast_to([P, KT, 2]),
                                             ALU.mult)).done()

            def gate_diag(r):
                q, v = r % 4, r // 4 % 2
                if r:
                    dve.wait_ge(s_gb, r)
                nc.vector.tensor_tensor(dg[:, :, :], ident.unsqueeze(1).broadcast_to([P, 4, P]),
                                        gp[:, 4 * q:4 * q + 4, v].unsqueeze(2).broadcast_to([P, 4, P]), ALU.mult).then_inc(s_gd, 1)

            conv_x(7)
            lo(st.chunk("out0", 0, 0))
            for k in range(4):
                low_y(k, Y0[:, k, :], TOK, 0)
            ada_row(24, st.chunk("conv", 7, 7))
            conv_mix(7)
            for k in range(4, 8):
                low_y(k, Y0[:, k, :], TOK, 0)
            lo(st.chunk("out0", 0, 1))
            for k in range(8, KT):
                low_y(k, Y0[:, k, :], TOK, 0)
            ada_columns(24)
            dve.wait_ge(s_adaT, 25)
            gate_scale(0)
            gate_diag(0)

            def scale_y(T, bank, n, X, G, squared):
                f = slice(n * BLK, (n + 1) * BLK)
                for t in range(T):
                    dve.wait_ge(s_sqp, squared + (T * n + t + 1))
                    ins = nc.vector.tensor_tensor(X[:, t, f], ps[:, bank + t, :], G[:, t // 2, f], ALU.mult)
                ins.then_inc(s_oe, 1)

            def add_squares(T, n, need):
                dve.wait_ge(s_sqp, need)
                nc.vector.tensor_reduce(ssq[:, 0:T], part[:, 0:T * n].rearrange("p (t n) -> p t n", n=n), AX.X, ALU.add).then_inc(s_ssq, 1)

            diags = {2: (1, 2, 3), 3: (4, 5, 6, 7)}
            dve.wait_ge(s_yl, KT)
            for m in range(2, 18):
                if m < 16:
                    lo(st.chunk("out0", m // 8, m % 8))
                for r in diags.get(m, ()):
                    gate_diag(r)
                if m % 4 == 1:
                    n = m // 4 - 1
                    if n == 0:
                        dve.wait_ge(s_gbe, 8)
                    dve.wait_ge(s_used, st.chunk("out0", n // 2, 4 * (n % 2) + 3).half(1))
                    scale_y(4, 4 * (n % 2), n, X4, GB0, 0)

            def residual_add(T, r, base, X, XR):
                dve.wait_ge(s_rs, r)
                for u in range(2 * T):
                    t, f = u // 2, slice((u % 2) * (D // 2), (u % 2 + 1) * (D // 2))
                    dve.wait_ge(s_xr[u % 2], base * 8 + 16 * (u // 2 + 1))
                    nc.vector.scalar_tensor_tensor(out=X[:, t, f], in0=X[:, t, f], scalar=rs[:, t:t + 1],
                                                   in1=XR[:, u % 2, :], op0=ALU.mult, op1=ALU.add).then_inc(s_xa, 1)

            dve.wait_ge(s_oe, 4)
            add_squares(4, 4, 16)
            residual_add(4, 2, 0, X4, XR0)
            modulation(1)
            add_squares(4, 2, 17)
            for c in range(2):
                lo(st.chunk("hg", 0, c), 10 * P)
            diag(3, 4)
            low_h(1, HB, TOK, lambda k, v: modA[:, k, v:v + 1], lambda k, v: adaT[:, 48 + k, v:v + 1],
                  lambda k: lo(st.chunk("hg", 0, (k - 1) // 2), 10 * P) if k >= 5 and k % 2 else None)
            dve.wait_ge(s_plo, 2 * KT)
            dve.sem_inc(s_st, 1)
            dve.sem_inc(s_y1, 1)
            dve.sem_inc(s_kdr, 2)
            dve.sem_inc(s_sgr, 1)
            dve.sem_inc(s_sc, 2)
            nc.vector.memset(SC, 0.0).then_inc(s_l1, 1)
            dve.wait_ge(s_l1, 1)
            gate_scale(1)
            for r in range(8, 12):
                gate_diag(r)
            dve.wait_ge(s_pos, 16)
            nc.vector.tensor_copy(posr, posi).then_inc(s_posf, 1)
            dve.wait_ge(s_posT, 1)
            step(nc.vector.tensor_copy(posf, ps[:, 5, 0:2])).done()
            for t in range(2):
                step(nc.vector.tensor_scalar(ang[:, 32 * t:32 * t + 32], C("invf"), posf[:, t:t + 1], None, ALU.mult))
            step.done()
            step(nc.vector.tensor_scalar(turns_, ang, 1.0 / TWO_PI, ROUND, ALU.mult, ALU.add)).done()
            step(nc.vector.tensor_scalar(turns_, turns_, -ROUND, None, ALU.add)).done()
            for piece in (PI_HI, PI_MID, PI_LO):
                step(nc.vector.scalar_tensor_tensor(out=ang, in0=turns_, scalar=-piece, in1=ang, op0=ALU.mult, op1=ALU.add)).done()
            step(nc.vector.tensor_scalar(ang, ang, 3.1415925, -3.1415925, ALU.min, ALU.max)).done()
            step(nc.vector.scalar_tensor_tensor(out=turns_, in0=ang, scalar=-1.0, in1=ang, op0=ALU.mult, op1=ALU.max)).done()
            nc.vector.tensor_scalar(csn[:, 0:64], turns_, -1.0, 1.5707963267948966, ALU.mult, ALU.add).then_inc(s_ang, 1)
            dve.wait_ge(s_sin, 1)
            dve.wait_ge(s_save, 32)
            chunked = lambda x: x.rearrange("p (n c) -> p n c", c=CHUNK)

            def head(h, split, comp=True, fin=True):
                def bound(x, d):
                    return x[:, bass.ds(h + (d * KT - 1), 1)]

                def gates(d, between):
                    dve.wait_ge(s_hev, h * 4 - 3 + d)
                    step(nc.vector.tensor_scalar(R[:, d, :], Z[:, d, :], 1e30, 1.0, ALU.min, ALU.add)).done()
                    step(nc.vector.tensor_scalar(Z[:, d, :], Z[:, d, :], 1e30, bound(oml, d), ALU.min, ALU.mult))
                    step(nc.vector.reciprocal(R[:, d, :], R[:, d, :])).done()
                    between()
                    step(nc.vector.tensor_tensor(Z[:, d, :], Z[:, d, :], R[:, d, :], ALU.mult)).done()
                    nc.vector.tensor_scalar(R[:, d, :], R[:, d, :], bound(oml, d), bound(lb, d), ALU.mult, ALU.add).then_inc(s_f, 1)

                def decay_sums(d):
                    dve.wait_ge(s_ln, h * 2 - 1 + d)
                    o, i = (B[:, 0, :], R[:, 0, :]) if d == 0 else (B[:, 1, ::-1], R[:, 1, ::-1])
                    step(nc.vector.tensor_tensor_scan(o, C("reset"), i, 0.0, ALU.mult, ALU.add)).done()
                    edge = CHUNK - 1 if d == 0 else 0
                    nc.vector.tensor_tensor(chunked(R[:, d, :]), chunked(B[:, d, :])[:, :, edge:edge + 1].broadcast_to([P, NCH, CHUNK]),
                                            chunked(B[:, d, :]), ALU.subtract).then_inc(s_b, 1)

                def keys(d):
                    dve.wait_ge(s_ex, h * 2 - 1 + d)
                    nc.vector.tensor_tensor(R[:, d, :], R[:, d, :], Z[:, d, :], ALU.mult)
                    nc.vector.tensor_tensor(QD[:, d, :], QD[:, d, :], Q, ALU.mult)
                    nc.vector.tensor_tensor(KI[:, d, :], KI[:, d, :], Z[:, d, 0:SEQ], ALU.mult).then_inc(s_kdr, 1)

                def k_move(d):
                    dve.wait_ge(s_kT, h * 2 - 1 + d)
                    nc.vector.tensor_copy(KD, pT.rearrange("p (a b) -> p a b", a=4)).then_inc(s_kd, 1)

                def states(h, d):
                    dve.wait_ge(s_ds, h * 2 - 1 + d)
                    at = lambda n: ps[:, 5 + n % 2, (n // 2) * P:(n // 2 + 1) * P]
                    step(nc.vector.tensor_copy(SX[:, 0, :], at(ORDER[d][0]))).done()
                    src = SX[:, 0, :]
                    for j in range(1, 7):
                        n = ORDER[d][j]
                        if j == 6:
                            dve.wait_ge(s_scp, h * 2 - 1 + d)
                        dst = SX[:, j % 2, :] if j < 3 else ST[:, d, ORDER[d][j + 1] * P:(ORDER[d][j + 1] + 1) * P]
                        ins = nc.vector.scalar_tensor_tensor(out=dst, in0=src, scalar=DEC[:, d, n:n + 1], in1=at(n),
                                                             op0=ALU.mult, op1=ALU.add)
                        if j < 6:
                            step(ins).done()
                        src = dst
                    ins.then_inc(s_st, 1)
                    nc.vector.copy_predicated(SC[:, d, :].rearrange("p (a b) -> p a b", a=2),
                                              C(("mask_f", "mask_b")[d]).bitcast(I32).unsqueeze(1).broadcast_to([P, 2, P]),
                                              pT[:, 0:SEQ].rearrange("p (a b) -> p a b", a=2)).then_inc(s_sc, 1)

                def head_out(h):
                    dve.wait_ge(s_rso, h)
                    y = Y1[:, bass.ds(h - 1, 1), :].rearrange("p a b -> p (a b)")
                    step(nc.vector.tensor_tensor(OS, pO, RH, ALU.mult)).done()
                    nc.vector.tensor_tensor(y, OS, y, ALU.mult).then_inc(s_y1, 1)

                split(0)
                if fin:
                    states(h - 1, 1)
                if not comp:
                    head_out(h - 1)
                    return
                gates(0, lambda: split(1))
                split(2)
                decay_sums(0)
                gates(1, lambda: split(3))
                keys(0)
                if fin:
                    head_out(h - 1)
                decay_sums(1)
                split(4)
                keys(1)
                k_move(0)
                split(5)
                dve.wait_ge(s_hev, h * 4)
                step(nc.vector.tensor_scalar(GH, GH, 1.0, None, ALU.add)).done()
                step(nc.vector.reciprocal(GH, GH)).done()
                nc.vector.scalar_tensor_tensor(out=Y1[:, bass.ds(h - 1, 1), :].rearrange("p a b -> p (a b)"), in0=SG,
                                               scalar=prm[:, bass.ds(h + (PCOL["od_onorm_g"] - 1), 1)], in1=GH,
                                               op0=ALU.mult, op1=ALU.mult).then_inc(s_sgr, 1)
                states(h, 0)
                split(6)
                k_move(1)
                split(7)

            def head_chunks(h):
                return lambda c: lo(st.chunk("hg", h, c), 10 * P)

            head(1, head_chunks(1), fin=False)
            with dve.Fori(2, HEADS) as h, step.loop(h, 2, HEADS - 2, 25):
                head(h, head_chunks(h))

            def out_chunks(c):
                if c < 7:
                    lo(st.chunk("out1", 0, c))
                for k in {0: range(4), 1: range(4, 8), 2: range(8, 12), 4: range(12, 15)}.get(c, ()):
                    low_y(k, Y1[:, k, :], SEQ, KT)

            head(HEADS, out_chunks)
            head(HEADS + 1, lambda c: None, comp=False)
            low_y(KT - 1, Y1[:, KT - 1, :], SEQ, KT)
            for m in range(7, 16):
                lo(st.chunk("out1", m // 8, m % 8))
                if m in (8, 9):
                    dve.wait_ge(s_used, st.chunk("out1", 0, m - 2).half(1))
                    scale_y(2, 2 * (m - 8), m - 8, X1, GB1, 17)
                if m == 13:
                    dve.wait_ge(s_used, st.chunk("out1", 1, 3).half(1))
                    scale_y(2, 0, 2, X1, GB1, 17)
            dve.wait_ge(s_used, st.chunk("out1", 1, 7).half(1))
            scale_y(2, 2, 3, X1, GB1, 17)
            dve.wait_ge(s_oe, 8)
            add_squares(2, 4, 25)
            residual_add(2, 4, 8, X1, XR1)

            def hyb_layer(L):
                count = lambda total, n: L * total + n
                banks = lambda b: ps[:, 2 * (b % 2):2 * (b % 2) + 2, :]

                def split(i, halves=(0, 1)):
                    lo(st.chunk("hyb", L, i), {"kvr": 4 * 320, "uq_rope": 4 * 256}.get(BLOCKS[BLOCK_OF[i]][0], 4 * BLK), halves)

                add_squares(2, 2, L * 9 + 26)
                split(0)
                split(1)
                diag(L * 2 + 5, 2)
                low_h(L + 2, HBN, SEQ, lambda k, v: prm[:, bass.ds(L * KT + (PCOL["pre_norm_w_2"] + k), 1)], None,
                      lambda k: split({8: 2, 13: 3}[k]) if k in (8, 13) else None)
                dve.wait_ge(s_plo, L * KT + 3 * KT)

                def lambdas():
                    dve.wait_ge(s_lp, L * 96 + 96)
                    lq = LQ.rearrange("p (i j) d -> p i j d", j=2)
                    step(nc.vector.tensor_tensor(lq[:, :, 0, :], lq[:, :, 0, :], lq[:, :, 1, :], ALU.mult)).done()
                    nc.vector.tensor_reduce(lamt[:, 0:2], lq[:, :, 0, :], AX.X, ALU.add).then_inc(s_lam, 1)
                    step(nc.vector.tensor_scalar(SUB, SUB, C("eps")[:, bass.ds(L + 4, 1)], None, ALU.mult))
                    step(nc.vector.tensor_scalar(NSK, SNK, -1.0, None, ALU.mult))
                    dve.wait_ge(s_lamx, count(1, 1))
                    step(nc.vector.tensor_tensor(lamt[:, 2:3], lamt[:, 0:1], lamt[:, 1:2], ALU.subtract)).done()
                    step(nc.vector.tensor_scalar(lamt[:, 3:4], lamt[:, 2:3], C("eps")[:, bass.ds(L + 2, 1)], None, ALU.add)).done()
                    step(nc.vector.tensor_scalar(NL, lamt[:, 3:4], -1.0, None, ALU.mult)).done()

                def rope(src, dst, heads):
                    c, s = (x.unsqueeze(2).broadcast_to([P, 2, heads, 32]) for x in (cosv, sinv))
                    tm = TM[:, :, 0:32 * heads].rearrange("p t (h d) -> p t h d", d=32)
                    x1, x2, o1, o2 = src[:, :, :, 0:32], src[:, :, :, 32:64], dst[:, :, :, 0:32], dst[:, :, :, 32:64]
                    step(nc.vector.tensor_tensor(o1, x1, c, ALU.mult))
                    step(nc.vector.tensor_tensor(tm, x2, s, ALU.mult)).done()
                    step(nc.vector.tensor_tensor(o1, o1, tm, ALU.subtract)).done()
                    step(nc.vector.tensor_tensor(o2, x2, c, ALU.mult))
                    step(nc.vector.tensor_tensor(tm, x1, s, ALU.mult)).done()
                    return nc.vector.tensor_tensor(o2, o2, tm, ALU.add)

                def move(name, i):
                    b = BNUM[name]
                    dve.wait_ge(s_used, st.chunk("hyb", L, i).half(1))
                    if name in ("cq", "ckv"):
                        v = ("cq", "ckv").index(name)
                        dve.wait_ge(s_qs, count(2, v + 1))
                        for t in range(2):
                            ins = nc.vector.tensor_scalar(DQ[:, 2 * v + t, :], ident, qrs[:, 2 * v + t:2 * v + t + 1], None, ALU.mult)
                        ins.then_inc(s_qd, 1)
                    elif name == "kvr":
                        dve.wait_ge(s_qn, count(2, 2))
                        kv = banks(b)[:, :, 0:320].rearrange("p t (h d) -> p t h d", d=64)
                        ks = KS.rearrange("p t (h r d) -> p t h r d", h=3, r=2)
                        step(rope(kv[:, :, 0:2], ks[:, :, 0:2, 0], 2)).done()
                        step(rope(kv[:, :, 4:5], ks[:, :, 2:3, 0], 1)).done()
                        nc.vector.tensor_copy(BV, banks(b)[:, :, P:2 * P]).then_inc(s_bm[b % 2], 1)
                        for t in range(2):
                            ins = nc.vector.tensor_copy(ks[:, t, :, 1], ks[:, t, :, 0])
                        ins.then_inc(s_rr, 1)
                    elif name in ("bq0", "bq1", "aq", "ak", "uq_rope"):
                        heads = 4 if name == "uq_rope" else 8
                        at = TURNS.index(name)
                        dve.wait_ge(s_tn, count(len(TURNS), at))
                        if name in ("bq1", "aq"):
                            gate = BNUM["bg0" if name == "bq1" else "bg1"]
                            dve.wait_ge(s_bm[gate % 2], count(len(BLOCKS) // 2, gate // 2 + 1))
                        v = lambda x: x[:, :, 0:64 * heads].rearrange("p t (h d) -> p t h d", d=64)
                        ins = rope(v(banks(b)), v(SR), heads)
                        step(ins).done()
                        dve.sem_inc(s_bm[b % 2], 1)
                        dve.sem_inc(s_rr, 1)
                    elif name[1] == "g":
                        g = ("bg0", "bg1", "ag", "cg").index(name)
                        dve.wait_ge(s_gx, count(4, g + 1))
                        col = {"bg0": 512, "bg1": 1024, "ag": 0, "cg": 1536}[name]
                        y = Yt[:, :, col:col + BLK]
                        step(nc.vector.tensor_scalar(SR, SR, 1.0, None, ALU.add)).done()
                        step(nc.vector.reciprocal(SR, SR)).done()
                        if name[0] == "b":
                            nc.vector.tensor_tensor(y, banks(b), SR, ALU.mult).then_inc(s_bm[b % 2], 1)
                        else:
                            dve.wait_ge(s_45, count(len(USE45), USE45.index("weigh 11" if name == "ag" else "weigh 1") + 1))
                            n = 2 * P if name == "ag" else BLK
                            step(nc.vector.tensor_tensor(SR, banks(b), SR, ALU.mult)).done()
                            if n < BLK:
                                step(nc.vector.tensor_copy(y[:, :, n:], SR[:, :, n:]))
                            nc.vector.tensor_tensor(y[:, :, 0:n], y[:, :, 0:n], SR[:, :, 0:n], ALU.mult).then_inc(s_bm[b % 2], 1)

                def norm(name):
                    v = ("cq", "ckv").index(name)
                    w = PCOL["mla_q_norm_w_2"] if v == 0 else PCOL["mla_kv_norm_w_2"]
                    dve.wait_ge(s_qn, count(2, v + 1))
                    if v:
                        dve.wait_ge(s_qlo, count(8, 4))
                    for k in range(4):
                        ins = nc.vector.tensor_scalar(HQ[:, k, :], ps[:, 4 + k // 2, (k % 2) * SEQ:(k % 2 + 1) * SEQ],
                                                      prm[:, bass.ds(L * 4 + (w + k), 1)], None, ALU.mult)
                        ins.then_inc(s_qh, 1)
                    dve.wait_ge(s_qh, count(8, 4 * v + 4))
                    dve.sem_inc(s_45, 1)
                    for k in range(4):
                        dve.wait_ge(s_qhi, count(8, 4 * v + k + 1))
                        nc.vector.tensor_tensor(hTl[:, 4 * v + k, SEQ:TOK], HQ[:, k, :], hTh[:, 4 * v + k, SEQ:TOK].bitcast(F32),
                                                ALU.subtract).then_inc(s_qlo, 1)

                def score(n):
                    kind, h = PAIRS[n]
                    scale = 192 ** -0.5 if kind == "m" else 64 ** -0.5
                    dve.wait_ge(s_S, count(NPAIR, n + 1))
                    if n:
                        dve.wait_ge(s_fl, count(NPAIR, n))
                    mask = C("band") if kind == "b" else C("causal")
                    step(nc.vector.scalar_tensor_tensor(out=EX[:, :, 0:2 * P], in0=ps[:, 4:6, 0:2 * P], scalar=scale,
                                                        in1=mask.unsqueeze(1).broadcast_to([P, 2, 2 * P]), op0=ALU.mult, op1=ALU.add))
                    nc.vector.scalar_tensor_tensor(out=EX[:, :, 2 * P:3 * P], in0=ps[:, 4:6, 2 * P:3 * P], scalar=scale,
                                                   in1=C("causal")[:, P:2 * P].unsqueeze(1).broadcast_to([P, 2, P]),
                                                   op0=ALU.mult, op1=ALU.add).then_inc(s_45, 1)
                    dve.wait_ge(s_45, count(len(USE45), USE45.index(f"score {n}") + 1))
                    step(nc.vector.tensor_reduce(NM[:, 0:2], EX[:, :, 0:2 * P], AX.X, ALU.max, negate=True))
                    ins = nc.vector.tensor_reduce(NM[:, 2:4], EX[:, :, 2 * P:3 * P], AX.X, ALU.max, negate=True)
                    if kind == "b":
                        step(ins).done()
                        v = lambda x: x.rearrange("p (q m) -> p q m", q=2)
                        two = lambda x: x[:, 2 * h:2 * h + 2].unsqueeze(1).broadcast_to([P, 2, 2])
                        step(nc.vector.tensor_tensor(v(NM), v(NM), two(NSK), ALU.min)).done()
                        ins = nc.vector.tensor_tensor(v(ES), v(NM), two(SNK), ALU.add)
                    ins.then_inc(s_nm, 1)

                def flip(n):
                    kind, h = PAIRS[n]
                    dve.wait_ge(s_e, count(NPAIR, n + 1))
                    if n:
                        dve.wait_ge(s_45, count(len(USE45), USE45.index(f"weigh {n - 1}") + 1))
                    if kind == "b":
                        step(nc.vector.tensor_tensor(LS, LS, ES, ALU.add)).done()
                    ins = nc.vector.reciprocal(RL, LS)
                    if kind == "a":
                        step(ins).done()
                        step(nc.vector.tensor_scalar(LN, RL.rearrange("p (q m) -> p q m", q=2)[:, :, 1], NL, None, ALU.mult)).done()
                        for q, seg in ((0, slice(0, 2 * P)), (1, slice(2 * P, 3 * P))):
                            step(nc.vector.tensor_scalar(EX[:, 1, seg], EX[:, 1, seg], LN[:, q:q + 1], None, ALU.mult))
                        step.done()
                        for q, seg in ((0, slice(0, 2 * P)), (1, slice(2 * P, 3 * P))):
                            ins = nc.vector.scalar_tensor_tensor(out=EX[:, 0, seg], in0=EX[:, 0, seg], scalar=RL[:, 2 * q:2 * q + 1],
                                                                 in1=EX[:, 1, seg], op0=ALU.mult, op1=ALU.add)
                    ins.then_inc(s_p, 1)

                def moved(name):
                    b = BNUM[name]
                    dve.wait_ge(s_bm[b % 2], count(len(BLOCKS) // 2, b // 2 + 1))

                def weigh(n):
                    kind, h = PAIRS[n]
                    if kind == "b":
                        moved("bg0" if h < 4 else "bg1")
                    if kind == "a" and h >= 2:
                        moved("ag")
                    dve.wait_ge(s_W, count(NPAIR, n + 1))
                    if kind == "a":
                        dve.wait_ge(s_os, count(4, h + 1))
                        for q in range(2):
                            y = Yt[:, 1 - q, h * P:(h + 1) * P]
                            dst = y if h < 2 else OJ[:, q, :]
                            ins = nc.vector.scalar_tensor_tensor(out=dst, in0=ps[:, 4, q * P:(q + 1) * P], scalar=ors[:, q:q + 1], in1=SUB,
                                                                 op0=ALU.mult, op1=ALU.mult)
                            if h >= 2:
                                step(ins).done()
                                ins = nc.vector.tensor_tensor(y, OJ[:, q, :], y, ALU.mult)
                        ins.then_inc(s_45, 1)
                        return
                    for m in range(2):
                        for q in range(2):
                            r = RL[:, 2 * q + m:2 * q + m + 1]
                            if kind == "m":
                                y = Yt[:, 1 - q, 1536 + (2 * h + m) * P:1536 + (2 * h + m + 1) * P]
                                ins = nc.vector.tensor_scalar(y, ps[:, 4 + m, q * P:(q + 1) * P], r, None, ALU.mult)
                            else:
                                y = Yt[:, 1 - q, 512 + (2 * h + m) * 64:512 + (2 * h + m + 1) * 64]
                                ins = nc.vector.scalar_tensor_tensor(out=y, in0=ps[:, 4 + m, q * P:q * P + 64], scalar=r, in1=y,
                                                                     op0=ALU.mult, op1=ALU.mult)
                    ins.then_inc(s_45, 1)

                def after(i):
                    for what in AFTER.get(i, []):
                        verb, arg = what.split()
                        if verb == "move":
                            move(arg, (i - 1) // 2)
                        elif verb == "norm":
                            norm(arg)
                        elif verb != "turn":
                            {"score": score, "flip": flip, "weigh": weigh}[verb](int(arg))

                split(4, (0,))
                for i in range(6, 2 * NPROJ - 1):
                    if i + 3 < 2 * NPROJ:
                        split((i + 3) // 2, ((i + 3) % 2,))
                    if i == 8:
                        lambdas()
                    after(i)

                def low_turned(g):
                    dve.wait_ge(s_yth, count(YT, g + 1))
                    nc.vector.tensor_tensor(hTl[:, 2 * g:2 * g + 2, 0:SEQ], ps[:, 4 + g % 4, :].rearrange("p (a b) -> p a b", a=2),
                                            hTh[:, 2 * g:2 * g + 2, 0:SEQ].bitcast(F32), ALU.subtract).then_inc(s_ytl, 1)

                lo(st.chunk("hyb", L, NPROJ))
                for g in range(4):
                    low_turned(g)
                lo(st.chunk("hyb", L, NPROJ + 1))
                for g in range(4, 6):
                    low_turned(g)
                after(2 * NPROJ - 1)
                for g in range(6, YT):
                    low_turned(g)
                dve.wait_ge(s_gl, L * 16 + 16)
                for m in range(2, 18):
                    if m < 16:
                        lo(st.chunk("hyb", L, NPROJ + m))
                    if m % 4 == 1:
                        n = m // 4 - 1
                        dve.wait_ge(s_used, st.chunk("hyb", L, NPROJ + 4 * n + 3).half(1))
                        scale_y(2, 2 * (n % 2), n, XN, GBN, L * 9 + 26)
                dve.wait_ge(s_oe, L * 4 + 12)
                add_squares(2, 4, L * 9 + 34)
                residual_add(2, L * 2 + 6, L * 4 + 12, XN, XRN)

            with dve.Fori(0, 2) as L, step.loop(L, 0, 2, DVE_STEPS):
                hyb_layer(L)


_SHAPES = ["consts", "inv"]
_INS = ["x", "c", "ctx", "c_ctx", "ada_w", "ada_b", "pre_g", "post_g", "ev_w_in", "ev_pool_w", "ev_pool_scale",
        "ev_conv_w", "ev_conv_b", "ev_w_out", "od_w_in", "od_onorm_g", "od_w_out", "lb_logits", "positions_2",
        "pre_norm_w_2", "post_norm_w_2", "w_in_2", "diff_lambda_q1_2", "diff_lambda_k1_2", "diff_lambda_q2_2",
        "diff_lambda_k2_2", "diff_subln_w_2", "sink_logits_2", "mla_q_norm_w_2", "mla_kv_norm_w_2", "w_uq_2",
        "w_ukv_2", "w_out_2"]


def kernel(**inputs):
    import numpy as _np
    import concourse.bacc as _bacc
    from concourse import mybir as _mybir
    from concourse.bass_utils import run_bass_kernel_spmd as _run

    nc = _bacc.Bacc("TRN2", target_bir_lowering=False, num_devices=1)
    arrays, a = {}, {}
    consts, inv = shape_constants()
    given = {name: _np.ascontiguousarray(inputs[name]) for name in _INS}
    given["consts"], given["inv"] = consts, _np.ascontiguousarray(_np.broadcast_to(inv[:, None, :], (4, P, TOK)))
    for name, v in given.items():
        arrays[f"in_{name}_dram"] = v
        a[name] = nc.dram_tensor(f"in_{name}_dram", v.shape, _mybir.dt.from_np(v.dtype), kind="ExternalInput").ap()
    a["out"] = nc.dram_tensor("out_0_dram", (1, SEQ, D), F32, kind="ExternalOutput").ap()
    first_block_and_hybrid(nc, a)
    r = _run(nc, [arrays], core_ids=[0])
    return r.results[0]["out_0_dram"]
```
